# Optimizing a Trainium2 kernel written in Bass

```python
import math
import jax, jax.numpy as jnp
from jax import lax
import numpy as np

D_MODEL = 1024
BATCH = 1
SEQ = 512
DEPTH = 2

CHUNK = 64
N_META = 16
N_HEADS = 8
N_KV_HEADS = 2
HEAD_DIM = 128
KV_GROUP = N_HEADS // N_KV_HEADS
ATTN_WIDTH = N_HEADS * HEAD_DIM
IDX_HEADS = 8
IDX_DIM = 64
TOPK_MAX = 256
Q_BLOCK = 64
ROPE_THETA = 10000.0
RNN_WIDTH = D_MODEL
RNN_BLOCKS = 8
RNN_BLOCK_DIM = RNN_WIDTH // RNN_BLOCKS
RNN_CONV = 4
LRU_C = 8.0
CONV_WIDTH = D_MODEL
CONV_KERNEL = 31
D_FF = -(-8 * D_MODEL // (3 * 256)) * 256
N_BRANCH = 3
NORM_EPS = 1e-6

IN_SPLITS = (
    N_HEADS * HEAD_DIM,
    N_KV_HEADS * HEAD_DIM,
    N_KV_HEADS * HEAD_DIM,
    IDX_HEADS * IDX_DIM,
    IDX_DIM,
    IDX_HEADS,
    RNN_WIDTH,
    RNN_WIDTH,
    2 * CONV_WIDTH,
    N_BRANCH * D_MODEL,
)
IN_WIDTH = sum(IN_SPLITS)


def _split_cols(a):
    pts, acc = [], 0
    for w in IN_SPLITS[:-1]:
        acc += w
        pts.append(acc)
    return jnp.split(a, pts, axis=-1)

def rms_norm(x, g):
    xf = x.astype(jnp.float32)
    y = xf * lax.rsqrt(jnp.mean(xf * xf, axis=-1, keepdims=True) + NORM_EPS)
    return (y * g.astype(jnp.float32)).astype(x.dtype)

def layer_norm(x, g, b):
    xf = x.astype(jnp.float32)
    mu = jnp.mean(xf, axis=-1, keepdims=True)
    xc = xf - mu
    y = xc * lax.rsqrt(jnp.mean(xc * xc, axis=-1, keepdims=True) + NORM_EPS)
    return (y * g.astype(jnp.float32) + b.astype(jnp.float32)).astype(x.dtype)

def rope_tables(n, dim):
    inv = ROPE_THETA ** (-jnp.arange(0, dim, 2, dtype=jnp.float32) / dim)
    ang = jnp.arange(n, dtype=jnp.float32)[:, None] * inv[None, :]
    return jnp.cos(ang), jnp.sin(ang)

def rotary(x, cos, sin):
    xf = x.astype(jnp.float32)
    x1, x2 = jnp.split(xf, 2, axis=-1)
    c = cos[None, :, None, :]
    s = sin[None, :, None, :]
    return jnp.concatenate([x1 * c - x2 * s, x2 * c + x1 * s], axis=-1).astype(x.dtype)

def chunk_ids(n_valid, n_total):
    p = jnp.arange(n_total, dtype=jnp.int32)
    cid = jnp.where(p < N_META, 0, 1 + (p - N_META) // CHUNK)
    return jnp.where(p < n_valid, cid, jnp.iinfo(jnp.int32).max).astype(jnp.int32)

def causal_depthwise_conv(x, w, b):
    k = w.shape[0]
    y = lax.conv_general_dilated(
        x, w[:, None, :].astype(x.dtype), window_strides=(1,), padding=[(k - 1, 0)],
        dimension_numbers=("NWC", "WIO", "NWC"), feature_group_count=x.shape[-1])
    return y + b.astype(y.dtype)

def dsa_attention(q, k, v, qi, ki, wi):
    B, T = q.shape[0], q.shape[1]
    n_blocks = -(-T // Q_BLOCK)
    Tp = n_blocks * Q_BLOCK
    pad = Tp - T

    def pad_t(a):
        return jnp.pad(a, [(0, 0), (0, pad)] + [(0, 0)] * (a.ndim - 2))

    q, k, v, qi, ki, wi = (pad_t(a) for a in (q, k, v, qi, ki, wi))
    cid = chunk_ids(T, Tp)
    topk = min(TOPK_MAX, SEQ // 4)
    scale = HEAD_DIM ** -0.5

    def to_blocks(a):
        return a.reshape(B, n_blocks, Q_BLOCK, *a.shape[2:]).swapaxes(0, 1)

    def block(args):
        qb, qib, wib, cidb = args
        logits = jnp.einsum("bqhd,bsd->bqhs", qib, ki)
        iscore = jnp.einsum("bqhs,bqh->bqs", jax.nn.relu(logits), wib).astype(jnp.float32)
        admiss = cid[None, :] <= cidb[:, None]
        iscore = jnp.where(admiss[None], iscore, -jnp.inf)
        _, sel = lax.top_k(iscore, topk)
        valid = cid[sel] <= cidb[None, :, None]
        gather = jax.vmap(lambda tb, ib: tb[ib])
        ksel = gather(k, sel)
        vsel = gather(v, sel)
        qg = qb.reshape(B, Q_BLOCK, N_KV_HEADS, KV_GROUP, HEAD_DIM)
        s = jnp.einsum("bqngd,bqknd->bngqk", qg, ksel).astype(jnp.float32) * scale
        s = jnp.where(valid[:, None, None], s, -jnp.inf)
        p = jax.nn.softmax(s, axis=-1).astype(vsel.dtype)
        o = jnp.einsum("bngqk,bqknd->bqngd", p, vsel)
        return o.reshape(B, Q_BLOCK, N_HEADS, HEAD_DIM)

    out = lax.map(block, (to_blocks(q), to_blocks(qi), to_blocks(wi), cid.reshape(n_blocks, Q_BLOCK)))
    return out.swapaxes(0, 1).reshape(B, Tp, N_HEADS * HEAD_DIM)[:, :T]

def rg_lru_branch(xr, yg, conv_w, conv_b, wa, ba, wx, bx, lam):
    u = causal_depthwise_conv(xr, conv_w, conv_b)
    B, T, R = u.shape
    ub = u.reshape(B, T, RNN_BLOCKS, RNN_BLOCK_DIM)
    r = jax.nn.sigmoid(jnp.einsum("btnd,nde->btne", ub, wa).reshape(B, T, R).astype(jnp.float32)
                       + ba.astype(jnp.float32))
    i = jax.nn.sigmoid(jnp.einsum("btnd,nde->btne", ub, wx).reshape(B, T, R).astype(jnp.float32)
                       + bx.astype(jnp.float32))
    log_a = -LRU_C * r * jax.nn.softplus(-lam.astype(jnp.float32))
    a = jnp.exp(log_a)
    b_in = jnp.sqrt(-jnp.expm1(2.0 * log_a)) * (i * u.astype(jnp.float32))

    def step(h, ab):
        a_t, b_t = ab
        h = a_t * h + b_t
        return h, h

    _, hs = lax.scan(step, jnp.zeros((B, R), jnp.float32), (a.swapaxes(0, 1), b_in.swapaxes(0, 1)))
    h = hs.swapaxes(0, 1).astype(xr.dtype)
    return h * jax.nn.gelu(yg)

def conformer_conv_branch(c, dw_w, dw_b, ln_g, ln_b):
    a, g = jnp.split(c, 2, axis=-1)
    u = a * jax.nn.sigmoid(g)
    u = causal_depthwise_conv(u, dw_w, dw_b)
    u = layer_norm(u, ln_g, ln_b)
    return jax.nn.silu(u)

def first_inputs(seed: int = 0) -> dict:
    key = jax.random.key(seed)
    ks = iter(jax.random.split(key, 32))
    f32 = jnp.float32

    def nrm(shape, scale):
        return jax.random.normal(next(ks), shape, f32) * scale

    def gain(shape):
        return 1.0 + 0.01 * jax.random.normal(next(ks), shape, f32)

    a0 = jax.random.uniform(next(ks), (DEPTH, RNN_WIDTH), f32, minval=0.9, maxval=0.999)
    base = a0 ** (1.0 / LRU_C)
    rnn_lambda = jnp.log(base) - jnp.log1p(-base)
    return {
        "x": nrm((BATCH, SEQ, D_MODEL), 1.0),
        "meta": nrm((N_META, D_MODEL), 1.0),
        "mix_norm_g": gain((DEPTH, D_MODEL)),
        "w_in": nrm((DEPTH, D_MODEL, IN_WIDTH), D_MODEL ** -0.5),
        "q_norm_g": gain((DEPTH, HEAD_DIM)),
        "k_norm_g": gain((DEPTH, HEAD_DIM)),
        "rnn_conv_w": nrm((DEPTH, RNN_CONV, RNN_WIDTH), RNN_CONV ** -0.5),
        "rnn_conv_b": nrm((DEPTH, RNN_WIDTH), 0.01),
        "rnn_wa": nrm((DEPTH, RNN_BLOCKS, RNN_BLOCK_DIM, RNN_BLOCK_DIM), RNN_BLOCK_DIM ** -0.5),
        "rnn_ba": nrm((DEPTH, RNN_WIDTH), 0.01),
        "rnn_wx": nrm((DEPTH, RNN_BLOCKS, RNN_BLOCK_DIM, RNN_BLOCK_DIM), RNN_BLOCK_DIM ** -0.5),
        "rnn_bx": nrm((DEPTH, RNN_WIDTH), 0.01),
        "rnn_lambda": rnn_lambda,
        "conv_dw_w": nrm((DEPTH, CONV_KERNEL, CONV_WIDTH), CONV_KERNEL ** -0.5),
        "conv_dw_b": nrm((DEPTH, CONV_WIDTH), 0.01),
        "conv_ln_g": gain((DEPTH, CONV_WIDTH)),
        "conv_ln_b": nrm((DEPTH, CONV_WIDTH), 0.01),
        "w_o_attn": nrm((DEPTH, ATTN_WIDTH, D_MODEL), ATTN_WIDTH ** -0.5),
        "w_o_rnn": nrm((DEPTH, RNN_WIDTH, D_MODEL), RNN_WIDTH ** -0.5),
        "w_o_conv": nrm((DEPTH, CONV_WIDTH, D_MODEL), CONV_WIDTH ** -0.5),
        "w_out": nrm((DEPTH, D_MODEL, D_MODEL), D_MODEL ** -0.5),
        "ffn_norm_g": gain((DEPTH, D_MODEL)),
        "w_ffn_gate": nrm((DEPTH, D_MODEL, D_FF), D_MODEL ** -0.5),
        "w_ffn_up": nrm((DEPTH, D_MODEL, D_FF), D_MODEL ** -0.5),
        "w_ffn_down": nrm((DEPTH, D_FF, D_MODEL), D_FF ** -0.5),
    }

def first_block(x, meta, mix_norm_g, w_in, q_norm_g, k_norm_g, rnn_conv_w, rnn_conv_b, rnn_wa, rnn_ba,
              rnn_wx, rnn_bx, rnn_lambda, conv_dw_w, conv_dw_b, conv_ln_g, conv_ln_b, w_o_attn, w_o_rnn,
              w_o_conv, w_out, ffn_norm_g, w_ffn_gate, w_ffn_up, w_ffn_down):
    B = x.shape[0]
    h = jnp.concatenate([jnp.broadcast_to(meta[None].astype(x.dtype), (B, N_META, D_MODEL)), x], axis=1)
    T = h.shape[1]
    cos_a, sin_a = rope_tables(T, HEAD_DIM)
    cos_i, sin_i = rope_tables(T, IDX_DIM)
    idx_scale = (IDX_HEADS ** -0.5) * (IDX_DIM ** -0.5)

    for l in range(DEPTH):
        n = rms_norm(h, mix_norm_g[l])
        proj = jnp.einsum("btd,de->bte", n, w_in[l])
        q, k, v, qi, ki, wi, xr, yg, cv, gt = _split_cols(proj)

        q = rotary(rms_norm(q.reshape(B, T, N_HEADS, HEAD_DIM), q_norm_g[l]), cos_a, sin_a)
        k = rotary(rms_norm(k.reshape(B, T, N_KV_HEADS, HEAD_DIM), k_norm_g[l]), cos_a, sin_a)
        v = v.reshape(B, T, N_KV_HEADS, HEAD_DIM)
        qi = rotary(qi.reshape(B, T, IDX_HEADS, IDX_DIM), cos_i, sin_i)
        ki = rotary(ki.reshape(B, T, 1, IDX_DIM), cos_i, sin_i)[:, :, 0]
        attn = dsa_attention(q, k, v, qi, ki, wi * idx_scale)

        rnn = rg_lru_branch(xr, yg, rnn_conv_w[l], rnn_conv_b[l], rnn_wa[l], rnn_ba[l],
                            rnn_wx[l], rnn_bx[l], rnn_lambda[l])

        cnv = conformer_conv_branch(cv, conv_dw_w[l], conv_dw_b[l], conv_ln_g[l], conv_ln_b[l])

        g_attn, g_rnn, g_conv = jnp.split(jax.nn.sigmoid(gt), N_BRANCH, axis=-1)
        merged = (g_attn * jnp.einsum("bte,ed->btd", attn, w_o_attn[l])
                  + g_rnn * jnp.einsum("bte,ed->btd", rnn, w_o_rnn[l])
                  + g_conv * jnp.einsum("bte,ed->btd", cnv, w_o_conv[l]))
        h = h + jnp.einsum("btd,de->bte", merged, w_out[l])

        f = rms_norm(h, ffn_norm_g[l])
        a = jax.nn.silu(jnp.einsum("btd,df->btf", f, w_ffn_gate[l])) * jnp.einsum("btd,df->btf", f, w_ffn_up[l])
        h = h + jnp.einsum("btf,fd->btd", a, w_ffn_down[l])

    return h[:, N_META:]


DEPTH_2 = 1

GRID_W = 64
HEAD_DIM_2 = 64
ATTN_W = N_HEADS * HEAD_DIM_2
NA_WIN_H = 8
NA_WIN_W = 16
SSM_W = 512
SSM_GROUP = 16
SSM_GROUPS = SSM_W // SSM_GROUP
SSM_STATE = 64
N_DIR = 2
DT_MIN = 1e-3
DT_MAX = 1e-1
LAMBDA_RE_MAX = -1e-4
N_BRANCH_2 = 2
IN_COLS = 3 * ATTN_W + SSM_W + N_BRANCH_2 * D_MODEL
D_FF_2 = 2816
PLE_DIM = 256
RMS_EPS = 1e-6


def rms_norm_2(x, g):
    xf = x.astype(jnp.float32)
    y = xf * lax.rsqrt(jnp.mean(xf * xf, axis=-1, keepdims=True) + RMS_EPS)
    return (y * g.astype(jnp.float32)).astype(x.dtype)

def swiglu(x, w_gate, w_up, w_down):
    return (jax.nn.silu(x @ w_gate) * (x @ w_up)) @ w_down

def neighbourhood_attention(q, k, v, rpb):
    bn, s, h, hd = q.shape
    rows = s // GRID_W
    wh = min(NA_WIN_H, rows)
    ww = NA_WIN_W
    scale = hd ** -0.5
    qg = q.reshape(bn, rows, GRID_W, h, hd)
    kg = k.reshape(bn, rows, GRID_W, h, hd)
    vg = v.reshape(bn, rows, GRID_W, h, hd)
    cols = jnp.arange(GRID_W)
    col_start = jnp.clip(cols - ww // 2, 0, GRID_W - ww)
    col_idx = col_start[:, None] + jnp.arange(ww)[None, :]
    dc_idx = col_idx - cols[:, None] + (NA_WIN_W - 1)

    def row_block(r):
        rs = jnp.clip(r - wh // 2, 0, rows - wh)
        kr = lax.dynamic_slice_in_dim(kg, rs, wh, axis=1)
        vr = lax.dynamic_slice_in_dim(vg, rs, wh, axis=1)
        kn = kr[:, :, col_idx]
        vn = vr[:, :, col_idx]
        qr = lax.dynamic_index_in_dim(qg, r, axis=1, keepdims=False)
        dr_idx = rs + jnp.arange(wh) - r + (NA_WIN_H - 1)
        bias = rpb[:, dr_idx[:, None, None], dc_idx[None]]
        bias = bias.transpose(0, 2, 1, 3)
        sc = jnp.einsum('bchd,brcwhd->bhcrw', qr, kn) * scale + bias[None]
        sc = sc.reshape(bn, h, GRID_W, wh * ww).astype(jnp.float32)
        pr = jax.nn.softmax(sc, axis=-1).astype(v.dtype).reshape(bn, h, GRID_W, wh, ww)
        return jnp.einsum('bhcrw,brcwhd->bchd', pr, vn)

    out = lax.map(row_block, jnp.arange(rows))
    return out.transpose(1, 0, 2, 3, 4).reshape(bn, s, h * hd)

def _ssm_combine(ei, ej):
    a_i, b_i = ei
    a_j, b_j = ej
    return a_j * a_i, a_j * b_i + b_j

def s5_scan(u, lam_re, lam_im, log_dt, b_re, b_im, c_re, c_im, reverse):
    f32 = jnp.float32
    s = u.shape[1]
    lam = lax.complex(jnp.minimum(lam_re.astype(f32), LAMBDA_RE_MAX), lam_im.astype(f32))
    dt = jnp.exp(log_dt.astype(f32))[:, None]
    lam_bar = jnp.exp(lam * dt)
    b_bar = ((lam_bar - 1.0) / lam)[..., None] * lax.complex(b_re.astype(f32), b_im.astype(f32))
    bu = lax.complex(jnp.einsum('bsgi,gpi->bsgp', u, b_bar.real),
                     jnp.einsum('bsgi,gpi->bsgp', u, b_bar.imag))
    a = jnp.broadcast_to(lam_bar, (1, s) + lam_bar.shape)
    _, states = lax.associative_scan(_ssm_combine, (a, bu), reverse=reverse, axis=1)
    return (jnp.einsum('bsgp,gop->bsgo', states.real, c_re.astype(f32))
            - jnp.einsum('bsgp,gop->bsgo', states.imag, c_im.astype(f32)))

def s5_branch(s_in, lam_re, lam_im, log_dt, b_re, b_im, c_re, c_im, d_skip, glu_w, glu_b):
    f32 = jnp.float32
    bn, s, _ = s_in.shape
    u = s_in.astype(f32).reshape(bn, s, SSM_GROUPS, SSM_GROUP)
    y = d_skip.astype(f32).reshape(SSM_GROUPS, SSM_GROUP) * u
    for direction in range(N_DIR):
        y = y + s5_scan(u, lam_re[direction], lam_im[direction], log_dt[direction],
                        b_re[direction], b_im[direction], c_re[direction], c_im[direction],
                        reverse=(direction == 1))
    y = jax.nn.gelu(y.reshape(bn, s, SSM_W))
    y = y * jax.nn.sigmoid(y @ glu_w.astype(f32) + glu_b.astype(f32))
    return y.astype(s_in.dtype)

def second_inputs(seed: int = 0) -> dict:
    key = jax.random.key(seed)
    ks = iter(jax.random.split(key, 48))
    L = DEPTH_2
    f32 = jnp.float32

    def nrm(shape, fan_in):
        return jax.random.normal(next(ks), shape, f32) * fan_in ** -0.5

    def gain(shape):
        return 1.0 + 0.05 * jax.random.normal(next(ks), shape, f32)

    def small(shape, scale):
        return scale * jax.random.normal(next(ks), shape, f32)

    G, P, GC = SSM_GROUPS, SSM_STATE, SSM_GROUP
    return {
        "x": jax.random.normal(next(ks), (BATCH, SEQ, D_MODEL), f32),
        "p": jax.random.normal(next(ks), (DEPTH_2, BATCH, SEQ, PLE_DIM), f32),
        "ffn1_norm": gain((L, D_MODEL)),
        "ffn1_w_gate": nrm((L, D_MODEL, D_FF_2), D_MODEL),
        "ffn1_w_up": nrm((L, D_MODEL, D_FF_2), D_MODEL),
        "ffn1_w_down": nrm((L, D_FF_2, D_MODEL), D_FF_2),
        "mix_norm": gain((L, D_MODEL)),
        "w_in": nrm((L, D_MODEL, IN_COLS), D_MODEL),
        "na_rpb": small((L, N_HEADS, 2 * NA_WIN_H - 1, 2 * NA_WIN_W - 1), 0.02),
        "ssm_lam_re": -0.5 + small((L, N_DIR, G, P), 0.01),
        "ssm_lam_im": math.pi * jnp.arange(P, dtype=f32) + small((L, N_DIR, G, P), 0.01),
        "ssm_log_dt": jax.random.uniform(next(ks), (L, N_DIR, G), f32,
                                         minval=math.log(DT_MIN), maxval=math.log(DT_MAX)),
        "ssm_b_re": nrm((L, N_DIR, G, P, GC), 2 * GC),
        "ssm_b_im": nrm((L, N_DIR, G, P, GC), 2 * GC),
        "ssm_c_re": nrm((L, N_DIR, G, GC, P), 2 * P),
        "ssm_c_im": nrm((L, N_DIR, G, GC, P), 2 * P),
        "ssm_d": jax.random.normal(next(ks), (L, SSM_W), f32),
        "ssm_glu_w": nrm((L, SSM_W, SSM_W), SSM_W),
        "ssm_glu_b": small((L, SSM_W), 0.01),
        "w_attn_out": nrm((L, ATTN_W, D_MODEL), ATTN_W),
        "w_ssm_out": nrm((L, SSM_W, D_MODEL), SSM_W),
        "w_out": nrm((L, D_MODEL, D_MODEL), D_MODEL),
        "ffn2_norm": gain((L, D_MODEL)),
        "ffn2_w_gate": nrm((L, D_MODEL, D_FF_2), D_MODEL),
        "ffn2_w_up": nrm((L, D_MODEL, D_FF_2), D_MODEL),
        "ffn2_w_down": nrm((L, D_FF_2, D_MODEL), D_FF_2),
        "ple_norm": gain((L, D_MODEL)),
        "ple_w_gate": nrm((L, D_MODEL, D_MODEL), D_MODEL),
        "ple_w_proj": nrm((L, PLE_DIM, D_MODEL), PLE_DIM),
        "final_norm": gain((D_MODEL,)),
    }

def second_block(x, p, ffn1_norm, ffn1_w_gate, ffn1_w_up, ffn1_w_down, mix_norm, w_in, na_rpb,
              ssm_lam_re, ssm_lam_im, ssm_log_dt, ssm_b_re, ssm_b_im, ssm_c_re, ssm_c_im,
              ssm_d, ssm_glu_w, ssm_glu_b, w_attn_out, w_ssm_out, w_out,
              ffn2_norm, ffn2_w_gate, ffn2_w_up, ffn2_w_down,
              ple_norm, ple_w_gate, ple_w_proj, final_norm):
    bn, s, _ = x.shape
    splits = [ATTN_W, 2 * ATTN_W, 3 * ATTN_W, 3 * ATTN_W + SSM_W]
    h = x
    for i in range(DEPTH_2):
        h = h + 0.5 * swiglu(rms_norm_2(h, ffn1_norm[i]), ffn1_w_gate[i], ffn1_w_up[i], ffn1_w_down[i])
        u = rms_norm_2(h, mix_norm[i])
        z = u @ w_in[i]
        q, k, v, s_in, gates = jnp.split(z, splits, axis=-1)
        y_attn = neighbourhood_attention(q.reshape(bn, s, N_HEADS, HEAD_DIM_2),
                                         k.reshape(bn, s, N_HEADS, HEAD_DIM_2),
                                         v.reshape(bn, s, N_HEADS, HEAD_DIM_2),
                                         na_rpb[i]) @ w_attn_out[i]
        y_ssm = s5_branch(s_in, ssm_lam_re[i], ssm_lam_im[i], ssm_log_dt[i],
                          ssm_b_re[i], ssm_b_im[i], ssm_c_re[i], ssm_c_im[i],
                          ssm_d[i], ssm_glu_w[i], ssm_glu_b[i]) @ w_ssm_out[i]
        g_attn, g_ssm = jnp.split(jax.nn.sigmoid(gates), N_BRANCH_2, axis=-1)
        h = h + (g_attn * y_attn + g_ssm * y_ssm) @ w_out[i]
        h = h + 0.5 * swiglu(rms_norm_2(h, ffn2_norm[i]), ffn2_w_gate[i], ffn2_w_up[i], ffn2_w_down[i])
        h = h + (p[i] @ ple_w_proj[i]) * jax.nn.sigmoid(rms_norm_2(h, ple_norm[i]) @ ple_w_gate[i])
    return rms_norm_2(h, final_norm)


def setup_inputs(seed=0):
    out = dict(first_inputs(seed))
    for name, value in second_inputs(seed + 1).items():
        if name != "x":
            out[name + "_2"] = value
    return out


def reference(
    x, meta, mix_norm_g, w_in, q_norm_g, k_norm_g, rnn_conv_w, rnn_conv_b, rnn_wa, rnn_ba,
    rnn_wx, rnn_bx, rnn_lambda, conv_dw_w, conv_dw_b, conv_ln_g, conv_ln_b, w_o_attn, w_o_rnn,
    w_o_conv, w_out, ffn_norm_g, w_ffn_gate, w_ffn_up, w_ffn_down, p_2, ffn1_norm_2,
    ffn1_w_gate_2, ffn1_w_up_2, ffn1_w_down_2, mix_norm_2, w_in_2, na_rpb_2, ssm_lam_re_2,
    ssm_lam_im_2, ssm_log_dt_2, ssm_b_re_2, ssm_b_im_2, ssm_c_re_2, ssm_c_im_2, ssm_d_2,
    ssm_glu_w_2, ssm_glu_b_2, w_attn_out_2, w_ssm_out_2, w_out_2, ffn2_norm_2, ffn2_w_gate_2,
    ffn2_w_up_2, ffn2_w_down_2, ple_norm_2, ple_w_gate_2, ple_w_proj_2, final_norm_2,
):
    x = first_block(
        x, meta, mix_norm_g, w_in, q_norm_g, k_norm_g, rnn_conv_w, rnn_conv_b, rnn_wa, rnn_ba,
        rnn_wx, rnn_bx, rnn_lambda, conv_dw_w, conv_dw_b, conv_ln_g, conv_ln_b, w_o_attn,
        w_o_rnn, w_o_conv, w_out, ffn_norm_g, w_ffn_gate, w_ffn_up, w_ffn_down,
    )
    return second_block(
        x, p_2, ffn1_norm_2, ffn1_w_gate_2, ffn1_w_up_2, ffn1_w_down_2, mix_norm_2, w_in_2,
        na_rpb_2, ssm_lam_re_2, ssm_lam_im_2, ssm_log_dt_2, ssm_b_re_2, ssm_b_im_2, ssm_c_re_2,
        ssm_c_im_2, ssm_d_2, ssm_glu_w_2, ssm_glu_b_2, w_attn_out_2, w_ssm_out_2, w_out_2,
        ffn2_norm_2, ffn2_w_gate_2, ffn2_w_up_2, ffn2_w_down_2, ple_norm_2, ple_w_gate_2,
        ple_w_proj_2, final_norm_2,
    )


_drawn_inputs = setup_inputs


def setup_inputs(seed=0):
    import zlib

    import numpy as np

    out = dict(_drawn_inputs(seed))
    spreads = {}
    factors = {'mix_norm_g': 4.162,
     'q_norm_g': 8.0,
     'k_norm_g': 8.0,
     'rnn_ba': 8.0,
     'rnn_bx': 8.0,
     'conv_dw_b': 4.627,
     'conv_ln_g': 7.586,
     'conv_ln_b': 8.0,
     'ffn_norm_g': 4.947,
     'ffn1_norm_2': 4.015,
     'mix_norm_2': 6.203,
     'na_rpb_2': 64.0,
     'ssm_lam_re_2': 64.0,
     'ssm_lam_im_2': 38.976,
     'ssm_log_dt_2': 41.424,
     'ssm_b_re_2': 55.72,
     'ssm_b_im_2': 55.424,
     'ssm_c_re_2': 55.44,
     'ssm_c_im_2': 55.184,
     'ssm_glu_b_2': 200.0,
     'ffn2_norm_2': 15.692,
     'ple_norm_2': 200.0,
     'ple_w_gate_2': 29.28,
     'p_2': 7.408,
     'ple_w_proj_2': 7.397}
    for name, (base, spread) in spreads.items():
        noise = np.random.default_rng([zlib.crc32(name.encode()), seed]).standard_normal(out[name].shape)
        drawn = base * np.exp(spread * noise) if base else spread * noise
        out[name] = __import__('jax').numpy.asarray(drawn.astype(out[name].dtype))
    for name, factor in factors.items():
        out[name] = (out[name] * factor).astype(out[name].dtype)
    return out
```

```python
from contextlib import ExitStack

import numpy as np

import concourse.bass as bass
from concourse import mybir

F32 = mybir.dt.float32
F32R = mybir.dt.float32r
ALU = mybir.AluOpType
ACT = mybir.ActivationFunctionType
AX = mybir.AxisListType

P = 128
D = 1024
KD = D // P
DEPTH = 2
META = 16
SEQ = 512
T1 = META + SEQ
CHUNK = 64
TOPK = 128
HEADS = 8
KV = 2
HD = 128
IXH = 8
IXD = 64
FF = 2816
KF = FF // P
CONV = 4
DW = 31
NQT = SEQ // P
EPS = 1e-6
NEG = -1.0e30
BARRED = -3.0e38
CHOSEN = -3.4e38
BLK = 8
RAW = 4
TWO_PI = 2.0 * np.pi
MAGIC = 12582912.0
PI_SAFE = 3.1415925
NAW = 16
NAR = 14
HD2 = 64
UNITS = 16
ROUND = 4
SC = 4
NC = SEQ // SC


def two_pi_parts():
    c1 = np.float32(6.28125)
    r = TWO_PI - float(c1)
    c2 = np.float32(np.round(r * 2.0 ** 21) / 2.0 ** 21)
    return float(c1), float(c2), float(np.float32(r - float(c2)))


class Phase:
    def __init__(self, block, tile, tiles, per):
        self.b0, self.t0, self.tiles, self.per = block, tile, tiles, per

    def block(self, i):
        return self.b0 + i * self.per

    def slot(self, i):
        return (self.t0 + i) % 2

    def nth(self, i):
        return (self.t0 + i) // 2


PHASES = []
for _l in range(DEPTH):
    PHASES += [(f"qk{_l}", 10, 1), (f"v{_l}", 2, 1), (f"qi{_l}", 5, 1), (f"rnn{_l}", 16, 1), (f"mg_rnn{_l}", 16, 1),
               (f"conv{_l}", 16, 1), (f"mg_conv{_l}", 16, 1), (f"att{_l}", 8, 0), (f"mg_att{_l}", 16, 1),
               (f"out{_l}", 8, 1), (f"up{_l}", 2 * KF, 1), (f"down{_l}", 8, 3)]
PHASES += [("up2", 2 * KF, 1), ("down2", 8, 3), ("qkv2", 12, 1), ("sin2", 4, 1), ("att2", 4, 0), ("glu2", 4, 1),
           ("mg2", 32, 1), ("out2", 8, 1), ("up3", 2 * KF, 1), ("down3", 8, 3), ("ple2", 16, 1)]


def plan():
    at, block, tile = {}, 0, 0
    for name, tiles, per in PHASES:
        at[name] = Phase(block, tile, tiles, per)
        block += tiles * per
        tile += tiles
    return at, block


LAYER_COLS = [("mix_g", 8), ("q_g", 1), ("k_g", 1), ("cw", CONV * 8), ("cb", 8), ("ba", 8), ("bx", 8), ("lam", 8),
              ("dw", DW * 8), ("db", 8), ("ln_g", 8), ("ln_b", 8), ("ffn_g", 8)]
TAIL_COLS = [("ffn1_g", 8), ("mix2_g", 8), ("ffn2_g", 8), ("ple_g", 8), ("final_g", 8), ("dskip", 4), ("glu_b", 4)]


def columns():
    at, n = {}, 0
    for layer in range(DEPTH):
        for name, w in LAYER_COLS:
            at[(name, layer)] = n
            n += w
    for name, w in TAIL_COLS:
        at[name] = n
        n += w
    return at, n


def build(nc, A_w, A_par, A_h, A_rope, A_gate, A_natab, A_namask, A_ssm, A_chunk, A_p, A_ident, A_out):
    AT, NBLK = plan()
    COL, NPAR = columns()
    ROW = T1 * 4

    with ExitStack() as ctx:
        sems = {}

        def sem(name):
            if name not in sems:
                sems[name] = ctx.enter_context(nc.semaphore(name))
            return sems[name]

        BASE = 16512
        place = [BASE]

        def fixed(name, shape, dt=F32):
            t = nc.alloc_sbuf_tensor_at(name, shape, dt, offset=place[0])
            n = 4
            for s in shape[1:]:
                n *= s
            place[0] += (n + 31) // 32 * 32
            return t

        ident = fixed("ident", [P, P])
        ones = fixed("ones", [P, P])
        par = fixed("par", [P, NPAR])
        spc = fixed("spc", [P, DEPTH, 8])
        nspc = fixed("nspc", [P, DEPTH, 8])
        h = fixed("h", [P, KD, T1])
        nhi = fixed("nhi", [P, KD, T1], F32R)
        nlo = fixed("nlo", [P, KD, T1], F32R)
        raw = fixed("raw", [P, RAW, BLK * P])
        whi = fixed("whi", [P, 2, BLK * P], F32R)
        wlo = fixed("wlo", [P, 2, BLK * P], F32R)
        zeros = fixed("zeros", [P, 128])
        ARENA = place[0]
        END = 229344

        def at(name, shape, off, dt=F32):
            n = 4
            for s in shape[1:]:
                n *= s
            assert ARENA + off + n <= END, (name, ARENA + off + n - END)
            return nc.alloc_sbuf_tensor_at(name, shape, dt, offset=ARENA + off), off + (n + 31) // 32 * 32

        o = 0
        q, o = at("q", [P, HEADS, T1], o)
        k, o = at("k", [P, KV, T1], o)
        v, o = at("v", [P, 5, KV * HD], o)
        mask, o = at("mask", [P, NQT, T1], o)
        wi, o = at("wi", [P, NQT, IXH], o)
        merged, end_merged = at("merged", [P, KD, T1], o)
        vT, o1 = at("vT", [P, KV, T1], o)
        rnn_w, o1 = at("rnn_w", [P, 2, 8, P], o1)
        assert o1 <= end_merged
        bhi, o = at("bhi", [P, KD, T1], end_merged, F32R)
        blo, o = at("blo", [P, KD, T1], o, F32R)
        area1 = o
        qi, o = at("qi", [P, 4, T1], o)
        ki, o = at("ki", [P, T1], o)
        rope, area2 = at("rope", [P, 4, T1], o)
        cu, _ = at("cu", [P, KD, T1], area1)
        o = area1
        ru, o = at("ru", [P, T1], o)
        rr, o = at("rr", [P, T1], o)
        ri, o = at("ri", [P, T1], o)
        rt, o = at("rt", [P, T1], o)
        ra, o = at("ra", [P, T1], o)
        rb, o = at("rb", [P, T1], o)
        rh, o = at("rh", [P, T1], o)
        rg, o = at("rg", [P, T1], o)
        assert o <= area2
        o = area2
        tsq, o = at("tsq", [P, 2, T1], o)
        tqg, o = at("tqg", [P, 2, T1], o)
        tsw, o = at("tsw", [P, 2, T1], o)
        tstd, o = at("tstd", [P, T1], o)
        trs, o = at("trs", [P, T1], o)
        wbuf, o = at("wbuf", [32, T1], o)
        top8, o = at("top8", [P, 8], o)
        o = area2
        rx, o = at("rx", [P, T1 + CONV - 1], o)
        o = area2
        sg, o = at("sg", [P, T1], o)
        mt, o = at("mt", [P, T1], o)
        cx, o = at("cx", [P, T1 + DW - 1], o)
        cstat, o = at("cstat", [P, 3, T1], o)
        csq, o = at("csq", [P, 2, T1], o)
        o = area1
        sm, o = at("sm", [P, 2, T1], o)
        pts, o = at("pts", [P, 5, P], o)
        ot, o = at("ot", [P, T1], o)
        mx, o = at("mx", [P, 2], o)
        nmx, o = at("nmx", [P, 2], o)
        rsum, o = at("rsum", [P, 2], o)
        rrs, o = at("rrs", [P, 2], o)
        prep, o = at("prep", [P, 8, DEPTH * 8], 0)

        o = 0
        fsq, o = at("fsq", [P, 2, T1], o)
        ftmp, o = at("ftmp", [P, 2, T1], o)
        fstd, o = at("fstd", [P, T1], o)
        frs, o = at("frs", [P, T1], o)
        o = 0
        ahi, o = at("ahi", [P, KF, T1], o, F32R)
        alo, o = at("alo", [P, KF, T1], o, F32R)
        fsl, o = at("fsl", [P, T1], o)
        fpr, o = at("fpr", [P, T1], o)

        S = SEQ
        o = 0
        attn_hi, o = at("attn_hi", [P, 4, S], o, F32R)
        attn_lo, o = at("attn_lo", [P, 4, S], o, F32R)
        zhi, o = at("zhi", [P, 4, S], o, F32R)
        zlo, o = at("zlo", [P, 4, S], o, F32R)
        uin, o = at("uin", [P, 4, S], o)
        yv, o = at("yv", [P, 4, S], o)
        base2 = o
        q2, o = at("q2", [P, 4, S], o)
        k2, o = at("k2", [P, 4, S], o)
        v2, o = at("v2", [P, 4, S], o)
        vT2, _ = at("vT2", [P, 4, S], o)
        natab, o = at("natab", [P, HEADS, NAR, GW], o)
        namask, o = at("namask", [P, GW], o)
        sm2, _ = at("sm2", [P, 2, S], 2 * 4 * S * 4)
        pts2, _ = at("pts2", [P, 4, P], 2 * 4 * S * 4 + 2 * S * 4)
        ot2, _ = at("ot2", [P, S], 2 * 4 * S * 4 + 3 * S * 4)
        sc2, _ = at("sc2", [P, 4, 2], 2 * 4 * S * 4 + 4 * S * 4)
        o = base2
        smp, o = at("smp", [P, 3, 32], o)
        sbc, o = at("sbc", [P, 4, 32, 32], o)
        spw, o = at("spw", [P, 20, 32], o)
        lc_r, o = at("lc_r", [P, 32, 5], o)
        lc_i, o = at("lc_i", [P, 32, 5], o)
        lb_r, o = at("lb_r", [P, 32, 4], o)
        lb_i, o = at("lb_i", [P, 32, 4], o)
        chk, o = at("chk", [P, NC], o)
        place_of_reps = o
        reps, o = at("reps", [P, 2, 8, 4, 32], o)
        zz, _ = at("zz", [P, 2, 8, NC], place_of_reps)
        ap_, o = at("ap_", [P, 2, 8, 4, 32], o)
        cp_, o = at("cp_", [P, 2, 8, 5, 32], o)
        w1s, o = at("w1s", [P, 8, 2, P], o)
        tm_, o = at("tm_", [P, 4, P], o)
        us, o = at("us", [P, 2, 4, NC], o)
        cs_, o = at("cs_", [P, 2, 8, NC], o)
        m4, o = at("m4", [P, 8, NC], o)
        o = 2 * 4 * S * 4
        st_, o = at("st_", [P, 2, 8, NC + 1], o)
        w8, o = at("w8", [P, 8, NC], o)
        bb, o = at("bb", [P, 2, 8, 32], o)
        o = base2
        merged2, o = at("merged2", [P, KD, S], o)
        mhi, o = at("mhi", [P, KD, S], o, F32R)
        mlo, o = at("mlo", [P, KD, S], o, F32R)
        sg2, o = at("sg2", [P, S], o)
        mt2, o = at("mt2", [P, S], o)
        o = 0
        pin, o = at("pin", [P, 2, S], o)
        phi, o = at("phi", [P, 2, S], o, F32R)
        plo, o = at("plo", [P, 2, S], o, F32R)
        psg, o = at("psg", [P, S], o)
        pmt, o = at("pmt", [P, S], o)
        o = max(o, 6 * ROW)
        yout, o = at("yout", [P, KD, S], o)

        acc = [ctx.enter_context(nc.psum_tensor(f"acc{i}", [P, 2, 512], F32)) for i in range(2)]
        aux = [ctx.enter_context(nc.psum_tensor(f"aux{i}", [P, 2, 512], F32)) for i in range(2)]

        evac = [sem("acc0_evacuated"), sem("acc1_evacuated")]
        pe_block = sem("pe_block_done")

        def halves(ap2, T):
            return ap2.rearrange("p (a b) -> p a b", a=2)

        def accv(s, T):
            return acc[s][:, :, 0:T // 2]

        def col(name, layer=None, j=0, n=1):
            c = COL[(name, layer)] if layer is not None else COL[name]
            return par[:, c + j:c + j + n]

        def h_ready(eng, phase):
            n = phase.tiles
            for i in (n - 2, n - 1):
                eng.wait_ge(evac[phase.slot(i)], phase.nth(i) + 1)

        def hview(T):
            return h[:, :, T1 - T:T1]

        NORMS = ["mix0", "ffn0", "mix1", "ffn1", "ffn2_1", "mix2", "ffn2_2", "ple2", "final"]
        NORM_G = [("mix_g", 0), ("ffn_g", 0), ("mix_g", 1), ("ffn_g", 1), ("ffn1_g", None), ("mix2_g", None),
                  ("ffn2_g", None), ("ple_g", None), ("final_g", None)]
        NORM_AFTER = [None, "out0", "down0", "out1", "down1", "down2", "out2", "down3", "ple2"]
        NORM_T = [T1] * 4 + [SEQ] * 5

        block = ctx.enter_context(nc.Block())

        @block.sync
        def _(sp):
            for b in range(RAW):
                sp.dma_start(raw[:, b], A_w[b]).then_inc(sem(f"w_loaded{b}"), 16)
            groups = NBLK // RAW
            with sp.Fori(1, groups) as g:
                for r in range(RAW):
                    sp.wait_ge(sem("w_split"), g * RAW + (r - RAW + 1))
                    sp.dma_start(raw[:, r], A_w[bass.ds(g * RAW + r, 1)].rearrange("a p n -> (a p) n"))\
                      .then_inc(sem(f"w_loaded{r}"), 16)
            for b in range(groups * RAW, NBLK):
                sp.wait_ge(sem("w_split"), b - RAW + 1)
                sp.dma_start(raw[:, b % RAW], A_w[b]).then_inc(sem(f"w_loaded{b % RAW}"), 16)
            for j in range(KD):
                sp.wait_ge(sem("final_out"), j + 1)
                sp.dma_start(A_out[j], yout[:, j]).then_inc(sem("stored"), 16)
            sp.wait_ge(sem("stored"), 16 * KD)

        @block.gpsimd
        def _(pool):
            pool.wait_ge(sem("consts_set"), 3)
            zb = zeros[:, :].unsqueeze(1).broadcast_to([P, BLK, P])

            def split(b, r, n):
                s = r % 2
                pool.wait_ge(sem(f"w_loaded{r}"), n)
                w = raw[:, r].rearrange("p (a c) -> p a c", a=BLK)
                hi = whi[:, s].rearrange("p (a c) -> p a c", a=BLK)
                lo = wlo[:, s].rearrange("p (a c) -> p a c", a=BLK)
                pool.tensor_tensor(hi, w, zb, ALU.add).then_inc(sem("w_hi"), 1)
                pool.wait_ge(sem("w_hi"), b + 1)
                pool.tensor_tensor(lo, w, hi.bitcast(F32), ALU.subtract).then_inc(sem("w_split"), 1)

            for b in range(RAW):
                if b >= 2:
                    pool.wait_ge(pe_block, b - 1)
                split(b, b, 16)
            groups = NBLK // RAW
            with pool.Fori(1, groups) as g:
                for r in range(RAW):
                    pool.wait_ge(pe_block, g * RAW + (r - 1))
                    split(g * RAW + r, r, g * 16 + 16)
            for b in range(groups * RAW, NBLK):
                pool.wait_ge(pe_block, b - 1)
                split(b, b % RAW, 16 * (b // RAW + 1))

        @block.tensor
        def _(pe):
            def products(s, slot, j0, nk, rhs, T, first, last):
                TH = T // 2
                for j in range(nk):
                    hi = whi[:, slot, j * P:(j + 1) * P]
                    lo = wlo[:, slot, j * P:(j + 1) * P]
                    xh, xl = rhs(j0 + j)
                    a, z = first and j == 0, last and j == nk - 1
                    for f in range(2):
                        pe.matmul(acc[s][:, f, 0:TH], hi, xh[:, f * TH:(f + 1) * TH], start=a, stop=False)
                        pe.matmul(acc[s][:, f, 0:TH], hi, xl[:, f * TH:(f + 1) * TH], start=False, stop=False)
                    for f in range(2):
                        m = pe.matmul(acc[s][:, f, 0:TH], lo, xh[:, f * TH:(f + 1) * TH], start=False, stop=z)
                return m

            def tile(ph, i, rhs, T, nk=KD, m=0, step=0):
                s = ph.slot(i)
                n = ph.nth(i) + m * (step // 2)
                if ph.t0 + i >= 2:
                    pe.wait_ge(evac[s], n)
                for c in range(ph.per):
                    b = ph.block(i) + c
                    pe.wait_ge(sem("w_split"), b + 1 + m * (step * ph.per))
                    kk = min(BLK, nk - c * BLK)
                    products(s, b % 2, c * BLK, kk, rhs, T, c == 0, c == ph.per - 1).then_inc(pe_block, 1)

            def R(hi, lo, T):
                return lambda j: (hi[:, j, 0:T], lo[:, j, 0:T])

            def sumsq(i):
                T = NORM_T[i]
                for j in range(KD):
                    pe.wait_ge(sem("norm_square"), i * KD + j + 1)
                    for f in range(2):
                        m = pe.matmul(aux[0][:, f, 0:T // 2], ones[:, :], fsq[:, j % 2, f * (T // 2):(f + 1) * (T // 2)],
                                      start=j == 0, stop=j == KD - 1)
                    m.then_inc(sem("norm_summed"), 1)

            def normed(i):
                pe.wait_ge(sem("norm_lo"), (i + 1) * KD)

            def ffn(i, up, down, T):
                sumsq(i)
                normed(i)
                with pe.Fori(0, KF) as m:
                    for j in range(2):
                        tile(AT[up], j, R(nhi, nlo, T), T, m=m, step=2)
                pe.wait_ge(sem("ff_lo"), (FFI[up] + 1) * KF + 1)
                with pe.Fori(0, KD // 2) as m:
                    for j in range(2):
                        tile(AT[down], j, R(ahi, alo, T), T, nk=KF, m=m, step=2)

            def proj(l):
                qk, rhs = AT[f"qk{l}"], R(nhi, nlo, T1)

                def qk_sum(e):
                    it = l * 10 + e
                    pe.wait_ge(sem("qk_square"), it + 1)
                    if it:
                        pe.wait_ge(sem("qk_std"), it)
                    for f in range(2):
                        m = pe.matmul(aux[0][:, f, 0:T1 // 2], ones[:, :],
                                      tsq[:, e % 2, f * (T1 // 2):(f + 1) * (T1 // 2)], start=True, stop=True)
                    m.then_inc(sem("qk_sum"), 1)

                for e in range(10):
                    tile(qk, e, rhs, T1)
                    if e:
                        qk_sum(e - 1)
                tile(AT[f"v{l}"], 0, rhs, T1)
                qk_sum(9)
                tile(AT[f"v{l}"], 1, rhs, T1)
                for e in range(4):
                    tile(AT[f"qi{l}"], e, rhs, T1)
                pe.wait_ge(evac[AT[f"v{l}"].slot(1)], AT[f"v{l}"].nth(1) + 1)
                pe.wait_ge(sem("qk_std"), (l + 1) * 10)
                for e in range(KV):
                    for c in range(4):
                        pe.transpose(aux[1][:, e, c * P:(c + 1) * P], vT[:, e, c * P:(c + 1) * P], ident[:, :])
                for e in range(KV):
                    m = pe.transpose(aux[0][0:16, e, 0:P], vT[:, e, 4 * P:T1], ident[:, :])
                m.then_inc(sem("v_turned"), 1)
                tile(AT[f"qi{l}"], 4, rhs, T1)
                pe.wait_ge(sem("wi_rows"), l + 1)
                pe.wait_ge(sem("v_copied"), 4 * (l + 1))
                for i in range(NQT):
                    m = pe.transpose(aux[0][:, 1, i * 32:(i + 1) * 32], wbuf[:, META + i * P:META + (i + 1) * P],
                                     ident[0:32, 0:32])
                m.then_inc(sem("wi_turned"), 1)

            def index(l):
                pe.wait_ge(sem("qi_done"), 5 * (l + 1))
                pe.wait_ge(sem("wi_copied"), l + 1)
                for i in range(NQT):
                    W = META + P * (i + 1)
                    for hh in range(IXH):
                        it = (l * NQT + i) * IXH + hh
                        if it >= 2:
                            pe.wait_ge(sem("ix_relu"), it - 1)
                        rows = slice(64 * (hh % 2), 64 * (hh % 2) + 64)
                        lhs = qi[rows, hh // 2, META + i * P:META + (i + 1) * P]
                        m = pe.matmul(aux[hh % 2][:, 0, 0:min(W, 512)], lhs, ki[rows, 0:min(W, 512)], start=True, stop=True)
                        if W > 512:
                            m = pe.matmul(aux[hh % 2][:, 1, 0:W - 512], lhs, ki[rows, 512:W], start=True, stop=True)
                        m.then_inc(sem("ix_logit"), 1)

            def rnn(l):
                ph, rhs = AT[f"rnn{l}"], R(nhi, nlo, T1)

                def gates(n):
                    it = l * 8 + n
                    pe.wait_ge(sem("rnn_conv"), 4 * (it + 1))
                    if n == 0:
                        pe.wait_ge(sem("rnn_w_loaded"), 16 * (l + 1))
                        pe.wait_ge(sem("ix_relu"), (l + 1) * NQT * IXH)
                    if it:
                        pe.wait_ge(sem("rnn_i"), it)
                    for g in range(2):
                        for f in range(2):
                            m = pe.matmul(aux[g][:, f, 0:T1 // 2], rnn_w[:, g, n],
                                          ru[:, f * (T1 // 2):(f + 1) * (T1 // 2)], start=True, stop=True)
                    m.then_inc(sem("rnn_gates"), 1)

                for n in range(8):
                    tile(ph, 2 * n, rhs, T1)
                    if n:
                        gates(n - 1)
                    tile(ph, 2 * n + 1, rhs, T1)
                gates(7)

            def merge(l, name, inst):
                pe.wait_ge(sem("br_lo"), (l * 4 + inst + 1) * KD)
                with pe.Fori(0, KD) as m:
                    tile(AT[f"mg_{name}{l}"], 0, R(nhi, nlo, T1), T1, m=m, step=2)
                    tile(AT[f"mg_{name}{l}"], 1, R(bhi, blo, T1), T1, m=m, step=2)

            def conv(l):
                for n in range(16):
                    tile(AT[f"conv{l}"], n, R(nhi, nlo, T1), T1)
                for n in range(KD):
                    pe.wait_ge(sem("cv_conv"), (l * 8 + n + 1) * DW)
                    if n == 0:
                        pe.wait_ge(sem("rnn_i"), (l + 1) * 8)
                    for f in range(2):
                        m = pe.matmul(aux[0][:, f, 0:T1 // 2], ones[:, :], cu[:, n, f * (T1 // 2):(f + 1) * (T1 // 2)],
                                      start=n == 0, stop=n == KD - 1)
                m.then_inc(sem("cv_mean"), 1)
                for n in range(KD):
                    pe.wait_ge(sem("cv_square"), l * 8 + n + 1)
                    for f in range(2):
                        m = pe.matmul(aux[1][:, f, 0:T1 // 2], ones[:, :], csq[:, n % 2, f * (T1 // 2):(f + 1) * (T1 // 2)],
                                      start=n == 0, stop=n == KD - 1)
                    m.then_inc(sem("cv_summed"), 1)

            def attention(l):
                ph = AT[f"att{l}"]
                items = [(hh, i) for hh in range(HEADS) for i in range(NQT + 1)]
                n0 = l * len(items)

                def shape(i):
                    return (P, META + i * P, META + (i + 1) * P) if i < NQT else (META, 0, META)

                def scores(j):
                    hh, i = items[j]
                    r, c, W = shape(i)
                    if n0 + j:
                        pe.wait_ge(sem("at_scored"), n0 + j)
                    lhs = q[:, hh, c:c + r]
                    m = pe.matmul(aux[0][0:r, 0, 0:min(W, 512)], lhs, k[:, hh // 4, 0:min(W, 512)], start=True, stop=True)
                    if W > 512:
                        m = pe.matmul(aux[0][0:r, 1, 0:W - 512], lhs, k[:, hh // 4, 512:W], start=True, stop=True)
                    m.then_inc(sem("at_s"), 1)

                def pieces(W):
                    return [(c, min(P, W - c * P)) for c in range(-(-W // P))]

                def turn(j):
                    hh, i = items[j]
                    r, _, W = shape(i)
                    pe.wait_ge(sem("at_p"), n0 + j + 1)
                    if n0 + j:
                        pe.wait_ge(sem("at_pt"), n0 + j)
                    for c, w in pieces(W):
                        m = pe.transpose(aux[1][0:w, c // 4, (c % 4) * P:(c % 4) * P + r], sm[0:r, j % 2, c * P:c * P + w],
                                         ident[0:r, 0:r])
                    m.then_inc(sem("at_turned"), 1)

                def values(j):
                    hh, i = items[j]
                    r, _, W = shape(i)
                    s = ph.slot(hh)
                    if i == 0:
                        pe.wait_ge(evac[s], ph.nth(hh))
                    pe.wait_ge(sem("at_pt"), n0 + j + 1)
                    ps = pieces(W)
                    for c, w in ps:
                        out = acc[s][:, 0, i * P:(i + 1) * P] if i < NQT else acc[s][:, 1, 0:META]
                        m = pe.matmul(out, v[0:w, c, (hh // 4) * P:(hh // 4 + 1) * P], pts[0:w, c, 0:r],
                                      start=c == 0, stop=c == len(ps) - 1)
                    m.then_inc(sem("at_pv"), 1)

                pe.wait_ge(sem("qk_done"), (l + 1) * 10)
                pe.wait_ge(sem("cv_scaled"), (l + 1) * 8)
                scores(0)
                for j in range(len(items)):
                    if j + 1 < len(items):
                        scores(j + 1)
                    turn(j)
                    values(j)

            def neighbours():
                items = [(hh, i) for hh in range(HEADS) for i in range(NQT)]
                ph = AT["att2"]
                pe.wait_ge(sem("v2_rows"), 1)
                for e in range(4):
                    for c in range(4):
                        m = pe.transpose(aux[e // 2][:, e % 2, c * P:(c + 1) * P], vT2[:, e, c * P:(c + 1) * P], ident[:, :])
                m.then_inc(sem("v2_turned"), 1)
                pe.wait_ge(sem("v2_copied"), 4)

                def scores(j):
                    hh, i = items[j]
                    rows = slice(64 * (hh % 2), 64 * (hh % 2) + 64)
                    if j:
                        pe.wait_ge(sem("na_scored"), j)
                    pe.matmul(aux[0][:, 0, :], q2[rows, hh // 2, i * P:(i + 1) * P], k2[rows, hh // 2, :],
                              start=True, stop=True).then_inc(sem("na_s"), 1)

                def turn(j):
                    pe.wait_ge(sem("na_p"), j + 1)
                    if j:
                        pe.wait_ge(sem("na_pt"), j)
                    for c in range(4):
                        m = pe.transpose(aux[1][:, 0, c * P:(c + 1) * P], sm2[:, j % 2, c * P:(c + 1) * P], ident[:, :])
                    m.then_inc(sem("na_turned"), 1)

                def values(j):
                    hh, i = items[j]
                    s = ph.slot(hh // 2)
                    if hh % 2 == 0 and i == 0:
                        pe.wait_ge(evac[s], ph.nth(hh // 2))
                    pe.wait_ge(sem("na_pt"), j + 1)
                    for c in range(4):
                        m = pe.matmul(acc[s][64 * (hh % 2):64 * (hh % 2) + 64, 0, i * P:(i + 1) * P],
                                      v2[:, c, 64 * hh:64 * hh + 64], pts2[:, c, :], start=c == 0, stop=c == 3)
                    m.then_inc(sem("na_pv"), 1)

                scores(0)
                for j in range(len(items)):
                    if j + 1 < len(items):
                        scores(j + 1)
                    turn(j)
                    values(j)

            def ssm():
                for r in range(4):
                    pe.wait_ge(sem("ss_rep"), 2 * (r + 1))
                    pe.wait_ge(sem("ss_cpow"), 2 * (r + 1))
                    if r:
                        pe.wait_ge(sem("ss_y"), 16 * r)
                    for d in range(2):
                        for u in range(4):
                            e = d * 4 + u
                            pe.matmul(aux[0][:, d, u * P:(u + 1) * P], reps[:, 0, e].rearrange("p a b -> p (a b)"),
                                      cp_[:, 0, e, d:d + 4].rearrange("p a b -> p (a b)"), start=True, stop=False)
                            m = pe.matmul(aux[0][:, d, u * P:(u + 1) * P], reps[:, 1, e].rearrange("p a b -> p (a b)"),
                                          cp_[:, 1, e, d:d + 4].rearrange("p a b -> p (a b)"), start=False, stop=True)
                    m.then_inc(sem("ss_lags"), 1)
                    pe.wait_ge(sem("ss_bpow"), 4 * (r + 1))
                    for g in range(4):
                        if g or r:
                            pe.wait_ge(sem("ss_w1"), 4 * r + g)
                        for c in range(4):
                            e, z = (g * 4 + c) // 2, c % 2
                            m = pe.transpose(aux[1][:, 0, c * P:(c + 1) * P], ap_[:, z, e].rearrange("p a b -> p (a b)"),
                                             ident[:, :])
                        m.then_inc(sem("ss_w1_turned"), 1)
                    pe.wait_ge(sem("ss_w1"), 4 * (r + 1))
                    pe.wait_ge(sem("ss_u"), 32 * (r + 1))
                    pe.wait_ge(sem("ss_t"), r + 1)
                    for z in range(2):
                        for e in range(8):
                            m = pe.matmul(aux[z][:, e // 4, (e % 4) * NC:(e % 4 + 1) * NC], w1s[:, e, z],
                                          us[:, e // 4, e % 4], start=True, stop=True)
                    m.then_inc(sem("ss_s"), 1)
                    pe.wait_ge(sem("ss_x"), 4 * (r + 1))
                    for u in range(4):
                        out = aux[0][:, 0, u * NC:(u + 1) * NC]
                        pe.matmul(out, tm_[:, u], us[:, 0, u], start=True, stop=False)
                        for d in range(2):
                            for z in range(2):
                                lhs = cp_[:, z, d * 4 + u, 1 - d:5 - d].rearrange("p a b -> p (a b)")
                                m = pe.matmul(out, lhs, st_[:, z, d * 4 + u, d:d + NC], start=False, stop=(d, z) == (1, 1))
                    m.then_inc(sem("ss_out"), 1)

            pe.wait_ge(sem("consts_set"), 3)
            pe.wait_ge(sem("ident_loaded"), 16)
            for l in range(DEPTH):
                sumsq(2 * l)
                normed(2 * l)
                proj(l)
                index(l)
                rnn(l)
                merge(l, "rnn", 0)
                conv(l)
                merge(l, "conv", 1)
                attention(l)
                merge(l, "att", 2)
                pe.wait_ge(sem("br_lo"), (l * 4 + 4) * KD)
                with pe.Fori(0, KD // 2) as m:
                    for j in range(2):
                        tile(AT[f"out{l}"], j, R(bhi, blo, T1), T1, m=m, step=2)
                ffn(2 * l + 1, f"up{l}", f"down{l}", T1)
            ffn(4, "up2", "down2", SEQ)
            sumsq(5)
            normed(5)
            for i in range(12):
                tile(AT["qkv2"], i, R(nhi, nlo, S), S)
            for i in range(4):
                tile(AT["sin2"], i, R(nhi, nlo, S), S)
            neighbours()
            ssm()
            pe.wait_ge(sem("y_lo"), 4)
            for i in range(4):
                tile(AT["glu2"], i, R(zhi, zlo, S), S, nk=4)
            pe.wait_ge(sem("z_lo"), 4)
            with pe.Fori(0, KD) as m:
                tile(AT["mg2"], 0, R(nhi, nlo, S), S, m=m, step=4)
                tile(AT["mg2"], 1, R(attn_hi, attn_lo, S), S, nk=4, m=m, step=4)
                tile(AT["mg2"], 2, R(nhi, nlo, S), S, m=m, step=4)
                tile(AT["mg2"], 3, R(zhi, zlo, S), S, nk=4, m=m, step=4)
            pe.wait_ge(sem("m2_lo"), KD)
            with pe.Fori(0, KD // 2) as m:
                for j in range(2):
                    tile(AT["out2"], j, R(mhi, mlo, S), S, m=m, step=2)
            ffn(6, "up3", "down3", SEQ)
            sumsq(7)
            normed(7)
            pe.wait_ge(sem("p_lo"), 2)
            with pe.Fori(0, KD) as m:
                tile(AT["ple2"], 0, R(nhi, nlo, S), S, m=m, step=2)
                tile(AT["ple2"], 1, R(phi, plo, S), S, nk=2, m=m, step=2)
            sumsq(8)

        @block.scalar
        def _(act):
            def block_done(b):
                act.wait_ge(pe_block, b)

            def norm(i):
                T = NORM_T[i]
                if NORM_AFTER[i]:
                    h_ready(act, AT[NORM_AFTER[i]])
                else:
                    act.wait_ge(sem("h_loaded"), 16)
                for j in range(KD):
                    if j >= 2:
                        act.wait_ge(sem("norm_summed"), i * KD + j - 1)
                    act.activation(fsq[:, j % 2, 0:T], hview(T)[:, j], ACT.Square).then_inc(sem("norm_square"), 1)
                act.wait_ge(sem("norm_summed"), (i + 1) * KD)
                act.activation(halves(fstd[:, 0:T], T), aux[0][:, :, 0:T // 2], ACT.Sqrt, bias=EPS, scale=1.0 / D)\
                   .then_inc(sem("norm_std"), 1)
                if i == 8:
                    return
                for j in range(KD):
                    act.wait_ge(sem("norm_scaled"), i * KD + j + 1)
                    act.activation(nhi[:, j, 0:T], ftmp[:, j % 2, 0:T], ACT.Copy).then_inc(sem("norm_hi"), 1)

            def ffn(i, up, T):
                norm(i)
                ph, f = AT[up], FFI[up]
                with act.Fori(0, KF) as m:
                    block_done(m * 2 + (ph.block(0) + 1))
                    act.wait_ge(evac[ph.slot(1)], m + ph.nth(1))
                    act.activation(halves(fsl[:, 0:T], T), accv(ph.slot(0), T), ACT.Silu).then_inc(evac[ph.slot(0)], 1)
                    act.wait_ge(evac[ph.slot(1)], m + (ph.nth(1) + 1))
                    act.activation(ahi[:, bass.ds(m, 1), 0:T], fpr[:, 0:T].unsqueeze(1), ACT.Copy).then_inc(sem("ff_hi"), 1)

            def proj(l):
                qk, vp, qp = AT[f"qk{l}"], AT[f"v{l}"], AT[f"qi{l}"]

                def std(e):
                    it = l * 10 + e
                    act.wait_ge(sem("qk_sum"), it + 1)
                    if it:
                        act.wait_ge(sem("qk_done"), it)
                    act.activation(halves(tstd[:, :], T1), aux[0][:, :, 0:T1 // 2], ACT.Sqrt, bias=EPS, scale=1.0 / HD)\
                       .then_inc(sem("qk_std"), 1)

                for e in range(10):
                    it, s = l * 10 + e, qk.slot(e)
                    block_done(qk.block(e) + 1)
                    if e >= 2:
                        act.wait_ge(sem("qk_sum"), it - 1)
                    act.activation(halves(tsq[:, e % 2, :], T1), accv(s, T1), ACT.Square).then_inc(sem("qk_square"), 1)
                    if e >= 2:
                        act.wait_ge(sem("qk_done"), it - 1)
                    act.activation(halves(tqg[:, e % 2, :], T1), accv(s, T1), ACT.Copy,
                                   scale=col("q_g" if e < 8 else "k_g", l)).then_inc(evac[s], 1)
                    act.wait_ge(evac[s], qk.nth(e) + 1)
                    act.activation(tsw[0:64, e % 2, :], tqg[64:128, e % 2, :], ACT.Copy)
                    act.activation(tsw[64:128, e % 2, :], tqg[0:64, e % 2, :], ACT.Copy).then_inc(sem("qk_swap"), 1)
                    if e:
                        std(e - 1)
                for e in range(KV):
                    block_done(vp.block(e) + 1)
                    act.activation(halves(vT[:, e, :], T1), accv(vp.slot(e), T1), ACT.Copy).then_inc(evac[vp.slot(e)], 1)
                    if e == 0:
                        std(9)
                for e in range(5):
                    it, s = l * 5 + e, qp.slot(e)
                    block_done(qp.block(e) + 1)
                    if e < 2:
                        act.wait_ge(sem("qk_done"), (l + 1) * 10)
                    else:
                        act.wait_ge(sem("qi_done"), it - 1)
                    a, x, w = accv(s, T1), tqg[:, e % 2, :], tsw[:, e % 2, :]
                    if e < 4:
                        act.activation(halves(x, T1), a, ACT.Copy).then_inc(evac[s], 1)
                    else:
                        act.activation(halves(x[0:64], T1), a[0:64], ACT.Copy)
                        act.activation(halves(x[64:128], T1), a[0:64], ACT.Copy)
                        act.activation(halves(wbuf[:, :], T1), a[64:96], ACT.Copy, scale=IXH ** -0.5 * IXD ** -0.5)\
                           .then_inc(evac[s], 1)
                    act.wait_ge(evac[s], qp.nth(e) + 1)
                    for c in range(4):
                        m = act.activation(w[32 * c:32 * c + 32], x[32 * (c ^ 1):32 * (c ^ 1) + 32], ACT.Copy)
                    m.then_inc(sem("qi_swap"), 1)
                    if e == 3:
                        act.wait_ge(sem("v_turned"), l + 1)
                        for c in range(KV):
                            act.activation(v[:, 0:4, c * HD:(c + 1) * HD],
                                           aux[1][:, c, :].rearrange("p (a b) -> p a b", a=4), ACT.Copy).then_inc(sem("v_copied"), 1)
                            act.activation(v[0:16, 4, c * HD:(c + 1) * HD], aux[0][0:16, c, 0:P], ACT.Copy)\
                               .then_inc(sem("v_copied"), 1)
                    if e == 4:
                        act.wait_ge(evac[s], qp.nth(e) + 1)
                        act.sem_inc(sem("wi_rows"), 1)
                act.wait_ge(sem("wi_turned"), l + 1)
                act.activation(wi[:, :, :], aux[0][:, 1, 0:NQT * 32].rearrange("p (a b) -> p a b", a=NQT)[:, :, 0:IXH],
                               ACT.Copy).then_inc(sem("wi_copied"), 1)

            def index(l):
                for i in range(NQT):
                    W = META + P * (i + 1)
                    for hh in range(IXH):
                        it = (l * NQT + i) * IXH + hh
                        act.wait_ge(sem("ix_logit"), it + 1)
                        if hh >= 2 or i:
                            act.wait_ge(sem("ix_acc"), it - 1)
                        src = aux[hh % 2][:, :, :].rearrange("p a b -> p (a b)")[:, 0:W]
                        act.activation(tsq[:, hh % 2, 0:W], src, ACT.Relu).then_inc(sem("ix_relu"), 1)

            def rnn(l):
                ph = AT[f"rnn{l}"]

                def gates(n):
                    it = l * 8 + n
                    act.wait_ge(sem("rnn_gates"), it + 1)
                    if n:
                        act.wait_ge(sem("rnn_b"), it)
                    act.activation(halves(rr[:, :], T1), aux[0][:, :, 0:T1 // 2], ACT.Sigmoid, bias=col("ba", l, n))\
                       .then_inc(sem("rnn_r"), 1)
                    act.activation(halves(ri[:, :], T1), aux[1][:, :, 0:T1 // 2], ACT.Sigmoid, bias=col("bx", l, n))\
                       .then_inc(sem("rnn_i"), 1)
                    act.wait_ge(sem("rnn_r"), it + 1)
                    act.activation(rt[:, :], rr[:, :], ACT.Tanh, scale=spc[:, l, n:n + 1]).then_inc(sem("rnn_t"), 1)
                    if n:
                        act.wait_ge(sem("rnn_scan"), it)
                    act.activation(ra[:, :], rr[:, :], ACT.Exp, scale=nspc[:, l, n:n + 1]).then_inc(sem("rnn_a"), 1)
                    act.wait_ge(sem("rnn_m"), 3 * (it + 1))
                    act.activation(rb[:, :], rb[:, :], ACT.Sqrt, scale=2.0).then_inc(sem("rnn_sqrt"), 1)

                def part(n):
                    it = l * 8 + n
                    act.wait_ge(sem("rnn_out"), it + 1)
                    act.activation(bhi[:, n, :], rh[:, :], ACT.Copy).then_inc(sem("br_hi"), 1)

                act.wait_ge(sem("rnn_pad"), l + 1)
                for n in range(8):
                    it = l * 8 + n
                    sx, sy = ph.slot(2 * n), ph.slot(2 * n + 1)
                    block_done(ph.block(2 * n) + 1)
                    if n:
                        act.wait_ge(sem("rnn_conv"), 4 * it)
                    act.activation(halves(rx[:, CONV - 1:], T1), accv(sx, T1), ACT.Copy).then_inc(evac[sx], 1)
                    if n:
                        gates(n - 1)
                        part(n - 1)
                    block_done(ph.block(2 * n + 1) + 1)
                    act.activation(halves(rg[:, :], T1), accv(sy, T1), ACT.Gelu_apprx_tanh).then_inc(evac[sy], 1)
                gates(7)
                part(7)

            def merge(l, name):
                ph = AT[f"mg_{name}{l}"]
                with act.Fori(0, KD) as m:
                    block_done(m * 2 + (ph.block(0) + 1))
                    act.wait_ge(evac[ph.slot(1)], m + ph.nth(1))
                    act.activation(halves(sg[:, :], T1), accv(ph.slot(0), T1), ACT.Sigmoid).then_inc(evac[ph.slot(0)], 1)

            def conv(l):
                ph = AT[f"conv{l}"]
                for n in range(KD):
                    block_done(ph.block(2 * n + 1) + 1)
                    if n:
                        act.wait_ge(evac[ph.slot(0)], ph.nth(2 * n - 2) + 1)
                    act.activation(halves(sg[:, :], T1), accv(ph.slot(2 * n + 1), T1), ACT.Sigmoid)\
                       .then_inc(evac[ph.slot(2 * n + 1)], 1)
                act.wait_ge(sem("cv_mean"), l + 1)
                act.activation(halves(cstat[:, 0], T1), aux[0][:, :, 0:T1 // 2], ACT.Copy, scale=1.0 / D)\
                   .then_inc(sem("cv_mean_read"), 1)
                for n in range(KD):
                    act.wait_ge(sem("cv_centred"), l * 8 + n + 1)
                    if n >= 2:
                        act.wait_ge(sem("cv_summed"), l * 8 + n - 1)
                    act.activation(csq[:, n % 2], cu[:, n], ACT.Square).then_inc(sem("cv_square"), 1)
                act.wait_ge(sem("cv_summed"), (l + 1) * 8)
                act.activation(halves(cstat[:, 1], T1), aux[1][:, :, 0:T1 // 2], ACT.Sqrt, bias=EPS, scale=1.0 / D)\
                   .then_inc(sem("cv_std"), 1)
                for n in range(KD):
                    act.wait_ge(sem("cv_scaled"), l * 8 + n + 1)
                    act.activation(cu[:, n], cu[:, n], ACT.Silu, bias=col("ln_b", l, n), scale=col("ln_g", l, n))\
                       .then_inc(sem("cv_silu"), 1)
                    act.wait_ge(sem("cv_silu"), l * 8 + n + 1)
                    act.activation(bhi[:, n], cu[:, n], ACT.Copy).then_inc(sem("br_hi"), 1)

            def attention(l):
                ph = AT[f"att{l}"]
                items = [(hh, i) for hh in range(HEADS) for i in range(NQT + 1)]
                n0 = l * len(items)

                def exps(j):
                    r, W = (P, META + (items[j][1] + 1) * P) if items[j][1] < NQT else (META, META)
                    act.wait_ge(sem("at_max"), n0 + j + 1)
                    act.activation(sm[0:r, j % 2, 0:W], sm[0:r, j % 2, 0:W], ACT.Exp, bias=nmx[0:r, j % 2:j % 2 + 1],
                                   accum_out=rsum[0:r, j % 2:j % 2 + 1]).then_inc(sem("at_exp"), 1)

                def turned(j):
                    i = items[j][1]
                    act.wait_ge(sem("at_turned"), n0 + j + 1)
                    if j:
                        act.wait_ge(sem("at_pv"), n0 + j)
                    if i < NQT:
                        c = i + 1
                        act.activation(pts[:, 0:c, :], aux[1][:, :, :].rearrange("p a (b c) -> p (a b) c", c=P)[:, 0:c, :], ACT.Copy)
                        act.activation(pts[0:META, c, :], aux[1][0:META, c // 4, (c % 4) * P:(c % 4 + 1) * P], ACT.Copy)\
                           .then_inc(sem("at_pt"), 1)
                    else:
                        act.activation(pts[0:META, 0, 0:META], aux[1][0:META, 0, 0:META], ACT.Copy).then_inc(sem("at_pt"), 1)

                exps(0)
                for j in range(len(items)):
                    hh, i = items[j]
                    if j + 1 < len(items):
                        exps(j + 1)
                    turned(j)
                    if i == NQT:
                        s = ph.slot(hh)
                        act.wait_ge(sem("at_pv"), n0 + j + 1)
                        if hh:
                            act.wait_ge(sem("br_lo"), (l * 4 + 2) * KD + hh)
                        act.activation(ot[:, META:], acc[s][:, 0, :], ACT.Copy)
                        act.activation(ot[:, 0:META], acc[s][:, 1, 0:META], ACT.Copy).then_inc(evac[s], 1)
                        act.wait_ge(evac[s], ph.nth(hh) + 1)
                        act.activation(bhi[:, hh], ot[:, :], ACT.Copy).then_inc(sem("br_hi"), 1)

            def neighbours():
                ph = AT["att2"]
                act.wait_ge(sem("v2_turned"), 1)
                for e in range(4):
                    act.activation(v2[:, :, e * P:(e + 1) * P], aux[e // 2][:, e % 2, :].rearrange("p (a b) -> p a b", a=4),
                                   ACT.Copy).then_inc(sem("v2_copied"), 1)
                for e in range(HEADS):
                    act.wait_ge(sem("na_table_masked"), 1)
                items = [(hh, i) for hh in range(HEADS) for i in range(NQT)]

                def exps(j):
                    act.wait_ge(sem("na_max"), j + 1)
                    act.activation(sm2[:, j % 2], sm2[:, j % 2], ACT.Exp, bias=sc2[:, 1, j % 2:j % 2 + 1],
                                   accum_out=sc2[:, 2, j % 2:j % 2 + 1]).then_inc(sem("na_exp"), 1)

                exps(0)
                for j in range(len(items)):
                    hh, i = items[j]
                    if j + 1 < len(items):
                        exps(j + 1)
                    act.wait_ge(sem("na_turned"), j + 1)
                    if j:
                        act.wait_ge(sem("na_pv"), j)
                    act.activation(pts2[:, :, :], aux[1][:, 0, :].rearrange("p (a b) -> p a b", a=4), ACT.Copy)\
                       .then_inc(sem("na_pt"), 1)
                    if hh % 2 and i == NQT - 1:
                        s, t = ph.slot(hh // 2), hh // 2
                        act.wait_ge(sem("na_pv"), j + 1)
                        if t:
                            act.wait_ge(sem("attn2_lo"), t)
                        act.activation(ot2[:, :], acc[s][:, 0, :], ACT.Copy).then_inc(evac[s], 1)
                        act.wait_ge(evac[s], ph.nth(t) + 1)
                        act.activation(attn_hi[:, t], ot2[:, :], ACT.Copy).then_inc(sem("attn2_hi"), 1)

            def ssm():
                act.wait_ge(sem("attn2_lo"), 4)
                act.dma_start(smp[:, :, :], A_ssm[0:3].rearrange("a p n -> p a n")[:, :, 0:32]).then_inc(sem("ssm_loaded"), 16)
                act.dma_start(sbc[:, :, :, :].rearrange("p a b c -> p a (b c)"), A_ssm[3:7].rearrange("a p n -> p a n"))\
                   .then_inc(sem("ssm_loaded"), 16)
                act.dma_start(chk[:, :], A_chunk).then_inc(sem("ssm_loaded"), 16)
                act.wait_ge(sem("ssm_loaded"), 48)
                act.activation(spw[:, 0], smp[:, 0], ACT.Exp).then_inc(sem("ss_dt"), 1)
                act.wait_ge(sem("ss_reduced"), 1)
                act.activation(spw[:, 4], spw[:, 2], ACT.Sin)
                act.activation(spw[:, 5], spw[:, 2], ACT.Sin, scale=0.5)
                act.activation(spw[:, 6], spw[:, 1], ACT.Tanh, scale=0.5)
                act.activation(spw[:, 7], spw[:, 1], ACT.Exp, scale=4.0).then_inc(sem("ss_waves"), 1)
                for r in range(4):
                    if r:
                        act.wait_ge(sem("ss_out"), r)
                    for u in range(4):
                        src = uin[32 * u:32 * u + 32, r, :].rearrange("p (c j) -> p j c", j=SC)
                        for j in range(SC):
                            act.activation(us[32 * j:32 * j + 32, 0, u, :], src[:, j, :], ACT.Copy).then_inc(sem("ss_u"), 1)
                            act.activation(us[32 * j:32 * j + 32, 1, u, :], src[:, j, ::-1], ACT.Copy).then_inc(sem("ss_u"), 1)
                    act.wait_ge(sem("ss_bb"), r + 1)
                    for z in range(2):
                        act.activation(reps[:, z], bb[:, z].unsqueeze(2).broadcast_to([P, 8, 4, 32]), ACT.Copy)\
                           .then_inc(sem("ss_rep"), 1)
                    act.wait_ge(sem("ss_angle"), r + 1)
                    act.activation(cs_[:, 1], w8[:, :, :], ACT.Sin)
                    act.activation(cs_[:, 0], w8[:, :, :], ACT.Sin, scale=0.5).then_inc(sem("ss_sines"), 1)
                    act.wait_ge(sem("ss_lags"), r + 1)
                    act.wait_ge(sem("ss_t_zero"), r + 1)
                    lag = aux[0][:, 0, :].rearrange("p (u c) -> p u c", u=4)
                    for j in range(SC):
                        m = act.activation(tm_[32 * j:32 * j + 32, :, 32 * j:P], lag[32 * j:32 * j + 32, :, 0:P - 32 * j], ACT.Copy)
                    m.then_inc(sem("ss_t_forward"), 1)
                    for g in range(4):
                        act.wait_ge(sem("ss_w1_turned"), 4 * r + g + 1)
                        act.activation(w1s[:, 2 * g:2 * g + 2].rearrange("p a b c -> p (a b c)"), aux[1][:, 0, :], ACT.Copy)\
                           .then_inc(sem("ss_w1"), 1)
                    act.wait_ge(sem("ss_out"), r + 1)
                    for u in range(4):
                        dst = yv[32 * u:32 * u + 32, r, :].rearrange("p (c j) -> p j c", j=SC)
                        for j in range(SC):
                            act.activation(dst[:, j, :], aux[0][32 * j:32 * j + 32, 0, u * NC:(u + 1) * NC], ACT.Copy)\
                               .then_inc(sem("ss_y"), 1)
                for r in range(4):
                    act.wait_ge(sem("ss_skip"), r + 1)
                    act.activation(yv[:, r], yv[:, r], ACT.Gelu_apprx_tanh).then_inc(sem("y_gelu"), 1)
                for r in range(4):
                    act.wait_ge(sem("y_gelu"), r + 1)
                    act.activation(zhi[:, r], yv[:, r], ACT.Copy).then_inc(sem("y_hi"), 1)
                ph = AT["glu2"]
                for i in range(4):
                    block_done(ph.block(i) + 1)
                    act.activation(halves(uin[:, i], S), accv(ph.slot(i), S), ACT.Sigmoid, bias=col("glu_b", None, i))\
                       .then_inc(evac[ph.slot(i)], 1)
                for i in range(4):
                    act.wait_ge(sem("z_done"), i + 1)
                    if i == 0:
                        block_done(ph.block(3) + 1)
                    act.activation(zhi[:, i], yv[:, i], ACT.Copy).then_inc(sem("z_hi"), 1)

            act.dma_start(h[:, :, :], A_h).then_inc(sem("h_loaded"), 16)
            act.dma_start(par[:, :], A_par).then_inc(sem("par_loaded"), 16)
            act.dma_start(ident[:, :], A_ident).then_inc(sem("ident_loaded"), 16)
            act.wait_ge(sem("par_loaded"), 16)
            act.wait_ge(sem("lam_abs"), 1)
            act.activation(prep[:, 1, :], prep[:, 0, :], ACT.Exp, scale=-1.0).then_inc(sem("lam_exp"), 1)
            act.wait_ge(sem("spc_done"), 1)
            for l in range(DEPTH):
                norm(2 * l)
                act.wait_ge(sem("norm_lo"), (2 * l + 1) * KD)
                act.dma_start(rope[:, :, :], A_rope.rearrange("a p n -> p a n")).then_inc(sem("rope_loaded"), 16)
                act.dma_start(rnn_w[:, :, :, :].rearrange("p a b c -> p a (b c)"), A_gate[l].rearrange("a p n -> p a n"))\
                   .then_inc(sem("rnn_w_loaded"), 16)
                proj(l)
                index(l)
                rnn(l)
                merge(l, "rnn")
                conv(l)
                merge(l, "conv")
                attention(l)
                merge(l, "att")
                for n in range(KD):
                    if n == 0:
                        act.wait_ge(sem("mg_add"), (2 * l + 2) * KD + 1)
                        block_done(AT[f"out{l}"].b0)
                    act.activation(bhi[:, n], merged[:, n], ACT.Copy).then_inc(sem("br_hi"), 1)
                ffn(2 * l + 1, f"up{l}", T1)
            ffn(4, "up2", SEQ)
            norm(5)
            act.wait_ge(sem("norm_lo"), 6 * KD)
            act.dma_start(namask[:, :], A_namask).then_inc(sem("na_loaded"), 16)
            ph = AT["qkv2"]
            for i in range(12):
                s = ph.slot(i)
                dst = (q2, k2, vT2)[i // 4][:, i % 4]
                block_done(ph.block(i) + 1)
                act.activation(halves(dst, S), accv(s, S), ACT.Copy, scale=HD2 ** -0.5 if i < 4 else 1.0).then_inc(evac[s], 1)
            h_ready(act, ph)
            act.sem_inc(sem("v2_rows"), 1)
            ph = AT["sin2"]
            for i in range(4):
                block_done(ph.block(i) + 1)
                act.activation(halves(uin[:, i], S), accv(ph.slot(i), S), ACT.Copy).then_inc(evac[ph.slot(i)], 1)
            act.wait_ge(sem("v2_turned"), 1)
            for half in range(2):
                for hh in range(HEADS):
                    act.dma_start(natab[64 * half:64 * half + 64, hh], A_natab[half, hh]).then_inc(sem("na_loaded"), 16)
            neighbours()
            ssm()
            ph = AT["mg2"]
            with act.Fori(0, KD) as m:
                for z in range(2):
                    block_done(m * 4 + (ph.block(2 * z) + 1))
                    act.wait_ge(evac[ph.slot(1)], m * 2 + (ph.nth(1) + z))
                    act.activation(halves(sg2[:, :], S), accv(ph.slot(0), S), ACT.Sigmoid).then_inc(evac[ph.slot(0)], 1)
            for n in range(KD):
                act.wait_ge(sem("m2_add"), n + 2)
                act.activation(mhi[:, n], merged2[:, n], ACT.Copy).then_inc(sem("m2_hi"), 1)
            ffn(6, "up3", SEQ)
            norm(7)
            act.wait_ge(sem("norm_lo"), 8 * KD)
            act.dma_start(pin[:, :, :], A_p.rearrange("a p n -> p a n")).then_inc(sem("p_loaded"), 16)
            act.wait_ge(sem("p_loaded"), 16)
            act.activation(phi[:, :, :], pin[:, :, :], ACT.Copy).then_inc(sem("p_hi"), 1)
            ph = AT["ple2"]
            with act.Fori(0, KD) as m:
                block_done(m * 2 + (ph.block(0) + 1))
                act.wait_ge(evac[ph.slot(1)], m + ph.nth(1))
                act.activation(halves(psg[:, :], S), accv(ph.slot(0), S), ACT.Sigmoid).then_inc(evac[ph.slot(0)], 1)
            act.wait_ge(sem("ple_added"), KD + 1)
            norm(8)

        @block.vector
        def _(dve):
            def block_done(b):
                dve.wait_ge(pe_block, b)

            chain = [0]

            def then(ins):
                chain[0] += 1
                ins.then_inc(sem("dve_step"), 1)
                dve.wait_ge(sem("dve_step"), chain[0])

            def norm(i):
                T = NORM_T[i]
                name, l = NORM_G[i]
                if NORM_AFTER[i]:
                    h_ready(dve, AT[NORM_AFTER[i]])
                dve.wait_ge(sem("norm_std"), i + 1)
                then(dve.reciprocal(frs[:, 0:T], fstd[:, 0:T]))
                for j in range(KD):
                    if i < 8:
                        if j >= 2:
                            dve.wait_ge(sem("norm_lo"), i * KD + j - 1)
                        dve.scalar_tensor_tensor(ftmp[:, j % 2, 0:T], hview(T)[:, j], col(name, l, j), frs[:, 0:T],
                                                 ALU.mult, ALU.mult).then_inc(sem("norm_scaled"), 1)
                        dve.wait_ge(sem("norm_hi"), i * KD + j + 1)
                        dve.tensor_tensor(nlo[:, j, 0:T], ftmp[:, j % 2, 0:T], nhi[:, j, 0:T].bitcast(F32), ALU.subtract)\
                           .then_inc(sem("norm_lo"), 1)
                    else:
                        dve.scalar_tensor_tensor(yout[:, j], hview(T)[:, j], col(name, l, j), frs[:, 0:T],
                                                 ALU.mult, ALU.mult).then_inc(sem("final_out"), 1)

            def ffn(i, up, down, T, scale):
                norm(i)
                ph, f = AT[up], FFI[up]
                with dve.Fori(0, KF) as m:
                    block_done(m * 2 + (ph.block(1) + 1))
                    dve.wait_ge(evac[ph.slot(0)], m + (ph.nth(0) + 1))
                    dve.wait_ge(sem("ff_lo"), m + (f * KF + 1))
                    dve.tensor_tensor(halves(fpr[:, 0:T], T), accv(ph.slot(1), T), halves(fsl[:, 0:T], T), ALU.mult)\
                       .then_inc(evac[ph.slot(1)], 1)
                    dve.wait_ge(sem("ff_hi"), m + (f * KF + 1))
                    dve.tensor_tensor(alo[:, bass.ds(m, 1), 0:T], fpr[:, 0:T].unsqueeze(1),
                                      ahi[:, bass.ds(m, 1), 0:T].bitcast(F32), ALU.subtract).then_inc(sem("ff_lo"), 1)
                add_to_h(AT[down], T, scale)

            def add_to_h(ph, T, scale=1.0):
                with dve.Fori(0, KD // 2) as m:
                    for j in range(2):
                        s = ph.slot(j)
                        block_done(m * (2 * ph.per) + (ph.block(j) + ph.per))
                        hv = h[:, bass.ds(m * 2 + j, 1), T1 - T:T1].rearrange("p a (b c) -> p (a b) c", b=2)
                        if scale == 1.0:
                            dve.tensor_tensor(hv, accv(s, T), hv, ALU.add).then_inc(evac[s], 1)
                        else:
                            dve.scalar_tensor_tensor(hv, accv(s, T), scale, hv, ALU.mult, ALU.add).then_inc(evac[s], 1)

            def proj(l):
                dve.wait_ge(sem("rope_loaded"), 16 * (l + 1))
                for e in range(10):
                    it = l * 10 + e
                    x, w = tqg[:, e % 2], tsw[:, e % 2]
                    dve.wait_ge(sem("qk_swap"), it + 1)
                    then(dve.tensor_tensor(x, x, rope[:, 0], ALU.mult))
                    then(dve.tensor_tensor(w, w, rope[:, 1], ALU.mult))
                    then(dve.tensor_tensor(x, x, w, ALU.add))
                    dve.wait_ge(sem("qk_std"), it + 1)
                    then(dve.reciprocal(trs[:, :], tstd[:, :]))
                    dst = q[:, e] if e < 8 else k[:, e - 8]
                    dve.tensor_tensor(dst, x, trs[:, :], ALU.mult).then_inc(sem("qk_done"), 1)
                for e in range(5):
                    x, w = tqg[:, e % 2], tsw[:, e % 2]
                    dve.wait_ge(sem("qi_swap"), l * 5 + e + 1)
                    then(dve.tensor_tensor(x, x, rope[:, 2], ALU.mult))
                    then(dve.tensor_tensor(w, w, rope[:, 3], ALU.mult))
                    dst = qi[:, e] if e < 4 else ki[:, :]
                    dve.tensor_tensor(dst, x, w, ALU.add).then_inc(sem("qi_done"), 1)

            def index(l):
                dve.wait_ge(sem("wi_copied"), l + 1)
                for i in range(NQT):
                    W = META + P * (i + 1)
                    sc = mask[:, i, 0:W]
                    for hh in range(IXH):
                        it = (l * NQT + i) * IXH + hh
                        r, w = tsq[:, hh % 2, 0:W], wi[:, i, hh:hh + 1]
                        dve.wait_ge(sem("ix_relu"), it + 1)
                        if hh == 0:
                            dve.tensor_scalar(sc, r, w, None, ALU.mult).then_inc(sem("ix_acc"), 1)
                        else:
                            dve.wait_ge(sem("ix_acc"), it)
                            dve.scalar_tensor_tensor(sc, r, w, sc, ALU.mult, ALU.add).then_inc(sem("ix_acc"), 1)
                    dve.wait_ge(sem("ix_acc"), (l * NQT + i + 1) * IXH)
                    then(dve.memset(mask[0:CHUNK, i, W - CHUNK:W], BARRED))
                    for n in range(TOPK // 8):
                        then(dve.max(top8[:, :], sc))
                        then(dve.match_replace(sc, top8[:, :], sc, CHOSEN))
                    then(dve.tensor_scalar(sc, sc, CHOSEN, NEG, ALU.not_equal, ALU.mult))
                    then(dve.memset(mask[0:CHUNK, i, W - CHUNK:W], NEG))

            def rnn(l):
                dve.wait_ge(sem("ix_relu"), (l + 1) * NQT * IXH)
                dve.memset(rx[:, 0:CONV - 1], 0.0).then_inc(sem("rnn_pad"), 1)
                dve.wait_ge(sem("rnn_pad"), l + 1)
                ph = AT[f"rnn{l}"]

                def taps(n):
                    it = l * 8 + n
                    dve.wait_ge(evac[ph.slot(2 * n)], ph.nth(2 * n) + 1)
                    if n:
                        dve.wait_ge(sem("rnn_iu"), it)
                    for j in range(CONV):
                        t = CONV - 1 - j
                        w = col("cw", l, t * 8 + n)
                        if j == 0:
                            dve.tensor_scalar(ru[:, :], rx[:, t:t + T1], w, col("cb", l, n), ALU.mult, ALU.add)\
                               .then_inc(sem("rnn_conv"), 1)
                        else:
                            dve.wait_ge(sem("rnn_conv"), 4 * it + j)
                            dve.scalar_tensor_tensor(ru[:, :], rx[:, t:t + T1], w, ru[:, :], ALU.mult, ALU.add)\
                               .then_inc(sem("rnn_conv"), 1)

                def rest(n):
                    it = l * 8 + n
                    dve.wait_ge(sem("rnn_i"), it + 1)
                    dve.tensor_tensor(ri[:, :], ri[:, :], ru[:, :], ALU.mult).then_inc(sem("rnn_iu"), 1)
                    dve.wait_ge(sem("rnn_t"), it + 1)
                    dve.tensor_scalar(rb[:, :], rt[:, :], 1.0, None, ALU.add).then_inc(sem("rnn_m"), 1)
                    dve.wait_ge(sem("rnn_m"), 3 * it + 1)
                    dve.reciprocal(rb[:, :], rb[:, :]).then_inc(sem("rnn_m"), 1)
                    dve.wait_ge(sem("rnn_m"), 3 * it + 2)
                    dve.tensor_tensor(rb[:, :], rb[:, :], rt[:, :], ALU.mult).then_inc(sem("rnn_m"), 1)
                    dve.wait_ge(sem("rnn_sqrt"), it + 1)
                    dve.wait_ge(sem("rnn_iu"), it + 1)
                    dve.tensor_tensor(rb[:, :], rb[:, :], ri[:, :], ALU.mult).then_inc(sem("rnn_b"), 1)
                    dve.wait_ge(sem("rnn_b"), it + 1)
                    dve.wait_ge(sem("rnn_a"), it + 1)
                    dve.tensor_tensor_scan(rh[:, :], ra[:, :], rb[:, :], 0.0, ALU.mult, ALU.add).then_inc(sem("rnn_scan"), 1)
                    dve.wait_ge(sem("rnn_scan"), it + 1)
                    dve.wait_ge(evac[ph.slot(2 * n + 1)], ph.nth(2 * n + 1) + 1)
                    dve.tensor_tensor(rh[:, :], rh[:, :], rg[:, :], ALU.mult).then_inc(sem("rnn_out"), 1)
                    dve.wait_ge(sem("br_hi"), (l * 4) * KD + n + 1)
                    dve.tensor_tensor(blo[:, n], rh[:, :], bhi[:, n].bitcast(F32), ALU.subtract).then_inc(sem("br_lo"), 1)

                taps(0)
                for n in range(8):
                    rest(n)
                    if n < 7:
                        taps(n + 1)

            def merge(l, name, inst):
                ph = AT[f"mg_{name}{l}"]
                with dve.Fori(0, KD) as m:
                    block_done(m * 2 + (ph.block(1) + 1))
                    dve.wait_ge(evac[ph.slot(0)], m + (ph.nth(0) + 1))
                    a, g = accv(ph.slot(1), T1), halves(sg[:, :], T1)
                    mg = merged[:, bass.ds(m, 1), :]
                    if inst == 0:
                        dve.tensor_tensor(mg.rearrange("p a (b c) -> p (a b) c", b=2), a, g, ALU.mult).then_inc(evac[ph.slot(1)], 1)
                    else:
                        dve.wait_ge(sem("mg_add"), m + ((2 * l + inst - 1) * KD + 1))
                        dve.tensor_tensor(halves(mt[:, :], T1), a, g, ALU.mult).then_inc(evac[ph.slot(1)], 1)
                        dve.wait_ge(evac[ph.slot(1)], m + (ph.nth(1) + 1))
                        dve.tensor_tensor(mg, mg, mt[:, :].unsqueeze(1), ALU.add).then_inc(sem("mg_add"), 1)

            def conv(l):
                ph = AT[f"conv{l}"]
                then(dve.memset(cx[:, 0:DW - 1], 0.0))
                for n in range(KD):
                    s0, s1 = ph.slot(2 * n), ph.slot(2 * n + 1)
                    dve.wait_ge(evac[s1], ph.nth(2 * n + 1) + 1)
                    if n:
                        dve.wait_ge(sem("cv_conv"), (l * 8 + n) * DW)
                    dve.tensor_tensor(halves(cx[:, DW - 1:], T1), accv(s0, T1), halves(sg[:, :], T1), ALU.mult)\
                       .then_inc(evac[s0], 1)
                    dve.wait_ge(evac[s0], ph.nth(2 * n) + 1)
                    for j in range(DW):
                        t = DW - 1 - j
                        w = col("dw", l, t * 8 + n)
                        c = (l * 8 + n) * DW + j
                        if j == 0:
                            dve.tensor_scalar(cu[:, n], cx[:, t:t + T1], w, col("db", l, n), ALU.mult, ALU.add)\
                               .then_inc(sem("cv_conv"), 1)
                        else:
                            dve.wait_ge(sem("cv_conv"), c)
                            dve.scalar_tensor_tensor(cu[:, n], cx[:, t:t + T1], w, cu[:, n], ALU.mult, ALU.add)\
                               .then_inc(sem("cv_conv"), 1)
                dve.wait_ge(sem("cv_mean_read"), l + 1)
                for n in range(KD):
                    dve.tensor_tensor(cu[:, n], cu[:, n], cstat[:, 0], ALU.subtract).then_inc(sem("cv_centred"), 1)
                dve.wait_ge(sem("cv_std"), l + 1)
                then(dve.reciprocal(cstat[:, 2], cstat[:, 1]))
                for n in range(KD):
                    dve.tensor_tensor(cu[:, n], cu[:, n], cstat[:, 2], ALU.mult).then_inc(sem("cv_scaled"), 1)
                for n in range(KD):
                    dve.wait_ge(sem("br_hi"), (l * 4 + 1) * KD + n + 1)
                    dve.tensor_tensor(blo[:, n], cu[:, n], bhi[:, n].bitcast(F32), ALU.subtract).then_inc(sem("br_lo"), 1)

            def attention(l):
                items = [(hh, i) for hh in range(HEADS) for i in range(NQT + 1)]
                n0 = l * len(items)

                def score(j):
                    hh, i = items[j]
                    r, W = (P, META + (i + 1) * P) if i < NQT else (META, META)
                    b = j % 2
                    dve.wait_ge(sem("at_s"), n0 + j + 1)
                    if j >= 2:
                        dve.wait_ge(sem("at_turned"), n0 + j - 1)
                    src = aux[0][0:r].rearrange("p a b -> p (a b)")[:, 0:W]
                    add = mask[0:r, i, 0:W] if i < NQT else zeros[0:r, 0:W]
                    dve.tensor_tensor_reduce(sm[0:r, b, 0:W], src, add, float(HD) ** -0.5, CHOSEN, ALU.add, ALU.max,
                                             mx[0:r, b:b + 1]).then_inc(sem("at_scored"), 1)
                    dve.wait_ge(sem("at_scored"), n0 + j + 1)
                    dve.tensor_scalar(nmx[0:r, b:b + 1], mx[0:r, b:b + 1], -1.0, None, ALU.mult).then_inc(sem("at_max"), 1)

                def share(j):
                    hh, i = items[j]
                    r, W = (P, META + (i + 1) * P) if i < NQT else (META, META)
                    b = j % 2
                    dve.wait_ge(sem("at_exp"), n0 + j + 1)
                    then(dve.reciprocal(rrs[0:r, b:b + 1], rsum[0:r, b:b + 1]))
                    dve.tensor_scalar(sm[0:r, b, 0:W], sm[0:r, b, 0:W], rrs[0:r, b:b + 1], None, ALU.mult)\
                       .then_inc(sem("at_p"), 1)

                score(0)
                for j in range(len(items)):
                    if j + 1 < len(items):
                        score(j + 1)
                    share(j)
                    if items[j][1] == NQT:
                        hh = items[j][0]
                        dve.wait_ge(sem("br_hi"), (l * 4 + 2) * KD + hh + 1)
                        dve.tensor_tensor(blo[:, hh], ot[:, :], bhi[:, hh].bitcast(F32), ALU.subtract).then_inc(sem("br_lo"), 1)

            def neighbours():
                dve.wait_ge(sem("na_loaded"), 16 * 17)
                for hh in range(HEADS):
                    m = dve.tensor_tensor(natab[:, hh], natab[:, hh], namask[:, :].unsqueeze(1).broadcast_to([P, NAR, GW]),
                                          ALU.add)
                m.then_inc(sem("na_table_masked"), 1)
                dve.wait_ge(sem("na_table_masked"), 1)
                items = [(hh, i) for hh in range(HEADS) for i in range(NQT)]

                def score(j):
                    hh, i = items[j]
                    b = j % 2
                    dve.wait_ge(sem("na_s"), j + 1)
                    if j >= 2:
                        dve.wait_ge(sem("na_turned"), j - 1)
                    add = natab[:, hh, 6 - 2 * i:14 - 2 * i].rearrange("p a b -> p (a b)")
                    dve.tensor_tensor_reduce(sm2[:, b], aux[0][:, 0, :], add, 1.0, CHOSEN, ALU.add, ALU.max,
                                             sc2[:, 0, b:b + 1]).then_inc(sem("na_scored"), 1)
                    dve.wait_ge(sem("na_scored"), j + 1)
                    dve.tensor_scalar(sc2[:, 1, b:b + 1], sc2[:, 0, b:b + 1], -1.0, None, ALU.mult).then_inc(sem("na_max"), 1)

                score(0)
                for j in range(len(items)):
                    hh, i = items[j]
                    b = j % 2
                    if j + 1 < len(items):
                        score(j + 1)
                    dve.wait_ge(sem("na_exp"), j + 1)
                    then(dve.reciprocal(sc2[:, 3, b:b + 1], sc2[:, 2, b:b + 1]))
                    dve.tensor_scalar(sm2[:, b], sm2[:, b], sc2[:, 3, b:b + 1], None, ALU.mult).then_inc(sem("na_p"), 1)
                    if hh % 2 and i == NQT - 1:
                        dve.wait_ge(sem("attn2_hi"), hh // 2 + 1)
                        dve.tensor_tensor(attn_lo[:, hh // 2], ot2[:, :], attn_hi[:, hh // 2].bitcast(F32), ALU.subtract)\
                           .then_inc(sem("attn2_lo"), 1)

            C1, C2, C3 = two_pi_parts()

            def reduce_angle(out, kk, x):
                then(dve.tensor_scalar(kk, x, float(1.0 / TWO_PI), MAGIC, ALU.mult, ALU.add))
                then(dve.tensor_scalar(kk, kk, MAGIC, None, ALU.subtract))
                then(dve.scalar_tensor_tensor(out, kk, -C1, x, ALU.mult, ALU.add))
                then(dve.scalar_tensor_tensor(out, kk, -C2, out, ALU.mult, ALU.add))
                then(dve.scalar_tensor_tensor(out, kk, -C3, out, ALU.mult, ALU.add))
                then(dve.tensor_scalar(out, out, PI_SAFE, -PI_SAFE, ALU.min, ALU.max))

            def ssm():
                w = lambda j: spw[:, j]
                tt = lambda o_, a, b_, op: then(dve.tensor_tensor(o_, a, b_, op))
                dve.wait_ge(sem("ss_dt"), 1)
                lre, lim = smp[:, 1], smp[:, 2]
                then(dve.tensor_scalar(lre, lre, -1e-4, None, ALU.min))
                tt(w(1), lre, w(0), ALU.mult)
                tt(w(3), lim, w(0), ALU.mult)
                reduce_angle(w(2), w(8), w(3))
                dve.sem_inc(sem("ss_reduced"), 1)
                tt(w(8), lre, lre, ALU.mult)
                tt(w(9), lim, lim, ALU.mult)
                tt(w(8), w(8), w(9), ALU.add)
                then(dve.reciprocal(w(8), w(8)))
                dve.wait_ge(sem("ss_waves"), 1)
                then(dve.tensor_scalar(w(9), w(6), -1.0, 1.0, ALU.mult, ALU.add))
                then(dve.reciprocal(w(9), w(9)))
                then(dve.scalar_tensor_tensor(w(9), w(6), 2.0, w(9), ALU.mult, ALU.mult))
                then(dve.scalar_tensor_tensor(w(10), w(5), -2.0, w(5), ALU.mult, ALU.mult))
                tt(w(11), w(9), w(10), ALU.mult)
                tt(w(11), w(11), w(9), ALU.add)
                tt(w(11), w(11), w(10), ALU.add)
                then(dve.scalar_tensor_tensor(w(12), w(9), 1.0, w(4), ALU.add, ALU.mult))
                tt(w(13), w(11), lre, ALU.mult)
                tt(w(14), w(12), lim, ALU.mult)
                tt(w(13), w(13), w(14), ALU.add)
                tt(w(13), w(13), w(8), ALU.mult)
                tt(w(14), w(12), lre, ALU.mult)
                tt(w(15), w(11), lim, ALU.mult)
                tt(w(14), w(14), w(15), ALU.subtract)
                tt(w(14), w(14), w(8), ALU.mult)
                then(dve.tensor_scalar(w(11), w(11), 1.0, None, ALU.add))
                then(dve.memset(w(16), 1.0))
                then(dve.memset(w(17), 0.0))
                for p in range(5):
                    for src, c_, b_ in ((w(16), lc_r, lb_r), (w(17), lc_i, lb_i)):
                        s4 = src.rearrange("p (r d u) -> p r d u", r=4, d=2)
                        c4 = c_[:, :, :].rearrange("p (r d u) k -> p r d u k", r=4, d=2)
                        b4 = b_[:, :, :].rearrange("p (r d u) k -> p r d u k", r=4, d=2)
                        then(dve.tensor_copy(c4[:, :, 0, :, p], s4[:, :, 0, :]))
                        then(dve.tensor_copy(c4[:, :, 1, :, 4 - p], s4[:, :, 1, :]))
                        if p < 4:
                            then(dve.tensor_copy(b4[:, :, 0, :, 3 - p], s4[:, :, 0, :]))
                            then(dve.tensor_copy(b4[:, :, 1, :, p], s4[:, :, 1, :]))
                    if p < 4:
                        tt(w(15), w(16), w(12), ALU.mult)
                        tt(w(16), w(16), w(11), ALU.mult)
                        tt(w(18), w(17), w(12), ALU.mult)
                        tt(w(16), w(16), w(18), ALU.subtract)
                        tt(w(17), w(17), w(11), ALU.mult)
                        tt(w(17), w(17), w(15), ALU.add)
                then(dve.tensor_scalar(w(3), w(2), float(SC), None, ALU.mult))
                reduce_angle(w(2), w(0), w(3))

                for r in range(4):
                    u8 = slice(8 * r, 8 * r + 8)
                    f = [w(13)[:, u8].unsqueeze(2).broadcast_to([P, 8, 32]), w(14)[:, u8].unsqueeze(2).broadcast_to([P, 8, 32])]
                    b_, c_ = [sbc[:, 0, u8], sbc[:, 1, u8]], [sbc[:, 2, u8], sbc[:, 3, u8]]
                    t3 = w8[:, :, 0:32]
                    if r:
                        dve.wait_ge(sem("ss_rep"), 2 * r)
                        dve.wait_ge(sem("ss_out"), r)
                    tt(bb[:, 0], f[0], b_[0], ALU.mult)
                    tt(t3, f[1], b_[1], ALU.mult)
                    tt(bb[:, 0], bb[:, 0], t3, ALU.subtract)
                    tt(bb[:, 1], f[0], b_[1], ALU.mult)
                    tt(t3, f[1], b_[0], ALU.mult)
                    dve.tensor_tensor(bb[:, 1], bb[:, 1], t3, ALU.add).then_inc(sem("ss_bb"), 1)
                    dve.wait_ge(sem("ss_bb"), r + 1)
                    sh = [P, 8, 5, 32]
                    L = [x[:, u8].unsqueeze(3).broadcast_to(sh) for x in (lc_r, lc_i)]
                    C = [x.unsqueeze(2).broadcast_to(sh) for x in c_]
                    t5 = cs_[:, :, :, :].rearrange("p a b c -> p (a b c)")[:, 0:1280].rearrange("p (a b c) -> p a b c", a=8, b=5)
                    cmul(dve, then, cp_[:, 0], cp_[:, 1], C, L, t5, minus=True, last=sem("ss_cpow"))
                    t4 = cs_[:, :, :, :].rearrange("p a b c -> p (a b c)")[:, 0:1024].rearrange("p (a b c) -> p a b c", a=8, b=4)
                    sh = [P, 8, 4, 32]
                    L = [x[:, u8].unsqueeze(3).broadcast_to(sh) for x in (lb_r, lb_i)]
                    B = [bb[:, z].unsqueeze(2).broadcast_to(sh) for z in range(2)]
                    cmul(dve, then, ap_[:, 0], ap_[:, 1], B, L, t4, minus=False, last=sem("ss_bpow"), twice=True)
                    ang = w(2)[:, u8].unsqueeze(2).broadcast_to([P, 8, NC])
                    tt(m4[:, :, :], ang, chk[:, :].unsqueeze(1).broadcast_to([P, 8, NC]), ALU.mult)
                    reduce_angle(w8[:, :, :], cs_[:, 0], m4[:, :, :])
                    dve.sem_inc(sem("ss_angle"), 1)
                    then(dve.tensor_copy(m4[:, :, :], w(7)[:, u8].unsqueeze(2).broadcast_to([P, 8, NC])))
                    then(dve.memset(m4[:, :, 0:1], 0.0))
                    then(dve.memset(tm_[:, :, :], 0.0))
                    dve.sem_inc(sem("ss_t_zero"), 1)
                    dve.wait_ge(sem("ss_t_forward"), r + 1)
                    lag = aux[0][:, 1, :].rearrange("p (u c) -> p u c", u=4)
                    for j in range(SC):
                        rows = slice(32 * j, 32 * j + 32)
                        m = dve.tensor_tensor(tm_[rows, :, 0:32 * (j + 1)], tm_[rows, :, 0:32 * (j + 1)],
                                              lag[rows, :, (3 - j) * 32:P], ALU.add)
                    m.then_inc(sem("ss_t"), 1)
                    dve.wait_ge(sem("ss_sines"), r + 1)
                    co, si = cs_[:, 0], cs_[:, 1]
                    tt(co, co, co, ALU.mult)
                    then(dve.tensor_scalar(co, co, -2.0, 1.0, ALU.mult, ALU.add))
                    dve.wait_ge(sem("ss_s"), r + 1)
                    sr = aux[0][:, :, :].rearrange("p a (b c) -> p (a b) c", c=NC)
                    si_ = aux[1][:, :, :].rearrange("p a (b c) -> p (a b) c", c=NC)
                    zr, zi, t = zz[:, 0], zz[:, 1], w8[:, :, :]
                    tt(zr, sr, co, ALU.mult)
                    tt(t, si_, si, ALU.mult)
                    tt(zr, zr, t, ALU.add)
                    tt(zi, si_, co, ALU.mult)
                    tt(t, sr, si, ALU.mult)
                    tt(zi, zi, t, ALU.subtract)
                    flat = lambda x: x.rearrange("p a b -> p (a b)")
                    for z in (zr, zi):
                        then(dve.tensor_tensor_scan(flat(z), flat(m4[:, :, :]), flat(z), 0.0, ALU.mult, ALU.add))
                    if r == 0:
                        then(dve.memset(st_[:, :, 0:4, 0:1], 0.0))
                        then(dve.memset(st_[:, :, 4:8, NC:NC + 1], 0.0))
                    for z, (a, b2, op) in enumerate(((zr, zi, ALU.subtract), (zi, zr, ALU.add))):
                        tt(t, a, co, ALU.mult)
                        tt(m4[:, :, :], b2, si, ALU.mult)
                        dve.tensor_tensor(st_[:, z, 0:4, 1:NC + 1], t[:, 0:4], m4[:, 0:4], op).then_inc(sem("ss_x"), 1)
                        dve.tensor_tensor(st_[:, z, 4:8, NC - 1::-1], t[:, 4:8], m4[:, 4:8], op).then_inc(sem("ss_x"), 1)
                        dve.wait_ge(sem("ss_x"), 4 * r + 2 * z + 2)
                for r in range(4):
                    dve.wait_ge(sem("ss_y"), 16 * (r + 1))
                    dve.scalar_tensor_tensor(yv[:, r], uin[:, r], col("dskip", None, r), yv[:, r], ALU.mult, ALU.add)\
                       .then_inc(sem("ss_skip"), 1)
                for r in range(4):
                    dve.wait_ge(sem("y_hi"), r + 1)
                    dve.tensor_tensor(zlo[:, r], yv[:, r], zhi[:, r].bitcast(F32), ALU.subtract).then_inc(sem("y_lo"), 1)
                ph = AT["glu2"]
                for i in range(4):
                    dve.wait_ge(evac[ph.slot(i)], ph.nth(i) + 1)
                    dve.wait_ge(sem("y_lo"), 4)
                    dve.tensor_tensor(yv[:, i], yv[:, i], uin[:, i], ALU.mult).then_inc(sem("z_done"), 1)
                for i in range(4):
                    dve.wait_ge(sem("z_hi"), i + 1)
                    dve.tensor_tensor(zlo[:, i], yv[:, i], zhi[:, i].bitcast(F32), ALU.subtract).then_inc(sem("z_lo"), 1)

            then(dve.memset(ones[:, :], 1.0))
            dve.sem_inc(sem("consts_set"), 1)
            then(dve.memset(zeros[:, :], 0.0))
            for name in ("mg_add", "m2_add", "ple_added", "ff_lo"):
                dve.sem_inc(sem(name), 1)
            dve.sem_inc(sem("consts_set"), 2)
            dve.wait_ge(sem("par_loaded"), 16)
            pp = lambda j: prep[:, j, :]
            for l in range(DEPTH):
                then(dve.tensor_copy(prep[:, 2, 8 * l:8 * l + 8], col("lam", l, 0, 8)))
            then(dve.tensor_scalar(pp(3), pp(2), -1.0, None, ALU.mult))
            dve.tensor_tensor(pp(0), pp(2), pp(3), ALU.max).then_inc(sem("lam_abs"), 1)
            dve.wait_ge(sem("lam_exp"), 1)
            then(dve.tensor_scalar(pp(4), pp(1), 2.0, None, ALU.add))
            then(dve.reciprocal(pp(4), pp(4)))
            then(dve.tensor_tensor(pp(4), pp(4), pp(1), ALU.mult))
            then(dve.tensor_tensor(pp(5), pp(4), pp(4), ALU.mult))
            then(dve.tensor_scalar(pp(6), pp(5), 1.0 / 17, 1.0 / 15, ALU.mult, ALU.add))
            for d in (13, 11, 9, 7, 5, 3, 1):
                then(dve.tensor_tensor(pp(6), pp(6), pp(5), ALU.mult))
                then(dve.tensor_scalar(pp(6), pp(6), 1.0 / d, None, ALU.add))
            then(dve.tensor_tensor(pp(6), pp(6), pp(4), ALU.mult))
            then(dve.tensor_scalar(pp(3), pp(3), 0.0, None, ALU.max))
            then(dve.scalar_tensor_tensor(pp(6), pp(6), 2.0, pp(3), ALU.mult, ALU.add))
            then(dve.tensor_scalar(spc[:, :, :].rearrange("p a b -> p (a b)"), pp(6), 8.0, None, ALU.mult))
            dve.tensor_scalar(nspc[:, :, :].rearrange("p a b -> p (a b)"), pp(6), -8.0, None, ALU.mult)\
               .then_inc(sem("spc_done"), 1)
            for l in range(DEPTH):
                norm(2 * l)
                proj(l)
                index(l)
                rnn(l)
                merge(l, "rnn", 0)
                conv(l)
                merge(l, "conv", 1)
                attention(l)
                merge(l, "att", 2)
                for n in range(KD):
                    dve.wait_ge(sem("br_hi"), (l * 4 + 3) * KD + n + 1)
                    dve.tensor_tensor(blo[:, n], merged[:, n], bhi[:, n].bitcast(F32), ALU.subtract).then_inc(sem("br_lo"), 1)
                add_to_h(AT[f"out{l}"], T1)
                ffn(2 * l + 1, f"up{l}", f"down{l}", T1, 1.0)
            ffn(4, "up2", "down2", SEQ, 0.5)
            norm(5)
            neighbours()
            ssm()
            ph = AT["mg2"]
            with dve.Fori(0, KD) as m:
                for z in range(2):
                    block_done(m * 4 + (ph.block(2 * z + 1) + 1))
                    dve.wait_ge(evac[ph.slot(0)], m * 2 + (ph.nth(0) + z + 1))
                    a, g = accv(ph.slot(1), S), halves(sg2[:, :], S)
                    mg = merged2[:, bass.ds(m, 1), :]
                    if z == 0:
                        dve.tensor_tensor(mg.rearrange("p a (b c) -> p (a b) c", b=2), a, g, ALU.mult).then_inc(evac[ph.slot(1)], 1)
                    else:
                        dve.wait_ge(sem("m2_add"), m + 1)
                        dve.tensor_tensor(halves(mt2[:, :], S), a, g, ALU.mult).then_inc(evac[ph.slot(1)], 1)
                        dve.wait_ge(evac[ph.slot(1)], m * 2 + (ph.nth(1) + 2))
                        dve.tensor_tensor(mg, mg, mt2[:, :].unsqueeze(1), ALU.add).then_inc(sem("m2_add"), 1)
            for n in range(KD):
                dve.wait_ge(sem("m2_hi"), n + 1)
                dve.tensor_tensor(mlo[:, n], merged2[:, n], mhi[:, n].bitcast(F32), ALU.subtract).then_inc(sem("m2_lo"), 1)
            add_to_h(AT["out2"], SEQ)
            ffn(6, "up3", "down3", SEQ, 0.5)
            norm(7)
            dve.wait_ge(sem("p_hi"), 1)
            for n in range(2):
                dve.tensor_tensor(plo[:, n], pin[:, n], phi[:, n].bitcast(F32), ALU.subtract).then_inc(sem("p_lo"), 1)
            ph = AT["ple2"]
            with dve.Fori(0, KD) as m:
                block_done(m * 2 + (ph.block(1) + 1))
                dve.wait_ge(evac[ph.slot(0)], m + (ph.nth(0) + 1))
                dve.wait_ge(sem("ple_added"), m + 1)
                dve.tensor_tensor(halves(pmt[:, :], S), accv(ph.slot(1), S), halves(psg[:, :], S), ALU.mult)\
                   .then_inc(evac[ph.slot(1)], 1)
                dve.wait_ge(evac[ph.slot(1)], m + (ph.nth(1) + 1))
                hv = h[:, bass.ds(m, 1), T1 - S:T1]
                dve.tensor_tensor(hv, hv, pmt[:, :].unsqueeze(1), ALU.add).then_inc(sem("ple_added"), 1)
            dve.wait_ge(sem("ple_added"), KD + 1)
            norm(8)


GW = 64
FFI = {"up0": 0, "up1": 1, "up2": 2, "up3": 3}


def cmul(dve, then, out_r, out_i, a, b, t, minus, last, twice=False):
    each = lambda o, x, y, op: then(dve.tensor_tensor(o, x, y, op))
    each(out_r, a[0], b[0], ALU.mult)
    each(t, a[1], b[1], ALU.mult)
    then(dve.tensor_tensor(out_r, out_r, t, ALU.subtract))
    each(out_i, a[0], b[1], ALU.mult)
    each(t, a[1], b[0], ALU.mult)
    then(dve.tensor_tensor(out_i, out_i, t, ALU.add))
    if minus:
        then(dve.tensor_scalar(out_i, out_i, -1.0, None, ALU.mult))
    dve.sem_inc(last, 4 if twice else 2)


def blocks_of(w):
    K, M = w.shape
    nk, per = K // P, -(-K // (P * BLK))
    t = w.reshape(nk, P, M // P, P).transpose(2, 1, 0, 3)
    out = np.zeros((M // P, P, per * BLK, P), w.dtype)
    out[:, :, :nk] = t
    return out.reshape(M // P, P, per, BLK * P).transpose(0, 2, 1, 3).reshape(M // P * per, P, BLK * P)


def pairs(*ws):
    b = [blocks_of(w) for w in ws]
    return np.stack(b, 1).reshape(-1, P, BLK * P)


def tiles(x, n):
    return x.reshape(n, P).T


def rope_consts(n, dim):
    inv = (np.float32(10000.0) ** (-np.arange(0, dim, 2, dtype=np.float32) / np.float32(dim))).astype(np.float32)
    ang = (np.arange(n, dtype=np.float32)[:, None] * inv[None, :]).astype(np.float32)
    c, s = np.cos(ang).T.astype(np.float32), np.sin(ang).T.astype(np.float32)
    reps = P // dim
    return np.concatenate([c, c] * reps), np.concatenate([-s, s] * reps)


def kernel(**inputs):
    import concourse.bacc as _bacc
    from concourse.bass_utils import run_bass_kernel_spmd as _run

    I = {n: np.asarray(a) for n, a in inputs.items()}
    ws = []
    for l in range(DEPTH):
        w = I["w_in"][l]
        edge = np.cumsum([0, 1024, 256, 256, 512, 64, 8, 1024, 1024, 2048, 3072])
        q, k, v, qi, ki, wi, xr, yg, cv, gt = (w[:, a:b] for a, b in zip(edge[:-1], edge[1:]))
        last = np.zeros((D, P), w.dtype)
        last[:, 0:64], last[:, 64:72] = ki, wi
        ws += [blocks_of(q), blocks_of(k), blocks_of(v), blocks_of(qi), blocks_of(last), pairs(xr, yg),
               pairs(gt[:, D:2 * D], I["w_o_rnn"][l]), pairs(cv[:, 0:D], cv[:, D:]), pairs(gt[:, 2 * D:], I["w_o_conv"][l]),
               pairs(gt[:, 0:D], I["w_o_attn"][l]), blocks_of(I["w_out"][l]),
               pairs(I["w_ffn_gate"][l], I["w_ffn_up"][l]), blocks_of(I["w_ffn_down"][l])]
    w = I["w_in_2"][0]
    ws += [pairs(I["ffn1_w_gate_2"][0], I["ffn1_w_up_2"][0]), blocks_of(I["ffn1_w_down_2"][0]), blocks_of(w[:, 0:1536]),
           blocks_of(w[:, 1536:2048]), blocks_of(I["ssm_glu_w_2"][0]),
           pairs(w[:, 2048:3072], I["w_attn_out_2"][0], w[:, 3072:4096], I["w_ssm_out_2"][0]), blocks_of(I["w_out_2"][0]),
           pairs(I["ffn2_w_gate_2"][0], I["ffn2_w_up_2"][0]), blocks_of(I["ffn2_w_down_2"][0]),
           pairs(I["ple_w_gate_2"][0], I["ple_w_proj_2"][0])]
    wpack = np.concatenate(ws)
    assert wpack.shape[0] == plan()[1]

    cols = []
    for l in range(DEPTH):
        cols += [tiles(I["mix_norm_g"][l], 8), tiles(I["q_norm_g"][l], 1), tiles(I["k_norm_g"][l], 1),
                 *[tiles(I["rnn_conv_w"][l, t], 8) for t in range(CONV)], tiles(I["rnn_conv_b"][l], 8),
                 tiles(I["rnn_ba"][l], 8), tiles(I["rnn_bx"][l], 8), tiles(I["rnn_lambda"][l], 8),
                 *[tiles(I["conv_dw_w"][l, t], 8) for t in range(DW)], tiles(I["conv_dw_b"][l], 8),
                 tiles(I["conv_ln_g"][l], 8), tiles(I["conv_ln_b"][l], 8), tiles(I["ffn_norm_g"][l], 8)]
    cols += [tiles(I["ffn1_norm_2"][0], 8), tiles(I["mix_norm_2"][0], 8), tiles(I["ffn2_norm_2"][0], 8),
             tiles(I["ple_norm_2"][0], 8), tiles(I["final_norm_2"], 8), tiles(I["ssm_d_2"][0], 4), tiles(I["ssm_glu_b_2"][0], 4)]
    par = np.ascontiguousarray(np.concatenate(cols, 1))
    assert par.shape[1] == columns()[1]

    hT = np.concatenate([I["meta"], I["x"][0]]).T.reshape(KD, P, T1).transpose(1, 0, 2)
    rope = np.stack(rope_consts(T1, HD) + rope_consts(T1, IXD)).astype(np.float32)
    gate = np.stack([I["rnn_wa"], I["rnn_wx"]], 1).transpose(0, 1, 3, 2, 4).reshape(DEPTH, 2, P, 8 * P)

    rpb = I["na_rpb_2"][0]
    padded = np.zeros((HEADS, 16, 127), rpb.dtype)
    padded[:, 1:16, 48:79] = rpb
    qc, kc = np.arange(GW)[:, None], np.arange(GW)[None, :]
    natab = np.zeros((2, HEADS, GW, NAR, GW), rpb.dtype)
    for half in range(2):
        for e in range(NAR):
            natab[half, :, :, e] = padded[:, e + 2 - half][:, kc - qc + 63]
    start = np.clip(np.arange(GW) - NAW // 2, 0, GW - NAW)[:, None]
    inside = (kc >= start) & (kc < start + NAW)
    namask = np.tile(np.where(inside, 0.0, NEG).astype(np.float32), (2, 1))

    def states(a):
        a = a.reshape(2, 4, 4, 2, 64, *a.shape[3:])
        a = np.moveaxis(a, [3, 4, 1, 0, 2], [0, 1, 2, 3, 4])
        return a.reshape(P, 32, *a.shape[5:])

    ssm = np.zeros((7, P, 1024), np.float32)
    ssm[0, :, 0:32] = states(np.repeat(I["ssm_log_dt_2"][0][:, :, None], 64, 2))
    ssm[1, :, 0:32] = states(I["ssm_lam_re_2"][0])
    ssm[2, :, 0:32] = states(I["ssm_lam_im_2"][0])
    for n, a in enumerate((I["ssm_b_re_2"][0], I["ssm_b_im_2"][0], I["ssm_c_re_2"][0].transpose(0, 1, 3, 2),
                           I["ssm_c_im_2"][0].transpose(0, 1, 3, 2))):
        a, full = states(a), ssm[3 + n].reshape(P, 32, 32)
        full[0:64, :, 0:16], full[64:, :, 16:] = a[0:64], a[64:]
    chunks = np.tile(np.arange(NC, dtype=np.float32), (P, 1))
    pT = np.ascontiguousarray(I["p_2"][0, 0].T.reshape(2, P, SEQ))

    arrays = {"w": wpack, "par": par, "h": np.ascontiguousarray(hT), "rope": rope, "gate": np.ascontiguousarray(gate),
              "natab": natab, "namask": namask, "ssm": ssm, "chunk": chunks, "p": pT, "ident": np.eye(P, dtype=np.float32)}
    nc = _bacc.Bacc("TRN2", target_bir_lowering=False, num_devices=1)
    args = [nc.dram_tensor(f"in_{n}", a.shape, mybir.dt.from_np(a.dtype), kind="ExternalInput").ap() for n, a in arrays.items()]
    out = nc.dram_tensor("out_0", (KD, P, SEQ), F32, kind="ExternalOutput").ap()
    build(nc, *args, out)
    r = _run(nc, [{f"in_{n}": a for n, a in arrays.items()}], core_ids=[0])
    y = r.results[0]["out_0"]
    return np.ascontiguousarray(y.reshape(D, SEQ).T)[None]
```

```python
from contextlib import ExitStack

import numpy as np

import concourse.bass as bass
from concourse import mybir

F32 = mybir.dt.float32
F32R = mybir.dt.float32r
ALU = mybir.AluOpType
ACT = mybir.ActivationFunctionType
AX = mybir.AxisListType

P = 128
D = 1024
KD = D // P
DEPTH = 2
META = 16
SEQ = 512
T1 = META + SEQ
CHUNK = 64
TOPK = 128
HEADS = 8
KV = 2
HD = 128
IXH = 8
IXD = 64
FF = 2816
KF = FF // P
CONV = 4
DW = 31
NQT = SEQ // P
EPS = 1e-6
NEG = -1.0e30
BARRED = -3.0e38
CHOSEN = -3.4e38
BLK = 8
RAW = 4
TWO_PI = 2.0 * np.pi
MAGIC = 12582912.0
PI_SAFE = 3.1415925
NAW = 16
NAR = 14
HD2 = 64
UNITS = 16
ROUND = 4
SC = 4
NC = SEQ // SC


def two_pi_parts():
    c1 = np.float32(6.28125)
    r = TWO_PI - float(c1)
    c2 = np.float32(np.round(r * 2.0 ** 21) / 2.0 ** 21)
    return float(c1), float(c2), float(np.float32(r - float(c2)))


class Phase:
    def __init__(self, block, used, tiles, per, only):
        self.b0, self.used, self.tiles, self.per, self.only = block, tuple(used), tiles, per, only

    def block(self, i):
        return self.b0 + i * self.per

    def slot(self, i):
        return i % 2 if self.only is None else self.only

    def nth(self, i):
        return self.used[self.slot(i)] + (i // 2 if self.only is None else i)


PHASES = []
for _l in range(DEPTH):
    PHASES += [(f"qk{_l}", 10, 1), (f"v{_l}", 2, 1), (f"qi{_l}", 5, 1), (f"conv{_l}", 16, 1), (f"rnn{_l}", 16, 1),
               (f"mg_rnn{_l}", 16, 1, 0), (f"att{_l}", 8, 0, 1), (f"mg_att{_l}", 16, 1), (f"mg_conv{_l}", 16, 1),
               (f"out{_l}", 8, 1), (f"up{_l}", 2 * KF, 1), (f"down{_l}", 8, 3)]
PHASES += [("up2", 2 * KF, 1), ("down2", 8, 3), ("qkv2", 12, 1), ("sin2", 4, 1), ("att2", 4, 0), ("glu2", 4, 1),
           ("mg2", 32, 1), ("out2", 8, 1), ("up3", 2 * KF, 1), ("down3", 8, 3), ("ple2", 16, 1)]


def plan():
    at, block, used = {}, 0, [0, 0]
    for name, tiles, per, *only in PHASES:
        ph = at[name] = Phase(block, used, tiles, per, only[0] if only else None)
        block += tiles * per
        for i in range(tiles):
            used[ph.slot(i)] += 1
    return at, block


LAYER_COLS = [("mix_g", 8), ("q_g", 1), ("k_g", 1), ("cw", CONV * 8), ("cb", 8), ("ba", 8), ("bx", 8), ("lam", 8),
              ("dw", DW * 8), ("db", 8), ("ln_g", 8), ("ln_b", 8), ("ffn_g", 8)]
TAIL_COLS = [("ffn1_g", 8), ("mix2_g", 8), ("ffn2_g", 8), ("ple_g", 8), ("final_g", 8), ("dskip", 4), ("glu_b", 4)]


def columns():
    at, n = {}, 0
    for layer in range(DEPTH):
        for name, w in LAYER_COLS:
            at[(name, layer)] = n
            n += w
    for name, w in TAIL_COLS:
        at[name] = n
        n += w
    return at, n


def build(nc, A_w, A_par, A_h, A_rope, A_gate, A_natab, A_namask, A_ssm, A_chunk, A_p, A_ident, A_out):
    AT, NBLK = plan()
    COL, NPAR = columns()
    ROW = T1 * 4

    with ExitStack() as ctx:
        sems = {}

        def sem(name):
            if name not in sems:
                sems[name] = ctx.enter_context(nc.semaphore(name))
            return sems[name]

        BASE = 16512
        place = [BASE]

        def fixed(name, shape, dt=F32):
            t = nc.alloc_sbuf_tensor_at(name, shape, dt, offset=place[0])
            n = 4
            for s in shape[1:]:
                n *= s
            place[0] += (n + 31) // 32 * 32
            return t

        ident = fixed("ident", [P, P])
        ones = fixed("ones", [P, P])
        par = fixed("par", [P, NPAR])
        spc = fixed("spc", [P, DEPTH, 8])
        nspc = fixed("nspc", [P, DEPTH, 8])
        hba = fixed("hba", [P, DEPTH, 2, 8])
        h = fixed("h", [P, KD, T1])
        nhi = fixed("nhi", [P, KD, T1], F32R)
        nlo = fixed("nlo", [P, KD, T1], F32R)
        raw = fixed("raw", [P, RAW, BLK * P])
        whi = fixed("whi", [P, 2, BLK * P], F32R)
        wlo = fixed("wlo", [P, 2, BLK * P], F32R)
        zeros = fixed("zeros", [P, 128])
        ARENA = place[0]
        END = 229344

        def at(name, shape, off, dt=F32):
            n = 4
            for s in shape[1:]:
                n *= s
            assert ARENA + off + n <= END, (name, ARENA + off + n - END)
            return nc.alloc_sbuf_tensor_at(name, shape, dt, offset=ARENA + off), off + (n + 31) // 32 * 32

        o = 0
        q, o = at("q", [P, HEADS, T1], o)
        k, o = at("k", [P, KV, T1], o)
        v, o = at("v", [P, 5, KV * HD], o)
        mask, o = at("mask", [P, NQT, T1], o)
        wi, o = at("wi", [P, NQT, IXH], o)
        merged, end_merged = at("merged", [P, KD, T1], o)
        vT, o1 = at("vT", [P, KV, T1], o)
        rnn_w, o1 = at("rnn_w", [P, 2, 8, P], o1)
        assert o1 <= end_merged
        bhi, o = at("bhi", [P, KD, T1], end_merged, F32R)
        blo, o = at("blo", [P, KD, T1], o, F32R)
        area1 = o
        qi, o = at("qi", [P, 4, T1], o)
        ki, o = at("ki", [P, T1], o)
        rope, area2 = at("rope", [P, 4, T1], o)
        cu, _ = at("cu", [P, KD, T1], area1)
        o = area2
        rx, o = at("rx", [P, T1 + CONV - 1], o)
        ru, o = at("ru", [P, T1], o)
        rr, o = at("rr", [P, T1], o)
        ri, o = at("ri", [P, T1], o)
        rt, o = at("rt", [P, T1], o)
        ra, o = at("ra", [P, T1], o)
        rb, o = at("rb", [P, T1], o)
        rh, o = at("rh", [P, T1], o)
        rg, o = at("rg", [P, T1], o)
        o = area2
        tsq, o = at("tsq", [P, 2, T1], o)
        tqg, o = at("tqg", [P, 2, T1], o)
        tsw, o = at("tsw", [P, 2, T1], o)
        tstd, o = at("tstd", [P, T1], o)
        trs, o = at("trs", [P, T1], o)
        wbuf, o = at("wbuf", [32, T1], o)
        top8, o = at("top8", [P, 8], o)
        csg, _ = at("csg", [P, T1], area2 + 6 * ROW)
        o = area2
        sm, o = at("sm", [P, 3, T1], o)
        pts, o = at("pts", [P, 5, P], o)
        cx, o = at("cx", [P, T1 + DW - 1], o)
        sg, o = at("sg", [P, T1], o)
        mt, o = at("mt", [P, T1], o)
        csq, o = at("csq", [P, 2, T1], o)
        mx, o = at("mx", [P, 4], o)
        nmx, o = at("nmx", [P, 4], o)
        rsum, o = at("rsum", [P, 4], o)
        rrs, o = at("rrs", [P, 4], o)
        cstat, _ = at("cstat", [P, 3, T1], area2)
        prep, o = at("prep", [P, 8, DEPTH * 8], 0)

        o = area2
        fsq, o = at("fsq", [P, 2, T1], o)
        facc, o = at("facc", [P, T1], o)
        ftmp, o = at("ftmp", [P, 2, T1], o)
        fstd, o = at("fstd", [P, T1], o)
        frs, o = at("frs", [P, T1], o)
        o = 0
        ahi, o = at("ahi", [P, KF, T1], o, F32R)
        alo, o = at("alo", [P, KF, T1], o, F32R)
        fsl, o = at("fsl", [P, T1], o)
        fpr, o = at("fpr", [P, T1], o)

        S = SEQ
        o = 0
        attn_hi, o = at("attn_hi", [P, 4, S], o, F32R)
        attn_lo, o = at("attn_lo", [P, 4, S], o, F32R)
        zhi, o = at("zhi", [P, 4, S], o, F32R)
        zlo, o = at("zlo", [P, 4, S], o, F32R)
        uin, o = at("uin", [P, 4, S], o)
        yv, o = at("yv", [P, 4, S], o)
        base2 = o
        q2, o = at("q2", [P, 4, S], o)
        k2, o = at("k2", [P, 4, S], o)
        v2, o = at("v2", [P, 4, S], o)
        vT2, _ = at("vT2", [P, 4, S], o)
        natab, o = at("natab", [P, HEADS, NAR, GW], o)
        namask, o = at("namask", [P, GW], o)
        sm2, _ = at("sm2", [P, 2, S], 2 * 4 * S * 4)
        pts2, _ = at("pts2", [P, 4, P], 2 * 4 * S * 4 + 2 * S * 4)
        ot2, _ = at("ot2", [P, S], 2 * 4 * S * 4 + 3 * S * 4)
        sc2, _ = at("sc2", [P, 4, 2], 2 * 4 * S * 4 + 4 * S * 4)
        o = base2
        smp, o = at("smp", [P, 3, 32], o)
        sbc, o = at("sbc", [P, 4, 32, 32], o)
        spw, o = at("spw", [P, 20, 32], o)
        lc_r, o = at("lc_r", [P, 32, 5], o)
        lc_i, o = at("lc_i", [P, 32, 5], o)
        lb_r, o = at("lb_r", [P, 32, 4], o)
        lb_i, o = at("lb_i", [P, 32, 4], o)
        chk, o = at("chk", [P, NC], o)
        place_of_reps = o
        reps, o = at("reps", [P, 2, 8, 4, 32], o)
        zz, _ = at("zz", [P, 2, 8, NC], place_of_reps)
        ap_, o = at("ap_", [P, 2, 8, 4, 32], o)
        cp_, o = at("cp_", [P, 2, 8, 5, 32], o)
        w1s, o = at("w1s", [P, 8, 2, P], o)
        tm_, o = at("tm_", [P, 4, P], o)
        us, o = at("us", [P, 2, 4, NC], o)
        cs_, o = at("cs_", [P, 2, 8, NC], o)
        m4, o = at("m4", [P, 8, NC], o)
        o = 2 * 4 * S * 4
        st_, o = at("st_", [P, 2, 8, NC + 1], o)
        w8, o = at("w8", [P, 8, NC], o)
        bb, o = at("bb", [P, 2, 8, 32], o)
        o = base2
        merged2, o = at("merged2", [P, KD, S], o)
        mhi, o = at("mhi", [P, KD, S], o, F32R)
        mlo, o = at("mlo", [P, KD, S], o, F32R)
        sg2, o = at("sg2", [P, S], o)
        mt2, o = at("mt2", [P, S], o)
        o = 0
        pin, o = at("pin", [P, 2, S], o)
        phi, o = at("phi", [P, 2, S], o, F32R)
        plo, o = at("plo", [P, 2, S], o, F32R)
        psg, o = at("psg", [P, S], o)
        pmt, o = at("pmt", [P, S], o)
        o = max(o, 6 * ROW)
        yout, o = at("yout", [P, KD, S], o)

        acc = [ctx.enter_context(nc.psum_tensor(f"acc{i}", [P, 2, 512], F32)) for i in range(2)]
        aux = [ctx.enter_context(nc.psum_tensor(f"aux{i}", [P, 2, 512], F32)) for i in range(2)]

        evac = [sem("acc0_evacuated"), sem("acc1_evacuated")]
        pe_block = sem("pe_block_done")

        def halves(ap2, T):
            return ap2.rearrange("p (a b) -> p a b", a=2)

        def accv(s, T):
            return acc[s][:, :, 0:T // 2]

        def col(name, layer=None, j=0, n=1):
            c = COL[(name, layer)] if layer is not None else COL[name]
            return par[:, c + j:c + j + n]

        def h_ready(eng, phase):
            n = phase.tiles
            for i in (n - 2, n - 1):
                eng.wait_ge(evac[phase.slot(i)], phase.nth(i) + 1)

        def hview(T):
            return h[:, :, T1 - T:T1]

        NORMS = ["mix0", "ffn0", "mix1", "ffn1", "ffn2_1", "mix2", "ffn2_2", "ple2", "final"]
        NORM_G = [("mix_g", 0), ("ffn_g", 0), ("mix_g", 1), ("ffn_g", 1), ("ffn1_g", None), ("mix2_g", None),
                  ("ffn2_g", None), ("ple_g", None), ("final_g", None)]
        NORM_AFTER = [None, "out0", "down0", "out1", "down1", "down2", "out2", "down3", "ple2"]
        NORM_T = [T1] * 4 + [SEQ] * 5

        block = ctx.enter_context(nc.Block())

        @block.sync
        def _(sp):
            for b in range(RAW):
                sp.dma_start(raw[:, b], A_w[b]).then_inc(sem(f"w_loaded{b}"), 16)
            groups = NBLK // RAW
            with sp.Fori(1, groups) as g:
                for r in range(RAW):
                    sp.wait_ge(sem("w_split"), g * RAW + (r - RAW + 1))
                    sp.dma_start(raw[:, r], A_w[bass.ds(g * RAW + r, 1)].rearrange("a p n -> (a p) n"))\
                      .then_inc(sem(f"w_loaded{r}"), 16)
            for b in range(groups * RAW, NBLK):
                sp.wait_ge(sem("w_split"), b - RAW + 1)
                sp.dma_start(raw[:, b % RAW], A_w[b]).then_inc(sem(f"w_loaded{b % RAW}"), 16)
            for j in range(KD):
                sp.wait_ge(sem("final_out"), j + 1)
                sp.dma_start(A_out[j], yout[:, j]).then_inc(sem("stored"), 16)
            sp.wait_ge(sem("stored"), 16 * KD)

        @block.gpsimd
        def _(pool):
            pool.wait_ge(sem("consts_set"), 3)
            zb = zeros[:, :].unsqueeze(1).broadcast_to([P, BLK, P])

            def split(b, r, n):
                s = r % 2
                pool.wait_ge(sem(f"w_loaded{r}"), n)
                w = raw[:, r].rearrange("p (a c) -> p a c", a=BLK)
                hi = whi[:, s].rearrange("p (a c) -> p a c", a=BLK)
                lo = wlo[:, s].rearrange("p (a c) -> p a c", a=BLK)
                pool.tensor_tensor(hi, w, zb, ALU.add).then_inc(sem("w_hi"), 1)
                pool.wait_ge(sem("w_hi"), b + 1)
                pool.tensor_tensor(lo, w, hi.bitcast(F32), ALU.subtract).then_inc(sem("w_split"), 1)

            for b in range(RAW):
                if b >= 2:
                    pool.wait_ge(pe_block, b - 1)
                split(b, b, 16)
            groups = NBLK // RAW
            with pool.Fori(1, groups) as g:
                for r in range(RAW):
                    pool.wait_ge(pe_block, g * RAW + (r - 1))
                    split(g * RAW + r, r, g * 16 + 16)
            for b in range(groups * RAW, NBLK):
                pool.wait_ge(pe_block, b - 1)
                split(b, b % RAW, 16 * (b // RAW + 1))

        @block.tensor
        def _(pe):
            def part(s, slot, j, rhs, T, a, z):
                return products(s, slot, j, 1, rhs, T, a, z, w0=j)

            def products(s, slot, j0, nk, rhs, T, first, last, w0=0):
                TH = T // 2
                for j in range(nk):
                    hi = whi[:, slot, (w0 + j) * P:(w0 + j + 1) * P]
                    lo = wlo[:, slot, (w0 + j) * P:(w0 + j + 1) * P]
                    xh, xl = rhs(j0 + j)
                    a, z = first and j == 0, last and j == nk - 1
                    for f in range(2):
                        pe.matmul(acc[s][:, f, 0:TH], hi, xh[:, f * TH:(f + 1) * TH], start=a, stop=False)
                        pe.matmul(acc[s][:, f, 0:TH], hi, xl[:, f * TH:(f + 1) * TH], start=False, stop=False)
                    for f in range(2):
                        m = pe.matmul(acc[s][:, f, 0:TH], lo, xh[:, f * TH:(f + 1) * TH], start=False, stop=z)
                return m

            def tile(ph, i, rhs, T, nk=KD, m=0, step=0, fresh=None):
                s = ph.slot(i)
                n = ph.nth(i) + m * (step // 2)
                if ph.nth(i):
                    pe.wait_ge(evac[s], n)
                for c in range(ph.per):
                    b = ph.block(i) + c
                    pe.wait_ge(sem("w_split"), b + 1 + m * (step * ph.per))
                    kk = min(BLK, nk - c * BLK)
                    if fresh is None:
                        products(s, b % 2, c * BLK, kk, rhs, T, c == 0, c == ph.per - 1).then_inc(pe_block, 1)
                        continue
                    for j in range(KD):
                        pe.wait_ge(sem("norm_lo"), fresh * KD + j + 1)
                        p = part(s, b % 2, j, rhs, T, j == 0, j == KD - 1)
                    p.then_inc(pe_block, 1)

            def R(hi, lo, T):
                return lambda j: (hi[:, j, 0:T], lo[:, j, 0:T])

            def sumsq(i):
                T = NORM_T[i]
                pe.wait_ge(sem("norm_added"), (i + 1) * KD)
                for f in range(2):
                    m = pe.matmul(aux[0][:, f, 0:T // 2], ones[:, :],
                                  facc[:, T1 - T + f * (T // 2):T1 - T + (f + 1) * (T // 2)], start=True, stop=True)
                m.then_inc(sem("norm_summed"), 1)

            def normed(i):
                pe.wait_ge(sem("norm_lo"), (i + 1) * KD)

            def ffn(i, up, down, T):
                sumsq(i)
                for j in range(2):
                    tile(AT[up], j, R(nhi, nlo, T), T, fresh=i if j == 0 else None)
                with pe.Fori(1, KF) as m:
                    for j in range(2):
                        tile(AT[up], j, R(nhi, nlo, T), T, m=m, step=2)
                pe.wait_ge(sem("ff_lo"), (FFI[up] + 1) * KF + 1)
                with pe.Fori(0, KD // 2) as m:
                    for j in range(2):
                        tile(AT[down], j, R(ahi, alo, T), T, nk=KF, m=m, step=2)

            def proj(l):
                qk, rhs = AT[f"qk{l}"], R(nhi, nlo, T1)

                def qk_sum(e):
                    it = l * 10 + e
                    pe.wait_ge(sem("qk_square"), it + 1)
                    if it:
                        pe.wait_ge(sem("qk_std"), it)
                    for f in range(2):
                        m = pe.matmul(aux[0][:, f, 0:T1 // 2], ones[:, :],
                                      tsq[:, e % 2, f * (T1 // 2):(f + 1) * (T1 // 2)], start=True, stop=True)
                    m.then_inc(sem("qk_sum"), 1)

                for e in range(10):
                    tile(qk, e, rhs, T1, fresh=2 * l if e == 0 else None)
                    if e:
                        qk_sum(e - 1)
                tile(AT[f"v{l}"], 0, rhs, T1)
                qk_sum(9)
                tile(AT[f"v{l}"], 1, rhs, T1)
                for e in range(4):
                    tile(AT[f"qi{l}"], e, rhs, T1)
                pe.wait_ge(evac[AT[f"v{l}"].slot(1)], AT[f"v{l}"].nth(1) + 1)
                pe.wait_ge(sem("qk_std"), (l + 1) * 10)
                for e in range(KV):
                    for c in range(4):
                        pe.transpose(aux[1][:, e, c * P:(c + 1) * P], vT[:, e, c * P:(c + 1) * P], ident[:, :])
                for e in range(KV):
                    m = pe.transpose(aux[0][0:16, e, 0:P], vT[:, e, 4 * P:T1], ident[:, :])
                m.then_inc(sem("v_turned"), 1)
                tile(AT[f"qi{l}"], 4, rhs, T1)
                pe.wait_ge(sem("wi_rows"), l + 1)
                pe.wait_ge(sem("v_copied"), 4 * (l + 1))
                for i in range(NQT):
                    m = pe.transpose(aux[0][:, 1, i * 32:(i + 1) * 32], wbuf[:, META + i * P:META + (i + 1) * P],
                                     ident[0:32, 0:32])
                m.then_inc(sem("wi_turned"), 1)

            def index(l):
                pe.wait_ge(sem("qi_done"), 5 * (l + 1))
                pe.wait_ge(sem("wi_copied"), l + 1)
                for i in range(NQT):
                    W = META + P * (i + 1)
                    for hh in range(IXH):
                        it = (l * NQT + i) * IXH + hh
                        if it >= 2:
                            pe.wait_ge(sem("ix_relu"), it - 1)
                        rows = slice(64 * (hh % 2), 64 * (hh % 2) + 64)
                        lhs = qi[rows, hh // 2, META + i * P:META + (i + 1) * P]
                        m = pe.matmul(aux[hh % 2][:, 0, 0:min(W, 512)], lhs, ki[rows, 0:min(W, 512)], start=True, stop=True)
                        if W > 512:
                            m = pe.matmul(aux[hh % 2][:, 1, 0:W - 512], lhs, ki[rows, 512:W], start=True, stop=True)
                        m.then_inc(sem("ix_logit"), 1)

            def rnn(l):
                ph, rhs = AT[f"rnn{l}"], R(nhi, nlo, T1)

                def gates(n):
                    it = l * 8 + n
                    pe.wait_ge(sem("rnn_conv"), 4 * (it + 1))
                    if n == 0:
                        pe.wait_ge(sem("rnn_w_loaded"), 16 * (l + 1))
                        pe.wait_ge(sem("ix_relu"), (l + 1) * NQT * IXH)
                    if it:
                        pe.wait_ge(sem("rnn_i"), it)
                    for g in range(2):
                        for f in range(2):
                            m = pe.matmul(aux[g][:, f, 0:T1 // 2], rnn_w[:, g, n],
                                          ru[:, f * (T1 // 2):(f + 1) * (T1 // 2)], start=True, stop=True)
                    m.then_inc(sem("rnn_gates"), 1)

                for n in range(8):
                    tile(ph, 2 * n, rhs, T1)
                    if n:
                        gates(n - 1)
                    tile(ph, 2 * n + 1, rhs, T1)
                gates(7)

            def ln_mean(l):
                for n in range(KD):
                    pe.wait_ge(sem("cv_conv"), (l * 8 + n + 1) * DW)
                    if n == 0:
                        pe.wait_ge(sem("at_scored"), (l + 1) * ITEMS)
                    for f in range(2):
                        m = pe.matmul(aux[0][:, f, 0:T1 // 2], ones[:, :], cu[:, n, f * (T1 // 2):(f + 1) * (T1 // 2)],
                                      start=n == 0, stop=n == KD - 1)
                m.then_inc(sem("cv_mean"), 1)

            def ln_square(l):
                for n in range(KD):
                    pe.wait_ge(sem("cv_square"), l * 8 + n + 1)
                    for f in range(2):
                        m = pe.matmul(aux[1][:, f, 0:T1 // 2], ones[:, :], csq[:, n % 2, f * (T1 // 2):(f + 1) * (T1 // 2)],
                                      start=n == 0, stop=n == KD - 1)
                    m.then_inc(sem("cv_summed"), 1)

            def mix(l):
                ph, mg = AT[f"att{l}"], AT[f"mg_rnn{l}"]
                items = [(hh, i) for hh in range(HEADS) for i in range(NQT + 1)]
                n0 = l * len(items)

                def shape(i):
                    return (P, META + i * P, META + (i + 1) * P) if i < NQT else (META, 0, META)

                def scores(j):
                    hh, i = items[j]
                    r, c, W = shape(i)
                    if n0 + j:
                        pe.wait_ge(sem("at_scored"), n0 + j)
                    lhs = q[:, hh, c:c + r]
                    m = pe.matmul(aux[0][0:r, 0, 0:min(W, 512)], lhs, k[:, hh // 4, 0:min(W, 512)], start=True, stop=True)
                    if W > 512:
                        m = pe.matmul(aux[0][0:r, 1, 0:W - 512], lhs, k[:, hh // 4, 512:W], start=True, stop=True)
                    m.then_inc(sem("at_s"), 1)

                def pieces(W):
                    return [(c, min(P, W - c * P)) for c in range(-(-W // P))]

                def turn(j):
                    hh, i = items[j]
                    r, _, W = shape(i)
                    pe.wait_ge(sem("at_p"), n0 + j + 1)
                    if n0 + j:
                        pe.wait_ge(sem("at_pt"), n0 + j)
                    for c, w in pieces(W):
                        m = pe.transpose(aux[1][0:w, c // 4, (c % 4) * P:(c % 4) * P + r], sm[0:r, j % 3, c * P:c * P + w],
                                         ident[0:r, 0:r])
                    m.then_inc(sem("at_turned"), 1)

                def values(j):
                    hh, i = items[j]
                    r, _, W = shape(i)
                    s = ph.slot(hh)
                    if i == 0:
                        pe.wait_ge(evac[s], ph.nth(hh))
                    pe.wait_ge(sem("at_pt"), n0 + j + 1)
                    ps = pieces(W)
                    for c, w in ps:
                        out = acc[s][:, 0, i * P:(i + 1) * P] if i < NQT else acc[s][:, 1, 0:META]
                        m = pe.matmul(out, v[0:w, c, (hh // 4) * P:(hh // 4 + 1) * P], pts[0:w, c, 0:r],
                                      start=c == 0, stop=c == len(ps) - 1)
                    m.then_inc(sem("at_pv"), 1)

                def merge_part(j):
                    i, a, z = MERGE_PARTS[j % 5]
                    t = 2 * (j // 5) + i
                    s, b = mg.slot(t), mg.block(t)
                    if a == 0:
                        pe.wait_ge(evac[s], mg.nth(t))
                        pe.wait_ge(sem("w_split"), b + 1)
                    rhs = R(bhi, blo, T1) if i else R(nhi, nlo, T1)
                    for c in range(a, z):
                        p = part(s, b % 2, c, rhs, T1, c == 0, c == KD - 1)
                    if z == KD:
                        p.then_inc(pe_block, 1)

                pe.wait_ge(sem("qk_done"), (l + 1) * 10)
                pe.wait_ge(sem("mask_done"), l + 1)
                pe.wait_ge(sem("rnn_i"), (l + 1) * 8)
                scores(0)
                scores(1)
                for j in range(len(items)):
                    if j == 3:
                        pe.wait_ge(sem("br_lo"), (l * 4 + 1) * KD)
                    turn(j)
                    if j + 2 < len(items):
                        scores(j + 2)
                    merge_part(j)
                    values(j)

            def neighbours():
                items = [(hh, i) for hh in range(HEADS) for i in range(NQT)]
                ph = AT["att2"]
                pe.wait_ge(sem("v2_rows"), 1)
                for e in range(4):
                    for c in range(4):
                        m = pe.transpose(aux[e // 2][:, e % 2, c * P:(c + 1) * P], vT2[:, e, c * P:(c + 1) * P], ident[:, :])
                m.then_inc(sem("v2_turned"), 1)
                pe.wait_ge(sem("v2_copied"), 4)

                def scores(j):
                    hh, i = items[j]
                    rows = slice(64 * (hh % 2), 64 * (hh % 2) + 64)
                    if j:
                        pe.wait_ge(sem("na_scored"), j)
                    pe.matmul(aux[0][:, 0, :], q2[rows, hh // 2, i * P:(i + 1) * P], k2[rows, hh // 2, :],
                              start=True, stop=True).then_inc(sem("na_s"), 1)

                def turn(j):
                    pe.wait_ge(sem("na_p"), j + 1)
                    if j:
                        pe.wait_ge(sem("na_pt"), j)
                    for c in range(4):
                        m = pe.transpose(aux[1][:, 0, c * P:(c + 1) * P], sm2[:, j % 2, c * P:(c + 1) * P], ident[:, :])
                    m.then_inc(sem("na_turned"), 1)

                def values(j):
                    hh, i = items[j]
                    s = ph.slot(hh // 2)
                    if hh % 2 == 0 and i == 0:
                        pe.wait_ge(evac[s], ph.nth(hh // 2))
                    pe.wait_ge(sem("na_pt"), j + 1)
                    for c in range(4):
                        m = pe.matmul(acc[s][64 * (hh % 2):64 * (hh % 2) + 64, 0, i * P:(i + 1) * P],
                                      v2[:, c, 64 * hh:64 * hh + 64], pts2[:, c, :], start=c == 0, stop=c == 3)
                    m.then_inc(sem("na_pv"), 1)

                scores(0)
                for j in range(len(items)):
                    if j + 1 < len(items):
                        scores(j + 1)
                    turn(j)
                    values(j)

            def ssm():
                for r in range(4):
                    pe.wait_ge(sem("ss_rep"), 2 * (r + 1))
                    pe.wait_ge(sem("ss_cpow"), 2 * (r + 1))
                    if r:
                        pe.wait_ge(sem("ss_y"), 16 * r)
                    for d in range(2):
                        for u in range(4):
                            e = d * 4 + u
                            pe.matmul(aux[0][:, d, u * P:(u + 1) * P], reps[:, 0, e].rearrange("p a b -> p (a b)"),
                                      cp_[:, 0, e, d:d + 4].rearrange("p a b -> p (a b)"), start=True, stop=False)
                            m = pe.matmul(aux[0][:, d, u * P:(u + 1) * P], reps[:, 1, e].rearrange("p a b -> p (a b)"),
                                          cp_[:, 1, e, d:d + 4].rearrange("p a b -> p (a b)"), start=False, stop=True)
                    m.then_inc(sem("ss_lags"), 1)
                    pe.wait_ge(sem("ss_bpow"), 4 * (r + 1))
                    for g in range(4):
                        if g or r:
                            pe.wait_ge(sem("ss_w1"), 4 * r + g)
                        for c in range(4):
                            e, z = (g * 4 + c) // 2, c % 2
                            m = pe.transpose(aux[1][:, 0, c * P:(c + 1) * P], ap_[:, z, e].rearrange("p a b -> p (a b)"),
                                             ident[:, :])
                        m.then_inc(sem("ss_w1_turned"), 1)
                    pe.wait_ge(sem("ss_w1"), 4 * (r + 1))
                    pe.wait_ge(sem("ss_u"), 32 * (r + 1))
                    pe.wait_ge(sem("ss_t"), r + 1)
                    for z in range(2):
                        for e in range(8):
                            m = pe.matmul(aux[z][:, e // 4, (e % 4) * NC:(e % 4 + 1) * NC], w1s[:, e, z],
                                          us[:, e // 4, e % 4], start=True, stop=True)
                    m.then_inc(sem("ss_s"), 1)
                    pe.wait_ge(sem("ss_x"), 4 * (r + 1))
                    for u in range(4):
                        out = aux[0][:, 0, u * NC:(u + 1) * NC]
                        pe.matmul(out, tm_[:, u], us[:, 0, u], start=True, stop=False)
                        for d in range(2):
                            for z in range(2):
                                lhs = cp_[:, z, d * 4 + u, 1 - d:5 - d].rearrange("p a b -> p (a b)")
                                m = pe.matmul(out, lhs, st_[:, z, d * 4 + u, d:d + NC], start=False, stop=(d, z) == (1, 1))
                    m.then_inc(sem("ss_out"), 1)

            pe.wait_ge(sem("consts_set"), 3)
            pe.wait_ge(sem("ident_loaded"), 16)
            for l in range(DEPTH):
                sumsq(2 * l)
                proj(l)
                index(l)
                for n in range(16):
                    tile(AT[f"conv{l}"], n, R(nhi, nlo, T1), T1)
                rnn(l)
                mix(l)
                pe.wait_ge(sem("br_lo"), (l * 4 + 1) * KD + 1)
                ph = AT[f"mg_att{l}"]
                tile(ph, 0, R(nhi, nlo, T1), T1)
                pe.wait_ge(sem("br_lo"), (l * 4 + 2) * KD)
                tile(ph, 1, R(bhi, blo, T1), T1)
                with pe.Fori(1, LN_AFTER) as m:
                    tile(ph, 0, R(nhi, nlo, T1), T1, m=m, step=2)
                    tile(ph, 1, R(bhi, blo, T1), T1, m=m, step=2)
                ln_mean(l)
                for n in range(2 * LN_AFTER, 2 * LN_AFTER + 2):
                    tile(ph, n, R(bhi, blo, T1) if n % 2 else R(nhi, nlo, T1), T1)
                ln_square(l)
                for n in range(2 * LN_AFTER + 2, 2 * KD):
                    tile(ph, n, R(bhi, blo, T1) if n % 2 else R(nhi, nlo, T1), T1)
                ph = AT[f"mg_conv{l}"]
                tile(ph, 0, R(nhi, nlo, T1), T1)
                pe.wait_ge(sem("br_lo"), (l * 4 + 3) * KD)
                tile(ph, 1, R(bhi, blo, T1), T1)
                with pe.Fori(1, KD) as m:
                    tile(ph, 0, R(nhi, nlo, T1), T1, m=m, step=2)
                    tile(ph, 1, R(bhi, blo, T1), T1, m=m, step=2)
                pe.wait_ge(sem("br_lo"), (l * 4 + 4) * KD)
                with pe.Fori(0, KD // 2) as m:
                    for j in range(2):
                        tile(AT[f"out{l}"], j, R(bhi, blo, T1), T1, m=m, step=2)
                ffn(2 * l + 1, f"up{l}", f"down{l}", T1)
            ffn(4, "up2", "down2", SEQ)
            sumsq(5)
            for i in range(12):
                tile(AT["qkv2"], i, R(nhi, nlo, S), S, fresh=5 if i == 0 else None)
            for i in range(4):
                tile(AT["sin2"], i, R(nhi, nlo, S), S)
            neighbours()
            ssm()
            pe.wait_ge(sem("y_lo"), 4)
            for i in range(4):
                tile(AT["glu2"], i, R(zhi, zlo, S), S, nk=4)
            pe.wait_ge(sem("z_lo"), 4)
            with pe.Fori(0, KD) as m:
                tile(AT["mg2"], 0, R(nhi, nlo, S), S, m=m, step=4)
                tile(AT["mg2"], 1, R(attn_hi, attn_lo, S), S, nk=4, m=m, step=4)
                tile(AT["mg2"], 2, R(nhi, nlo, S), S, m=m, step=4)
                tile(AT["mg2"], 3, R(zhi, zlo, S), S, nk=4, m=m, step=4)
            pe.wait_ge(sem("m2_lo"), KD)
            with pe.Fori(0, KD // 2) as m:
                for j in range(2):
                    tile(AT["out2"], j, R(mhi, mlo, S), S, m=m, step=2)
            ffn(6, "up3", "down3", SEQ)
            sumsq(7)
            normed(7)
            pe.wait_ge(sem("p_lo"), 2)
            with pe.Fori(0, KD) as m:
                tile(AT["ple2"], 0, R(nhi, nlo, S), S, m=m, step=2)
                tile(AT["ple2"], 1, R(phi, plo, S), S, nk=2, m=m, step=2)
            sumsq(8)

        @block.scalar
        def _(act):
            def block_done(b):
                act.wait_ge(pe_block, b)

            def norm(i):
                T = NORM_T[i]
                if i == 0:
                    act.wait_ge(sem("h_loaded"), 16)
                    for j in range(KD):
                        if j >= 2:
                            act.wait_ge(sem("norm_added"), j - 1)
                        act.activation(fsq[:, j % 2, :], h[:, j, :], ACT.Square).then_inc(sem("norm_square"), 1)
                act.wait_ge(sem("norm_summed"), i + 1)
                act.activation(halves(fstd[:, 0:T], T), aux[0][:, :, 0:T // 2], ACT.Sqrt, bias=EPS, scale=1.0 / D)\
                   .then_inc(sem("norm_std"), 1)
                if i == 8:
                    return
                for j in range(KD):
                    act.wait_ge(sem("norm_scaled"), i * KD + j + 1)
                    act.activation(nhi[:, j, 0:T], ftmp[:, j % 2, 0:T], ACT.Copy).then_inc(sem("norm_hi"), 1)

            def ffn(i, up, T):
                norm(i)
                ph, f = AT[up], FFI[up]
                down = AT[up.replace("up", "down")]
                with act.Fori(0, KF) as m:
                    block_done(m * 2 + (ph.block(0) + 1))
                    act.wait_ge(evac[ph.slot(1)], m + ph.nth(1))
                    act.activation(halves(fsl[:, 0:T], T), accv(ph.slot(0), T), ACT.Silu).then_inc(evac[ph.slot(0)], 1)
                    act.wait_ge(evac[ph.slot(1)], m + (ph.nth(1) + 1))
                    act.activation(ahi[:, bass.ds(m, 1), 0:T], fpr[:, 0:T].unsqueeze(1), ACT.Copy).then_inc(sem("ff_hi"), 1)
                squares(i + 1, down)

            def squares(i, ph):
                with act.Fori(0, KD // 2) as m:
                    for j in range(2):
                        act.wait_ge(evac[ph.slot(j)], m + (ph.nth(j) + 1))
                        act.wait_ge(sem("norm_added"), m * 2 + (i * KD + j - 1))
                        act.activation(fsq[:, j].unsqueeze(1), h[:, bass.ds(m * 2 + j, 1), :], ACT.Square)\
                           .then_inc(sem("norm_square"), 1)

            def proj(l):
                qk, vp, qp = AT[f"qk{l}"], AT[f"v{l}"], AT[f"qi{l}"]

                def std(e):
                    it = l * 10 + e
                    act.wait_ge(sem("qk_sum"), it + 1)
                    if it:
                        act.wait_ge(sem("qk_done"), it)
                    act.activation(halves(tstd[:, :], T1), aux[0][:, :, 0:T1 // 2], ACT.Sqrt, bias=EPS, scale=1.0 / HD)\
                       .then_inc(sem("qk_std"), 1)

                for e in range(10):
                    it, s = l * 10 + e, qk.slot(e)
                    block_done(qk.block(e) + 1)
                    if e >= 2:
                        act.wait_ge(sem("qk_sum"), it - 1)
                    act.activation(halves(tsq[:, e % 2, :], T1), accv(s, T1), ACT.Square).then_inc(sem("qk_square"), 1)
                    if e >= 2:
                        act.wait_ge(sem("qk_done"), it - 1)
                    act.activation(halves(tqg[:, e % 2, :], T1), accv(s, T1), ACT.Copy,
                                   scale=col("q_g" if e < 8 else "k_g", l)).then_inc(evac[s], 1)
                    act.wait_ge(evac[s], qk.nth(e) + 1)
                    act.activation(tsw[0:64, e % 2, :], tqg[64:128, e % 2, :], ACT.Copy)
                    act.activation(tsw[64:128, e % 2, :], tqg[0:64, e % 2, :], ACT.Copy).then_inc(sem("qk_swap"), 1)
                    if e:
                        std(e - 1)
                for e in range(KV):
                    block_done(vp.block(e) + 1)
                    act.activation(halves(vT[:, e, :], T1), accv(vp.slot(e), T1), ACT.Copy).then_inc(evac[vp.slot(e)], 1)
                    if e == 0:
                        std(9)
                for e in range(5):
                    it, s = l * 5 + e, qp.slot(e)
                    block_done(qp.block(e) + 1)
                    if e < 2:
                        act.wait_ge(sem("qk_done"), (l + 1) * 10)
                    else:
                        act.wait_ge(sem("qi_done"), it - 1)
                    a, x, w = accv(s, T1), tqg[:, e % 2, :], tsw[:, e % 2, :]
                    if e < 4:
                        act.activation(halves(x, T1), a, ACT.Copy).then_inc(evac[s], 1)
                    else:
                        act.activation(halves(x[0:64], T1), a[0:64], ACT.Copy)
                        act.activation(halves(x[64:128], T1), a[0:64], ACT.Copy)
                        act.activation(halves(wbuf[:, :], T1), a[64:96], ACT.Copy, scale=IXH ** -0.5 * IXD ** -0.5)\
                           .then_inc(evac[s], 1)
                    act.wait_ge(evac[s], qp.nth(e) + 1)
                    for c in range(4):
                        m = act.activation(w[32 * c:32 * c + 32], x[32 * (c ^ 1):32 * (c ^ 1) + 32], ACT.Copy)
                    m.then_inc(sem("qi_swap"), 1)
                    if e == 3:
                        act.wait_ge(sem("v_turned"), l + 1)
                        for c in range(KV):
                            act.activation(v[:, 0:4, c * HD:(c + 1) * HD],
                                           aux[1][:, c, :].rearrange("p (a b) -> p a b", a=4), ACT.Copy).then_inc(sem("v_copied"), 1)
                            act.activation(v[0:16, 4, c * HD:(c + 1) * HD], aux[0][0:16, c, 0:P], ACT.Copy)\
                               .then_inc(sem("v_copied"), 1)
                    if e == 4:
                        act.wait_ge(evac[s], qp.nth(e) + 1)
                        act.sem_inc(sem("wi_rows"), 1)
                act.wait_ge(sem("wi_turned"), l + 1)
                act.activation(wi[:, :, :], aux[0][:, 1, 0:NQT * 32].rearrange("p (a b) -> p a b", a=NQT)[:, :, 0:IXH],
                               ACT.Copy).then_inc(sem("wi_copied"), 1)

            def index(l):
                for i in range(NQT):
                    W = META + P * (i + 1)
                    for hh in range(IXH):
                        it = (l * NQT + i) * IXH + hh
                        act.wait_ge(sem("ix_logit"), it + 1)
                        if hh >= 2 or i:
                            act.wait_ge(sem("ix_acc"), it - 1)
                        src = aux[hh % 2][:, :, :].rearrange("p a b -> p (a b)")[:, 0:W]
                        act.activation(tsq[:, hh % 2, 0:W], src, ACT.Relu).then_inc(sem("ix_relu"), 1)

            def rnn(l):
                ph = AT[f"rnn{l}"]

                def gates(n):
                    it = l * 8 + n
                    act.wait_ge(sem("rnn_gates"), it + 1)
                    if n:
                        act.wait_ge(sem("rnn_b"), it)
                    act.activation(halves(rr[:, :], T1), aux[0][:, :, 0:T1 // 2], ACT.Tanh, bias=hba[:, l, 0, n:n + 1],
                                   scale=0.5).then_inc(sem("rnn_r"), 1)
                    act.activation(halves(ri[:, :], T1), aux[1][:, :, 0:T1 // 2], ACT.Tanh, bias=hba[:, l, 1, n:n + 1],
                                   scale=0.5).then_inc(sem("rnn_i"), 1)
                    act.wait_ge(sem("rnn_r"), it + 1)
                    act.activation(rt[:, :], rr[:, :], ACT.Tanh, bias=spc[:, l, n:n + 1], scale=spc[:, l, n:n + 1])\
                       .then_inc(sem("rnn_t"), 1)
                    if n:
                        act.wait_ge(sem("rnn_scan"), it)
                    act.activation(ra[:, :], rr[:, :], ACT.Exp, bias=nspc[:, l, n:n + 1], scale=nspc[:, l, n:n + 1])\
                       .then_inc(sem("rnn_a"), 1)
                    act.wait_ge(sem("rnn_m"), 3 * (it + 1))
                    act.activation(rb[:, :], rb[:, :], ACT.Sqrt, scale=0.5).then_inc(sem("rnn_sqrt"), 1)

                def part(n):
                    it = l * 8 + n
                    act.wait_ge(sem("rnn_out"), it + 1)
                    act.activation(bhi[:, n, :], rh[:, :], ACT.Copy).then_inc(sem("br_hi"), 1)

                act.wait_ge(sem("rnn_pad"), l + 1)
                for n in range(8):
                    it = l * 8 + n
                    sx, sy = ph.slot(2 * n), ph.slot(2 * n + 1)
                    block_done(ph.block(2 * n) + 1)
                    if n:
                        act.wait_ge(sem("rnn_conv"), 4 * it)
                    act.activation(halves(rx[:, CONV - 1:], T1), accv(sx, T1), ACT.Copy).then_inc(evac[sx], 1)
                    if n:
                        gates(n - 1)
                        part(n - 1)
                    block_done(ph.block(2 * n + 1) + 1)
                    act.activation(halves(rg[:, :], T1), accv(sy, T1), ACT.Gelu_apprx_tanh).then_inc(evac[sy], 1)
                gates(7)
                part(7)

            def merge(l, name):
                ph = AT[f"mg_{name}{l}"]
                with act.Fori(0, KD) as m:
                    block_done(m * 2 + (ph.block(0) + 1))
                    act.wait_ge(evac[ph.slot(1)], m + ph.nth(1))
                    act.activation(halves(sg[:, :], T1), accv(ph.slot(0), T1), ACT.Sigmoid).then_inc(evac[ph.slot(0)], 1)

            def conv_gates(l):
                ph = AT[f"conv{l}"]
                for n in range(KD):
                    block_done(ph.block(2 * n) + 1)
                    if n:
                        act.wait_ge(evac[1], ph.nth(2 * n - 1) + 1)
                    act.activation(halves(csg[:, :], T1), accv(0, T1), ACT.Sigmoid).then_inc(evac[0], 1)

            def att_split(l):
                for n in range(KD):
                    if n == 0:
                        block_done(AT[f"mg_att{l}"].b0)
                    act.wait_ge(evac[1], AT[f"att{l}"].nth(n) + 1)
                    act.activation(bhi[:, n], q[:, n], ACT.Copy).then_inc(sem("br_hi"), 1)

            def gate(ph, m):
                block_done(ph.block(0) + 2 * m + 1)
                act.wait_ge(evac[ph.slot(1)], ph.nth(1) + m)
                act.activation(halves(sg[:, :], T1), accv(ph.slot(0), T1), ACT.Sigmoid).then_inc(evac[ph.slot(0)], 1)

            def mg_att(l):
                ph = AT[f"mg_att{l}"]
                with act.Fori(0, LN_AFTER) as m:
                    block_done(m * 2 + (ph.block(0) + 1))
                    act.wait_ge(evac[ph.slot(1)], m + ph.nth(1))
                    act.activation(halves(sg[:, :], T1), accv(ph.slot(0), T1), ACT.Sigmoid).then_inc(evac[ph.slot(0)], 1)
                ln_first(l)
                gate(ph, LN_AFTER)
                ln_second(l)
                for m in range(LN_AFTER + 1, KD):
                    gate(ph, m)
                for n in range(KD):
                    act.wait_ge(sem("cv_scaled"), l * 8 + n + 1)
                    act.activation(cu[:, n], cu[:, n], ACT.Silu, bias=col("ln_b", l, n), scale=col("ln_g", l, n))\
                       .then_inc(sem("cv_silu"), 1)
                block_done(AT[f"mg_conv{l}"].b0)
                act.wait_ge(sem("cv_silu"), (l + 1) * 8)
                for n in range(KD):
                    act.activation(bhi[:, n], cu[:, n], ACT.Copy).then_inc(sem("br_hi"), 1)

            def ln_first(l):
                act.wait_ge(sem("cv_mean"), l + 1)
                act.activation(halves(cstat[:, 0], T1), aux[0][:, :, 0:T1 // 2], ACT.Copy, scale=1.0 / D)\
                   .then_inc(sem("cv_mean_read"), 1)

            def ln_second(l):
                for n in range(KD):
                    act.wait_ge(sem("cv_centred"), l * 8 + n + 1)
                    if n >= 2:
                        act.wait_ge(sem("cv_summed"), l * 8 + n - 1)
                    act.activation(csq[:, n % 2], cu[:, n], ACT.Square).then_inc(sem("cv_square"), 1)
                act.wait_ge(sem("cv_summed"), (l + 1) * 8)
                act.activation(halves(cstat[:, 1], T1), aux[1][:, :, 0:T1 // 2], ACT.Sqrt, bias=EPS, scale=1.0 / D)\
                   .then_inc(sem("cv_std"), 1)

            def mix(l):
                ph, mg = AT[f"att{l}"], AT[f"mg_rnn{l}"]
                items = [(hh, i) for hh in range(HEADS) for i in range(NQT + 1)]
                n0 = l * len(items)

                def exps(j):
                    b = j % 3
                    r, W = (P, META + (items[j][1] + 1) * P) if items[j][1] < NQT else (META, META)
                    act.wait_ge(sem("at_max"), n0 + j + 1)
                    act.activation(sm[0:r, b, 0:W], sm[0:r, b, 0:W], ACT.Exp, bias=nmx[0:r, b:b + 1],
                                   accum_out=rsum[0:r, b:b + 1]).then_inc(sem("at_exp"), 1)

                def turned(j):
                    i = items[j][1]
                    act.wait_ge(sem("at_turned"), n0 + j + 1)
                    if j:
                        act.wait_ge(sem("at_pv"), n0 + j)
                    if i < NQT:
                        c = i + 1
                        act.activation(pts[:, 0:c, :], aux[1][:, :, :].rearrange("p a (b c) -> p (a b) c", c=P)[:, 0:c, :], ACT.Copy)
                        act.activation(pts[0:META, c, :], aux[1][0:META, c // 4, (c % 4) * P:(c % 4 + 1) * P], ACT.Copy)\
                           .then_inc(sem("at_pt"), 1)
                    else:
                        act.activation(pts[0:META, 0, 0:META], aux[1][0:META, 0, 0:META], ACT.Copy).then_inc(sem("at_pt"), 1)

                exps(0)
                exps(1)
                for j in range(len(items)):
                    hh, i = items[j]
                    turned(j)
                    if i == 0 and hh:
                        s = ph.slot(hh - 1)
                        act.wait_ge(sem("at_pv"), n0 + j)
                        act.activation(q[:, hh - 1, META:], acc[s][:, 0, :], ACT.Copy)
                        act.activation(q[:, hh - 1, 0:META], acc[s][:, 1, 0:META], ACT.Copy).then_inc(evac[s], 1)
                    if j + 2 < len(items):
                        exps(j + 2)
                    if i == 2:
                        t = 2 * hh
                        block_done(mg.block(t) + 1)
                        if t:
                            act.wait_ge(evac[0], mg.nth(t - 1) + 1)
                        act.activation(halves(sg[:, :], T1), accv(0, T1), ACT.Tanh, scale=0.5).then_inc(evac[0], 1)
                s, hh = ph.slot(HEADS - 1), HEADS - 1
                act.wait_ge(sem("at_pv"), n0 + len(items))
                act.activation(q[:, hh, META:], acc[s][:, 0, :], ACT.Copy)
                act.activation(q[:, hh, 0:META], acc[s][:, 1, 0:META], ACT.Copy).then_inc(evac[s], 1)

            def neighbours():
                ph = AT["att2"]
                act.wait_ge(sem("v2_turned"), 1)
                for e in range(4):
                    act.activation(v2[:, :, e * P:(e + 1) * P], aux[e // 2][:, e % 2, :].rearrange("p (a b) -> p a b", a=4),
                                   ACT.Copy).then_inc(sem("v2_copied"), 1)
                for e in range(HEADS):
                    act.wait_ge(sem("na_table_masked"), 1)
                items = [(hh, i) for hh in range(HEADS) for i in range(NQT)]

                def exps(j):
                    act.wait_ge(sem("na_max"), j + 1)
                    act.activation(sm2[:, j % 2], sm2[:, j % 2], ACT.Exp, bias=sc2[:, 1, j % 2:j % 2 + 1],
                                   accum_out=sc2[:, 2, j % 2:j % 2 + 1]).then_inc(sem("na_exp"), 1)

                exps(0)
                for j in range(len(items)):
                    hh, i = items[j]
                    if j + 1 < len(items):
                        exps(j + 1)
                    act.wait_ge(sem("na_turned"), j + 1)
                    if j:
                        act.wait_ge(sem("na_pv"), j)
                    act.activation(pts2[:, :, :], aux[1][:, 0, :].rearrange("p (a b) -> p a b", a=4), ACT.Copy)\
                       .then_inc(sem("na_pt"), 1)
                    if hh % 2 and i == NQT - 1:
                        s, t = ph.slot(hh // 2), hh // 2
                        act.wait_ge(sem("na_pv"), j + 1)
                        if t:
                            act.wait_ge(sem("attn2_lo"), t)
                        act.activation(ot2[:, :], acc[s][:, 0, :], ACT.Copy).then_inc(evac[s], 1)
                        act.wait_ge(evac[s], ph.nth(t) + 1)
                        act.activation(attn_hi[:, t], ot2[:, :], ACT.Copy).then_inc(sem("attn2_hi"), 1)

            def ssm():
                act.wait_ge(sem("attn2_lo"), 4)
                act.dma_start(smp[:, :, :], A_ssm[0:3].rearrange("a p n -> p a n")[:, :, 0:32]).then_inc(sem("ssm_loaded"), 16)
                act.dma_start(sbc[:, :, :, :].rearrange("p a b c -> p a (b c)"), A_ssm[3:7].rearrange("a p n -> p a n"))\
                   .then_inc(sem("ssm_loaded"), 16)
                act.dma_start(chk[:, :], A_chunk).then_inc(sem("ssm_loaded"), 16)
                act.wait_ge(sem("ssm_loaded"), 48)
                act.activation(spw[:, 0], smp[:, 0], ACT.Exp).then_inc(sem("ss_dt"), 1)
                act.wait_ge(sem("ss_reduced"), 1)
                act.activation(spw[:, 4], spw[:, 2], ACT.Sin)
                act.activation(spw[:, 5], spw[:, 2], ACT.Sin, scale=0.5)
                act.activation(spw[:, 6], spw[:, 1], ACT.Tanh, scale=0.5)
                act.activation(spw[:, 7], spw[:, 1], ACT.Exp, scale=4.0).then_inc(sem("ss_waves"), 1)
                for r in range(4):
                    if r:
                        act.wait_ge(sem("ss_out"), r)
                    for u in range(4):
                        src = uin[32 * u:32 * u + 32, r, :].rearrange("p (c j) -> p j c", j=SC)
                        for j in range(SC):
                            act.activation(us[32 * j:32 * j + 32, 0, u, :], src[:, j, :], ACT.Copy).then_inc(sem("ss_u"), 1)
                            act.activation(us[32 * j:32 * j + 32, 1, u, :], src[:, j, ::-1], ACT.Copy).then_inc(sem("ss_u"), 1)
                    act.wait_ge(sem("ss_bb"), r + 1)
                    for z in range(2):
                        act.activation(reps[:, z], bb[:, z].unsqueeze(2).broadcast_to([P, 8, 4, 32]), ACT.Copy)\
                           .then_inc(sem("ss_rep"), 1)
                    act.wait_ge(sem("ss_angle"), r + 1)
                    act.activation(cs_[:, 1], w8[:, :, :], ACT.Sin)
                    act.activation(cs_[:, 0], w8[:, :, :], ACT.Sin, scale=0.5).then_inc(sem("ss_sines"), 1)
                    act.wait_ge(sem("ss_lags"), r + 1)
                    act.wait_ge(sem("ss_t_zero"), r + 1)
                    lag = aux[0][:, 0, :].rearrange("p (u c) -> p u c", u=4)
                    for j in range(SC):
                        m = act.activation(tm_[32 * j:32 * j + 32, :, 32 * j:P], lag[32 * j:32 * j + 32, :, 0:P - 32 * j], ACT.Copy)
                    m.then_inc(sem("ss_t_forward"), 1)
                    for g in range(4):
                        act.wait_ge(sem("ss_w1_turned"), 4 * r + g + 1)
                        act.activation(w1s[:, 2 * g:2 * g + 2].rearrange("p a b c -> p (a b c)"), aux[1][:, 0, :], ACT.Copy)\
                           .then_inc(sem("ss_w1"), 1)
                    act.wait_ge(sem("ss_out"), r + 1)
                    for u in range(4):
                        dst = yv[32 * u:32 * u + 32, r, :].rearrange("p (c j) -> p j c", j=SC)
                        for j in range(SC):
                            act.activation(dst[:, j, :], aux[0][32 * j:32 * j + 32, 0, u * NC:(u + 1) * NC], ACT.Copy)\
                               .then_inc(sem("ss_y"), 1)
                for r in range(4):
                    act.wait_ge(sem("ss_skip"), r + 1)
                    act.activation(yv[:, r], yv[:, r], ACT.Gelu_apprx_tanh).then_inc(sem("y_gelu"), 1)
                for r in range(4):
                    act.wait_ge(sem("y_gelu"), r + 1)
                    act.activation(zhi[:, r], yv[:, r], ACT.Copy).then_inc(sem("y_hi"), 1)
                ph = AT["glu2"]
                for i in range(4):
                    block_done(ph.block(i) + 1)
                    act.activation(halves(uin[:, i], S), accv(ph.slot(i), S), ACT.Sigmoid, bias=col("glu_b", None, i))\
                       .then_inc(evac[ph.slot(i)], 1)
                for i in range(4):
                    act.wait_ge(sem("z_done"), i + 1)
                    if i == 0:
                        block_done(ph.block(3) + 1)
                    act.activation(zhi[:, i], yv[:, i], ACT.Copy).then_inc(sem("z_hi"), 1)

            act.dma_start(h[:, :, :], A_h).then_inc(sem("h_loaded"), 16)
            act.dma_start(par[:, :], A_par).then_inc(sem("par_loaded"), 16)
            act.dma_start(ident[:, :], A_ident).then_inc(sem("ident_loaded"), 16)
            act.wait_ge(sem("par_loaded"), 16)
            act.wait_ge(sem("lam_abs"), 1)
            act.activation(prep[:, 1, :], prep[:, 0, :], ACT.Exp, scale=-1.0).then_inc(sem("lam_exp"), 1)
            act.wait_ge(sem("spc_done"), 1)
            for l in range(DEPTH):
                norm(2 * l)
                act.wait_ge(sem("norm_lo"), (2 * l + 1) * KD)
                act.dma_start(rope[:, :, :], A_rope.rearrange("a p n -> p a n")).then_inc(sem("rope_loaded"), 16)
                act.dma_start(rnn_w[:, :, :, :].rearrange("p a b c -> p a (b c)"), A_gate[l].rearrange("a p n -> p a n"))\
                   .then_inc(sem("rnn_w_loaded"), 16)
                proj(l)
                index(l)
                conv_gates(l)
                rnn(l)
                mix(l)
                att_split(l)
                mg_att(l)
                merge(l, "conv")
                for n in range(KD):
                    if n == 0:
                        act.wait_ge(sem("mg_add"), (2 * l + 2) * KD + 1)
                        block_done(AT[f"out{l}"].b0)
                    act.activation(bhi[:, n], merged[:, n], ACT.Copy).then_inc(sem("br_hi"), 1)
                squares(2 * l + 1, AT[f"out{l}"])
                ffn(2 * l + 1, f"up{l}", T1)
            ffn(4, "up2", SEQ)
            norm(5)
            act.wait_ge(sem("norm_lo"), 6 * KD)
            act.dma_start(namask[:, :], A_namask).then_inc(sem("na_loaded"), 16)
            ph = AT["qkv2"]
            for i in range(12):
                s = ph.slot(i)
                dst = (q2, k2, vT2)[i // 4][:, i % 4]
                block_done(ph.block(i) + 1)
                act.activation(halves(dst, S), accv(s, S), ACT.Copy, scale=HD2 ** -0.5 if i < 4 else 1.0).then_inc(evac[s], 1)
            h_ready(act, ph)
            act.sem_inc(sem("v2_rows"), 1)
            ph = AT["sin2"]
            for i in range(4):
                block_done(ph.block(i) + 1)
                act.activation(halves(uin[:, i], S), accv(ph.slot(i), S), ACT.Copy).then_inc(evac[ph.slot(i)], 1)
            act.wait_ge(sem("v2_turned"), 1)
            for half in range(2):
                for hh in range(HEADS):
                    act.dma_start(natab[64 * half:64 * half + 64, hh], A_natab[half, hh]).then_inc(sem("na_loaded"), 16)
            neighbours()
            ssm()
            ph = AT["mg2"]
            with act.Fori(0, KD) as m:
                for z in range(2):
                    block_done(m * 4 + (ph.block(2 * z) + 1))
                    act.wait_ge(evac[ph.slot(1)], m * 2 + (ph.nth(1) + z))
                    act.activation(halves(sg2[:, :], S), accv(ph.slot(0), S), ACT.Sigmoid).then_inc(evac[ph.slot(0)], 1)
            for n in range(KD):
                act.wait_ge(sem("m2_add"), n + 2)
                act.activation(mhi[:, n], merged2[:, n], ACT.Copy).then_inc(sem("m2_hi"), 1)
            squares(6, AT["out2"])
            ffn(6, "up3", SEQ)
            norm(7)
            act.wait_ge(sem("norm_lo"), 8 * KD)
            act.dma_start(pin[:, :, :], A_p.rearrange("a p n -> p a n")).then_inc(sem("p_loaded"), 16)
            act.wait_ge(sem("p_loaded"), 16)
            act.activation(phi[:, :, :], pin[:, :, :], ACT.Copy).then_inc(sem("p_hi"), 1)
            ph = AT["ple2"]
            with act.Fori(0, KD) as m:
                block_done(m * 2 + (ph.block(0) + 1))
                act.wait_ge(evac[ph.slot(1)], m + ph.nth(1))
                act.activation(halves(psg[:, :], S), accv(ph.slot(0), S), ACT.Sigmoid).then_inc(evac[ph.slot(0)], 1)
                act.wait_ge(sem("ple_added"), m + 2)
                act.wait_ge(sem("norm_added"), m + 8 * KD)
                act.activation(fsq[:, 0].unsqueeze(1), h[:, bass.ds(m, 1), :], ACT.Square).then_inc(sem("norm_square"), 1)
            norm(8)

        @block.vector
        def _(dve):
            def block_done(b):
                dve.wait_ge(pe_block, b)

            chain = [0]

            def then(ins):
                chain[0] += 1
                ins.then_inc(sem("dve_step"), 1)
                dve.wait_ge(sem("dve_step"), chain[0])

            def norm(i):
                T = NORM_T[i]
                name, l = NORM_G[i]
                if i == 0:
                    then(dve.memset(facc[:, :], 0.0))
                    for j in range(KD):
                        dve.wait_ge(sem("norm_square"), j + 1)
                        if j:
                            dve.wait_ge(sem("norm_added"), j)
                        dve.tensor_tensor(facc[:, :], facc[:, :], fsq[:, j % 2], ALU.add).then_inc(sem("norm_added"), 1)
                dve.wait_ge(sem("norm_std"), i + 1)
                then(dve.reciprocal(frs[:, 0:T], fstd[:, 0:T]))
                for j in range(KD):
                    if i < 8:
                        if j >= 2:
                            dve.wait_ge(sem("norm_lo"), i * KD + j - 1)
                        dve.scalar_tensor_tensor(ftmp[:, j % 2, 0:T], hview(T)[:, j], col(name, l, j), frs[:, 0:T],
                                                 ALU.mult, ALU.mult).then_inc(sem("norm_scaled"), 1)
                        dve.wait_ge(sem("norm_hi"), i * KD + j + 1)
                        dve.tensor_tensor(nlo[:, j, 0:T], ftmp[:, j % 2, 0:T], nhi[:, j, 0:T].bitcast(F32), ALU.subtract)\
                           .then_inc(sem("norm_lo"), 1)
                    else:
                        dve.scalar_tensor_tensor(yout[:, j], hview(T)[:, j], col(name, l, j), frs[:, 0:T],
                                                 ALU.mult, ALU.mult).then_inc(sem("final_out"), 1)

            def ffn(i, up, down, T, scale):
                norm(i)
                ph, f = AT[up], FFI[up]
                with dve.Fori(0, KF) as m:
                    block_done(m * 2 + (ph.block(1) + 1))
                    dve.wait_ge(evac[ph.slot(0)], m + (ph.nth(0) + 1))
                    dve.wait_ge(sem("ff_lo"), m + (f * KF + 1))
                    dve.tensor_tensor(halves(fpr[:, 0:T], T), accv(ph.slot(1), T), halves(fsl[:, 0:T], T), ALU.mult)\
                       .then_inc(evac[ph.slot(1)], 1)
                    dve.wait_ge(sem("ff_hi"), m + (f * KF + 1))
                    dve.tensor_tensor(alo[:, bass.ds(m, 1), 0:T], fpr[:, 0:T].unsqueeze(1),
                                      ahi[:, bass.ds(m, 1), 0:T].bitcast(F32), ALU.subtract).then_inc(sem("ff_lo"), 1)
                add_to_h(AT[down], T, i + 1, scale)

            def add_to_h(ph, T, i, scale=1.0):
                dve.wait_ge(sem("norm_summed"), i)
                dve.memset(facc[:, :], 0.0).then_inc(sem("norm_clear"), 1)
                with dve.Fori(0, KD // 2) as m:
                    for j in range(2):
                        s = ph.slot(j)
                        block_done(m * (2 * ph.per) + (ph.block(j) + ph.per))
                        hv = h[:, bass.ds(m * 2 + j, 1), T1 - T:T1].rearrange("p a (b c) -> p (a b) c", b=2)
                        if scale == 1.0:
                            dve.tensor_tensor(hv, accv(s, T), hv, ALU.add).then_inc(evac[s], 1)
                        else:
                            dve.scalar_tensor_tensor(hv, accv(s, T), scale, hv, ALU.mult, ALU.add).then_inc(evac[s], 1)
                        dve.wait_ge(sem("norm_clear"), i)
                        dve.wait_ge(sem("norm_square"), m * 2 + (i * KD + j + 1))
                        dve.wait_ge(sem("norm_added"), m * 2 + (i * KD + j))
                        dve.tensor_tensor(facc[:, :], facc[:, :], fsq[:, j], ALU.add).then_inc(sem("norm_added"), 1)

            def proj(l):
                dve.wait_ge(sem("rope_loaded"), 16 * (l + 1))
                for e in range(10):
                    it = l * 10 + e
                    x, w = tqg[:, e % 2], tsw[:, e % 2]
                    dve.wait_ge(sem("qk_swap"), it + 1)
                    then(dve.tensor_tensor(x, x, rope[:, 0], ALU.mult))
                    then(dve.tensor_tensor(w, w, rope[:, 1], ALU.mult))
                    then(dve.tensor_tensor(x, x, w, ALU.add))
                    dve.wait_ge(sem("qk_std"), it + 1)
                    then(dve.reciprocal(trs[:, :], tstd[:, :]))
                    dst = q[:, e] if e < 8 else k[:, e - 8]
                    dve.tensor_tensor(dst, x, trs[:, :], ALU.mult).then_inc(sem("qk_done"), 1)
                for e in range(5):
                    x, w = tqg[:, e % 2], tsw[:, e % 2]
                    dve.wait_ge(sem("qi_swap"), l * 5 + e + 1)
                    then(dve.tensor_tensor(x, x, rope[:, 2], ALU.mult))
                    then(dve.tensor_tensor(w, w, rope[:, 3], ALU.mult))
                    dst = qi[:, e] if e < 4 else ki[:, :]
                    dve.tensor_tensor(dst, x, w, ALU.add).then_inc(sem("qi_done"), 1)

            def index(l):
                dve.wait_ge(sem("wi_copied"), l + 1)
                for i in range(NQT):
                    W = META + P * (i + 1)
                    sc = mask[:, i, 0:W]
                    for hh in range(IXH):
                        it = (l * NQT + i) * IXH + hh
                        r, w = tsq[:, hh % 2, 0:W], wi[:, i, hh:hh + 1]
                        dve.wait_ge(sem("ix_relu"), it + 1)
                        if hh == 0:
                            dve.tensor_scalar(sc, r, w, None, ALU.mult).then_inc(sem("ix_acc"), 1)
                        else:
                            dve.wait_ge(sem("ix_acc"), it)
                            dve.scalar_tensor_tensor(sc, r, w, sc, ALU.mult, ALU.add).then_inc(sem("ix_acc"), 1)
                dve.wait_ge(sem("ix_acc"), (l + 1) * NQT * IXH)

            def choose(l, n):
                for i in range(NQT):
                    W = META + P * (i + 1)
                    sc = mask[:, i, 0:W]
                    if n == 0:
                        then(dve.memset(mask[0:CHUNK, i, W - CHUNK:W], BARRED))
                    for _ in range(TOPK // 8 // KD):
                        then(dve.max(top8[:, :], sc))
                        then(dve.match_replace(sc, top8[:, :], sc, CHOSEN))
                    if n == KD - 1:
                        then(dve.tensor_scalar(sc, sc, CHOSEN, NEG, ALU.not_equal, ALU.mult))
                        then(dve.memset(mask[0:CHUNK, i, W - CHUNK:W], NEG))

            def rnn(l):
                dve.wait_ge(sem("ix_relu"), (l + 1) * NQT * IXH)
                dve.memset(rx[:, 0:CONV - 1], 0.0).then_inc(sem("rnn_pad"), 1)
                dve.wait_ge(sem("rnn_pad"), l + 1)
                ph = AT[f"rnn{l}"]

                def taps(n):
                    it = l * 8 + n
                    dve.wait_ge(evac[ph.slot(2 * n)], ph.nth(2 * n) + 1)
                    if n:
                        dve.wait_ge(sem("rnn_iu"), it)
                        dve.wait_ge(sem("rnn_gates"), it)
                    for j in range(CONV):
                        t = CONV - 1 - j
                        w = col("cw", l, t * 8 + n)
                        if j == 0:
                            dve.tensor_scalar(ru[:, :], rx[:, t:t + T1], w, col("cb", l, n), ALU.mult, ALU.add)\
                               .then_inc(sem("rnn_conv"), 1)
                        else:
                            dve.wait_ge(sem("rnn_conv"), 4 * it + j)
                            dve.scalar_tensor_tensor(ru[:, :], rx[:, t:t + T1], w, ru[:, :], ALU.mult, ALU.add)\
                               .then_inc(sem("rnn_conv"), 1)

                def rest(n):
                    it = l * 8 + n
                    dve.wait_ge(sem("rnn_i"), it + 1)
                    dve.scalar_tensor_tensor(ri[:, :], ri[:, :], 1.0, ru[:, :], ALU.add, ALU.mult).then_inc(sem("rnn_iu"), 1)
                    dve.wait_ge(sem("rnn_t"), it + 1)
                    dve.tensor_scalar(rb[:, :], rt[:, :], 1.0, None, ALU.add).then_inc(sem("rnn_m"), 1)
                    dve.wait_ge(sem("rnn_m"), 3 * it + 1)
                    dve.reciprocal(rb[:, :], rb[:, :]).then_inc(sem("rnn_m"), 1)
                    dve.wait_ge(sem("rnn_m"), 3 * it + 2)
                    dve.tensor_tensor(rb[:, :], rb[:, :], rt[:, :], ALU.mult).then_inc(sem("rnn_m"), 1)
                    if n < 7:
                        taps(n + 1)
                    dve.wait_ge(sem("rnn_sqrt"), it + 1)
                    dve.wait_ge(sem("rnn_iu"), it + 1)
                    dve.tensor_tensor(rb[:, :], rb[:, :], ri[:, :], ALU.mult).then_inc(sem("rnn_b"), 1)
                    dve.wait_ge(sem("rnn_b"), it + 1)
                    dve.wait_ge(sem("rnn_a"), it + 1)
                    dve.tensor_tensor_scan(rh[:, :], ra[:, :], rb[:, :], 0.0, ALU.mult, ALU.add).then_inc(sem("rnn_scan"), 1)
                    dve.wait_ge(sem("rnn_scan"), it + 1)
                    dve.wait_ge(evac[ph.slot(2 * n + 1)], ph.nth(2 * n + 1) + 1)
                    dve.tensor_tensor(rh[:, :], rh[:, :], rg[:, :], ALU.mult).then_inc(sem("rnn_out"), 1)
                    dve.wait_ge(sem("br_hi"), (l * 4) * KD + n + 1)
                    dve.tensor_tensor(blo[:, n], rh[:, :], bhi[:, n].bitcast(F32), ALU.subtract).then_inc(sem("br_lo"), 1)

                taps(0)
                for n in range(8):
                    rest(n)

            def merge(l, name, inst):
                ph = AT[f"mg_{name}{l}"]
                with dve.Fori(0, KD) as m:
                    block_done(m * 2 + (ph.block(1) + 1))
                    dve.wait_ge(evac[ph.slot(0)], m + (ph.nth(0) + 1))
                    a, g = accv(ph.slot(1), T1), halves(sg[:, :], T1)
                    mg = merged[:, bass.ds(m, 1), :]
                    if inst == 0:
                        dve.tensor_tensor(mg.rearrange("p a (b c) -> p (a b) c", b=2), a, g, ALU.mult).then_inc(evac[ph.slot(1)], 1)
                    else:
                        dve.wait_ge(sem("mg_add"), m + ((2 * l + inst - 1) * KD + 1))
                        dve.tensor_tensor(halves(mt[:, :], T1), a, g, ALU.mult).then_inc(evac[ph.slot(1)], 1)
                        dve.wait_ge(evac[ph.slot(1)], m + (ph.nth(1) + 1))
                        dve.tensor_tensor(mg, mg, mt[:, :].unsqueeze(1), ALU.add).then_inc(sem("mg_add"), 1)

            def conv_inputs(l):
                ph = AT[f"conv{l}"]
                for n in range(KD):
                    block_done(ph.block(2 * n + 1) + 1)
                    dve.wait_ge(evac[0], ph.nth(2 * n) + 1)
                    dve.tensor_tensor(halves(cu[:, n], T1), accv(1, T1), halves(csg[:, :], T1), ALU.mult)\
                       .then_inc(evac[1], 1)
                    choose(l, n)
                dve.sem_inc(sem("mask_done"), 1)

            def conv_taps(l):
                then(dve.memset(cx[:, 0:DW - 1], 0.0))
                for n in range(KD):
                    if n:
                        dve.wait_ge(sem("cv_conv"), (l * 8 + n) * DW)
                    then(dve.tensor_copy(cx[:, DW - 1:], cu[:, n]))
                    for j in range(DW):
                        t = DW - 1 - j
                        w = col("dw", l, t * 8 + n)
                        c = (l * 8 + n) * DW + j
                        if j == 0:
                            dve.tensor_scalar(cu[:, n], cx[:, t:t + T1], w, col("db", l, n), ALU.mult, ALU.add)\
                               .then_inc(sem("cv_conv"), 1)
                        else:
                            dve.wait_ge(sem("cv_conv"), c)
                            dve.scalar_tensor_tensor(cu[:, n], cx[:, t:t + T1], w, cu[:, n], ALU.mult, ALU.add)\
                               .then_inc(sem("cv_conv"), 1)
                        yield

            def merged_tile(l, ph, m, inst):
                block_done(ph.block(1) + 2 * m + 1)
                dve.wait_ge(evac[ph.slot(0)], ph.nth(0) + m + 1)
                dve.wait_ge(sem("mg_add"), (2 * l + inst - 1) * KD + m + 1)
                dve.tensor_tensor(halves(mt[:, :], T1), accv(ph.slot(1), T1), halves(sg[:, :], T1), ALU.mult)\
                   .then_inc(evac[ph.slot(1)], 1)
                dve.wait_ge(evac[ph.slot(1)], ph.nth(1) + m + 1)
                dve.tensor_tensor(merged[:, m], merged[:, m], mt[:, :], ALU.add).then_inc(sem("mg_add"), 1)

            def mg_att(l, taps):
                ph = AT[f"mg_att{l}"]
                for n in range(KD):
                    dve.wait_ge(sem("br_hi"), (l * 4 + 1) * KD + n + 1)
                    dve.tensor_tensor(blo[:, n], q[:, n], bhi[:, n].bitcast(F32), ALU.subtract).then_inc(sem("br_lo"), 1)
                for m in range(LN_AFTER):
                    merged_tile(l, ph, m, 1)
                    for _ in range(TAPS_MERGE):
                        next(taps, None)
                for _ in taps:
                    pass
                dve.wait_ge(sem("cv_mean_read"), l + 1)
                for n in range(KD):
                    dve.tensor_tensor(cu[:, n], cu[:, n], cstat[:, 0], ALU.subtract).then_inc(sem("cv_centred"), 1)
                merged_tile(l, ph, LN_AFTER, 1)
                dve.wait_ge(sem("cv_std"), l + 1)
                then(dve.reciprocal(cstat[:, 2], cstat[:, 1]))
                for n in range(KD):
                    dve.tensor_tensor(cu[:, n], cu[:, n], cstat[:, 2], ALU.mult).then_inc(sem("cv_scaled"), 1)
                for m in range(LN_AFTER + 1, KD):
                    merged_tile(l, ph, m, 1)
                for n in range(KD):
                    dve.wait_ge(sem("br_hi"), (l * 4 + 2) * KD + n + 1)
                    dve.tensor_tensor(blo[:, n], cu[:, n], bhi[:, n].bitcast(F32), ALU.subtract).then_inc(sem("br_lo"), 1)

            def mix(l, taps):
                mg = AT[f"mg_rnn{l}"]
                items = [(hh, i) for hh in range(HEADS) for i in range(NQT + 1)]
                n0 = l * len(items)

                def score(j):
                    hh, i = items[j]
                    r, W = (P, META + (i + 1) * P) if i < NQT else (META, META)
                    b = j % 3
                    dve.wait_ge(sem("at_s"), n0 + j + 1)
                    if j >= 3:
                        dve.wait_ge(sem("at_turned"), n0 + j - 2)
                    src = aux[0][0:r].rearrange("p a b -> p (a b)")[:, 0:W]
                    add = mask[0:r, i, 0:W] if i < NQT else zeros[0:r, 0:W]
                    dve.tensor_tensor_reduce(sm[0:r, b, 0:W], src, add, float(HD) ** -0.5, CHOSEN, ALU.add, ALU.max,
                                             mx[0:r, b:b + 1]).then_inc(sem("at_scored"), 1)
                    dve.wait_ge(sem("at_scored"), n0 + j + 1)
                    dve.tensor_scalar(nmx[0:r, b:b + 1], mx[0:r, b:b + 1], -1.0, None, ALU.mult).then_inc(sem("at_max"), 1)

                def share(j):
                    hh, i = items[j]
                    r, W = (P, META + (i + 1) * P) if i < NQT else (META, META)
                    b = j % 3
                    dve.wait_ge(sem("at_exp"), n0 + j + 1)
                    then(dve.reciprocal(rrs[0:r, b:b + 1], rsum[0:r, b:b + 1]))
                    dve.tensor_scalar(sm[0:r, b, 0:W], sm[0:r, b, 0:W], rrs[0:r, b:b + 1], None, ALU.mult)\
                       .then_inc(sem("at_p"), 1)

                score(0)
                score(1)
                for j in range(len(items)):
                    share(j)
                    if j + 2 < len(items):
                        score(j + 2)
                    for _ in range(TAPS_ITEM):
                        next(taps, None)
                    if items[j][1] == NQT:
                        m = items[j][0]
                        block_done(mg.block(2 * m + 1) + 1)
                        then(dve.tensor_scalar(sg[:, :], sg[:, :], 0.5, 0.5, ALU.mult, ALU.add))
                        dve.tensor_tensor(halves(merged[:, m], T1), accv(0, T1), halves(sg[:, :], T1), ALU.mult)\
                           .then_inc(evac[0], 1)

            def neighbours():
                dve.wait_ge(sem("na_loaded"), 16 * 17)
                for hh in range(HEADS):
                    m = dve.tensor_tensor(natab[:, hh], natab[:, hh], namask[:, :].unsqueeze(1).broadcast_to([P, NAR, GW]),
                                          ALU.add)
                m.then_inc(sem("na_table_masked"), 1)
                dve.wait_ge(sem("na_table_masked"), 1)
                items = [(hh, i) for hh in range(HEADS) for i in range(NQT)]

                def score(j):
                    hh, i = items[j]
                    b = j % 2
                    dve.wait_ge(sem("na_s"), j + 1)
                    if j >= 2:
                        dve.wait_ge(sem("na_turned"), j - 1)
                    add = natab[:, hh, 6 - 2 * i:14 - 2 * i].rearrange("p a b -> p (a b)")
                    dve.tensor_tensor_reduce(sm2[:, b], aux[0][:, 0, :], add, 1.0, CHOSEN, ALU.add, ALU.max,
                                             sc2[:, 0, b:b + 1]).then_inc(sem("na_scored"), 1)
                    dve.wait_ge(sem("na_scored"), j + 1)
                    dve.tensor_scalar(sc2[:, 1, b:b + 1], sc2[:, 0, b:b + 1], -1.0, None, ALU.mult).then_inc(sem("na_max"), 1)

                score(0)
                for j in range(len(items)):
                    hh, i = items[j]
                    b = j % 2
                    if j + 1 < len(items):
                        score(j + 1)
                    dve.wait_ge(sem("na_exp"), j + 1)
                    then(dve.reciprocal(sc2[:, 3, b:b + 1], sc2[:, 2, b:b + 1]))
                    dve.tensor_scalar(sm2[:, b], sm2[:, b], sc2[:, 3, b:b + 1], None, ALU.mult).then_inc(sem("na_p"), 1)
                    if hh % 2 and i == NQT - 1:
                        dve.wait_ge(sem("attn2_hi"), hh // 2 + 1)
                        dve.tensor_tensor(attn_lo[:, hh // 2], ot2[:, :], attn_hi[:, hh // 2].bitcast(F32), ALU.subtract)\
                           .then_inc(sem("attn2_lo"), 1)

            C1, C2, C3 = two_pi_parts()

            def reduce_angle(out, kk, x):
                then(dve.tensor_scalar(kk, x, float(1.0 / TWO_PI), MAGIC, ALU.mult, ALU.add))
                then(dve.tensor_scalar(kk, kk, MAGIC, None, ALU.subtract))
                then(dve.scalar_tensor_tensor(out, kk, -C1, x, ALU.mult, ALU.add))
                then(dve.scalar_tensor_tensor(out, kk, -C2, out, ALU.mult, ALU.add))
                then(dve.scalar_tensor_tensor(out, kk, -C3, out, ALU.mult, ALU.add))
                then(dve.tensor_scalar(out, out, PI_SAFE, -PI_SAFE, ALU.min, ALU.max))

            def ssm():
                w = lambda j: spw[:, j]
                tt = lambda o_, a, b_, op: then(dve.tensor_tensor(o_, a, b_, op))
                dve.wait_ge(sem("ss_dt"), 1)
                lre, lim = smp[:, 1], smp[:, 2]
                then(dve.tensor_scalar(lre, lre, -1e-4, None, ALU.min))
                tt(w(1), lre, w(0), ALU.mult)
                tt(w(3), lim, w(0), ALU.mult)
                reduce_angle(w(2), w(8), w(3))
                dve.sem_inc(sem("ss_reduced"), 1)
                tt(w(8), lre, lre, ALU.mult)
                tt(w(9), lim, lim, ALU.mult)
                tt(w(8), w(8), w(9), ALU.add)
                then(dve.reciprocal(w(8), w(8)))
                dve.wait_ge(sem("ss_waves"), 1)
                then(dve.tensor_scalar(w(9), w(6), -1.0, 1.0, ALU.mult, ALU.add))
                then(dve.reciprocal(w(9), w(9)))
                then(dve.scalar_tensor_tensor(w(9), w(6), 2.0, w(9), ALU.mult, ALU.mult))
                then(dve.scalar_tensor_tensor(w(10), w(5), -2.0, w(5), ALU.mult, ALU.mult))
                tt(w(11), w(9), w(10), ALU.mult)
                tt(w(11), w(11), w(9), ALU.add)
                tt(w(11), w(11), w(10), ALU.add)
                then(dve.scalar_tensor_tensor(w(12), w(9), 1.0, w(4), ALU.add, ALU.mult))
                tt(w(13), w(11), lre, ALU.mult)
                tt(w(14), w(12), lim, ALU.mult)
                tt(w(13), w(13), w(14), ALU.add)
                tt(w(13), w(13), w(8), ALU.mult)
                tt(w(14), w(12), lre, ALU.mult)
                tt(w(15), w(11), lim, ALU.mult)
                tt(w(14), w(14), w(15), ALU.subtract)
                tt(w(14), w(14), w(8), ALU.mult)
                then(dve.tensor_scalar(w(11), w(11), 1.0, None, ALU.add))
                then(dve.memset(w(16), 1.0))
                then(dve.memset(w(17), 0.0))
                for p in range(5):
                    for src, c_, b_ in ((w(16), lc_r, lb_r), (w(17), lc_i, lb_i)):
                        s4 = src.rearrange("p (r d u) -> p r d u", r=4, d=2)
                        c4 = c_[:, :, :].rearrange("p (r d u) k -> p r d u k", r=4, d=2)
                        b4 = b_[:, :, :].rearrange("p (r d u) k -> p r d u k", r=4, d=2)
                        then(dve.tensor_copy(c4[:, :, 0, :, p], s4[:, :, 0, :]))
                        then(dve.tensor_copy(c4[:, :, 1, :, 4 - p], s4[:, :, 1, :]))
                        if p < 4:
                            then(dve.tensor_copy(b4[:, :, 0, :, 3 - p], s4[:, :, 0, :]))
                            then(dve.tensor_copy(b4[:, :, 1, :, p], s4[:, :, 1, :]))
                    if p < 4:
                        tt(w(15), w(16), w(12), ALU.mult)
                        tt(w(16), w(16), w(11), ALU.mult)
                        tt(w(18), w(17), w(12), ALU.mult)
                        tt(w(16), w(16), w(18), ALU.subtract)
                        tt(w(17), w(17), w(11), ALU.mult)
                        tt(w(17), w(17), w(15), ALU.add)
                then(dve.tensor_scalar(w(3), w(2), float(SC), None, ALU.mult))
                reduce_angle(w(2), w(0), w(3))

                for r in range(4):
                    u8 = slice(8 * r, 8 * r + 8)
                    f = [w(13)[:, u8].unsqueeze(2).broadcast_to([P, 8, 32]), w(14)[:, u8].unsqueeze(2).broadcast_to([P, 8, 32])]
                    b_, c_ = [sbc[:, 0, u8], sbc[:, 1, u8]], [sbc[:, 2, u8], sbc[:, 3, u8]]
                    t3 = w8[:, :, 0:32]
                    if r:
                        dve.wait_ge(sem("ss_rep"), 2 * r)
                        dve.wait_ge(sem("ss_out"), r)
                    tt(bb[:, 0], f[0], b_[0], ALU.mult)
                    tt(t3, f[1], b_[1], ALU.mult)
                    tt(bb[:, 0], bb[:, 0], t3, ALU.subtract)
                    tt(bb[:, 1], f[0], b_[1], ALU.mult)
                    tt(t3, f[1], b_[0], ALU.mult)
                    dve.tensor_tensor(bb[:, 1], bb[:, 1], t3, ALU.add).then_inc(sem("ss_bb"), 1)
                    dve.wait_ge(sem("ss_bb"), r + 1)
                    sh = [P, 8, 5, 32]
                    L = [x[:, u8].unsqueeze(3).broadcast_to(sh) for x in (lc_r, lc_i)]
                    C = [x.unsqueeze(2).broadcast_to(sh) for x in c_]
                    t5 = cs_[:, :, :, :].rearrange("p a b c -> p (a b c)")[:, 0:1280].rearrange("p (a b c) -> p a b c", a=8, b=5)
                    cmul(dve, then, cp_[:, 0], cp_[:, 1], C, L, t5, minus=True, last=sem("ss_cpow"))
                    t4 = cs_[:, :, :, :].rearrange("p a b c -> p (a b c)")[:, 0:1024].rearrange("p (a b c) -> p a b c", a=8, b=4)
                    sh = [P, 8, 4, 32]
                    L = [x[:, u8].unsqueeze(3).broadcast_to(sh) for x in (lb_r, lb_i)]
                    B = [bb[:, z].unsqueeze(2).broadcast_to(sh) for z in range(2)]
                    cmul(dve, then, ap_[:, 0], ap_[:, 1], B, L, t4, minus=False, last=sem("ss_bpow"), twice=True)
                    ang = w(2)[:, u8].unsqueeze(2).broadcast_to([P, 8, NC])
                    tt(m4[:, :, :], ang, chk[:, :].unsqueeze(1).broadcast_to([P, 8, NC]), ALU.mult)
                    reduce_angle(w8[:, :, :], cs_[:, 0], m4[:, :, :])
                    dve.sem_inc(sem("ss_angle"), 1)
                    then(dve.tensor_copy(m4[:, :, :], w(7)[:, u8].unsqueeze(2).broadcast_to([P, 8, NC])))
                    then(dve.memset(m4[:, :, 0:1], 0.0))
                    then(dve.memset(tm_[:, :, :], 0.0))
                    dve.sem_inc(sem("ss_t_zero"), 1)
                    dve.wait_ge(sem("ss_t_forward"), r + 1)
                    lag = aux[0][:, 1, :].rearrange("p (u c) -> p u c", u=4)
                    for j in range(SC):
                        rows = slice(32 * j, 32 * j + 32)
                        m = dve.tensor_tensor(tm_[rows, :, 0:32 * (j + 1)], tm_[rows, :, 0:32 * (j + 1)],
                                              lag[rows, :, (3 - j) * 32:P], ALU.add)
                    m.then_inc(sem("ss_t"), 1)
                    dve.wait_ge(sem("ss_sines"), r + 1)
                    co, si = cs_[:, 0], cs_[:, 1]
                    tt(co, co, co, ALU.mult)
                    then(dve.tensor_scalar(co, co, -2.0, 1.0, ALU.mult, ALU.add))
                    dve.wait_ge(sem("ss_s"), r + 1)
                    sr = aux[0][:, :, :].rearrange("p a (b c) -> p (a b) c", c=NC)
                    si_ = aux[1][:, :, :].rearrange("p a (b c) -> p (a b) c", c=NC)
                    zr, zi, t = zz[:, 0], zz[:, 1], w8[:, :, :]
                    tt(zr, sr, co, ALU.mult)
                    tt(t, si_, si, ALU.mult)
                    tt(zr, zr, t, ALU.add)
                    tt(zi, si_, co, ALU.mult)
                    tt(t, sr, si, ALU.mult)
                    tt(zi, zi, t, ALU.subtract)
                    flat = lambda x: x.rearrange("p a b -> p (a b)")
                    for z in (zr, zi):
                        then(dve.tensor_tensor_scan(flat(z), flat(m4[:, :, :]), flat(z), 0.0, ALU.mult, ALU.add))
                    if r == 0:
                        then(dve.memset(st_[:, :, 0:4, 0:1], 0.0))
                        then(dve.memset(st_[:, :, 4:8, NC:NC + 1], 0.0))
                    for z, (a, b2, op) in enumerate(((zr, zi, ALU.subtract), (zi, zr, ALU.add))):
                        tt(t, a, co, ALU.mult)
                        tt(m4[:, :, :], b2, si, ALU.mult)
                        dve.tensor_tensor(st_[:, z, 0:4, 1:NC + 1], t[:, 0:4], m4[:, 0:4], op).then_inc(sem("ss_x"), 1)
                        dve.tensor_tensor(st_[:, z, 4:8, NC - 1::-1], t[:, 4:8], m4[:, 4:8], op).then_inc(sem("ss_x"), 1)
                        dve.wait_ge(sem("ss_x"), 4 * r + 2 * z + 2)
                for r in range(4):
                    dve.wait_ge(sem("ss_y"), 16 * (r + 1))
                    dve.scalar_tensor_tensor(yv[:, r], uin[:, r], col("dskip", None, r), yv[:, r], ALU.mult, ALU.add)\
                       .then_inc(sem("ss_skip"), 1)
                for r in range(4):
                    dve.wait_ge(sem("y_hi"), r + 1)
                    dve.tensor_tensor(zlo[:, r], yv[:, r], zhi[:, r].bitcast(F32), ALU.subtract).then_inc(sem("y_lo"), 1)
                ph = AT["glu2"]
                for i in range(4):
                    dve.wait_ge(evac[ph.slot(i)], ph.nth(i) + 1)
                    dve.wait_ge(sem("y_lo"), 4)
                    dve.tensor_tensor(yv[:, i], yv[:, i], uin[:, i], ALU.mult).then_inc(sem("z_done"), 1)
                for i in range(4):
                    dve.wait_ge(sem("z_hi"), i + 1)
                    dve.tensor_tensor(zlo[:, i], yv[:, i], zhi[:, i].bitcast(F32), ALU.subtract).then_inc(sem("z_lo"), 1)

            then(dve.memset(ones[:, :], 1.0))
            dve.sem_inc(sem("consts_set"), 1)
            then(dve.memset(zeros[:, :], 0.0))
            for name in ("mg_add", "m2_add", "ple_added", "ff_lo"):
                dve.sem_inc(sem(name), 1)
            dve.sem_inc(sem("consts_set"), 2)
            dve.wait_ge(sem("par_loaded"), 16)
            pp = lambda j: prep[:, j, :]
            for l in range(DEPTH):
                then(dve.tensor_copy(prep[:, 2, 8 * l:8 * l + 8], col("lam", l, 0, 8)))
            then(dve.tensor_scalar(pp(3), pp(2), -1.0, None, ALU.mult))
            dve.tensor_tensor(pp(0), pp(2), pp(3), ALU.max).then_inc(sem("lam_abs"), 1)
            dve.wait_ge(sem("lam_exp"), 1)
            then(dve.tensor_scalar(pp(4), pp(1), 2.0, None, ALU.add))
            then(dve.reciprocal(pp(4), pp(4)))
            then(dve.tensor_tensor(pp(4), pp(4), pp(1), ALU.mult))
            then(dve.tensor_tensor(pp(5), pp(4), pp(4), ALU.mult))
            then(dve.tensor_scalar(pp(6), pp(5), 1.0 / 17, 1.0 / 15, ALU.mult, ALU.add))
            for d in (13, 11, 9, 7, 5, 3, 1):
                then(dve.tensor_tensor(pp(6), pp(6), pp(5), ALU.mult))
                then(dve.tensor_scalar(pp(6), pp(6), 1.0 / d, None, ALU.add))
            then(dve.tensor_tensor(pp(6), pp(6), pp(4), ALU.mult))
            then(dve.tensor_scalar(pp(3), pp(3), 0.0, None, ALU.max))
            then(dve.scalar_tensor_tensor(pp(6), pp(6), 2.0, pp(3), ALU.mult, ALU.add))
            for l in range(DEPTH):
                for g, name in enumerate(("ba", "bx")):
                    then(dve.tensor_scalar(hba[:, l, g], col(name, l, 0, 8), 0.5, None, ALU.mult))
            then(dve.tensor_scalar(spc[:, :, :].rearrange("p a b -> p (a b)"), pp(6), 4.0, None, ALU.mult))
            dve.tensor_scalar(nspc[:, :, :].rearrange("p a b -> p (a b)"), pp(6), -4.0, None, ALU.mult)\
               .then_inc(sem("spc_done"), 1)
            for l in range(DEPTH):
                norm(2 * l)
                proj(l)
                index(l)
                conv_inputs(l)
                rnn(l)
                taps = conv_taps(l)
                mix(l, taps)
                mg_att(l, taps)
                merge(l, "conv", 2)
                for n in range(KD):
                    dve.wait_ge(sem("br_hi"), (l * 4 + 3) * KD + n + 1)
                    dve.tensor_tensor(blo[:, n], merged[:, n], bhi[:, n].bitcast(F32), ALU.subtract).then_inc(sem("br_lo"), 1)
                add_to_h(AT[f"out{l}"], T1, 2 * l + 1)
                ffn(2 * l + 1, f"up{l}", f"down{l}", T1, 1.0)
            ffn(4, "up2", "down2", SEQ, 0.5)
            norm(5)
            neighbours()
            ssm()
            ph = AT["mg2"]
            with dve.Fori(0, KD) as m:
                for z in range(2):
                    block_done(m * 4 + (ph.block(2 * z + 1) + 1))
                    dve.wait_ge(evac[ph.slot(0)], m * 2 + (ph.nth(0) + z + 1))
                    a, g = accv(ph.slot(1), S), halves(sg2[:, :], S)
                    mg = merged2[:, bass.ds(m, 1), :]
                    if z == 0:
                        dve.tensor_tensor(mg.rearrange("p a (b c) -> p (a b) c", b=2), a, g, ALU.mult).then_inc(evac[ph.slot(1)], 1)
                    else:
                        dve.wait_ge(sem("m2_add"), m + 1)
                        dve.tensor_tensor(halves(mt2[:, :], S), a, g, ALU.mult).then_inc(evac[ph.slot(1)], 1)
                        dve.wait_ge(evac[ph.slot(1)], m * 2 + (ph.nth(1) + 2))
                        dve.tensor_tensor(mg, mg, mt2[:, :].unsqueeze(1), ALU.add).then_inc(sem("m2_add"), 1)
            for n in range(KD):
                dve.wait_ge(sem("m2_hi"), n + 1)
                dve.tensor_tensor(mlo[:, n], merged2[:, n], mhi[:, n].bitcast(F32), ALU.subtract).then_inc(sem("m2_lo"), 1)
            add_to_h(AT["out2"], SEQ, 6)
            ffn(6, "up3", "down3", SEQ, 0.5)
            norm(7)
            dve.wait_ge(sem("p_hi"), 1)
            for n in range(2):
                dve.tensor_tensor(plo[:, n], pin[:, n], phi[:, n].bitcast(F32), ALU.subtract).then_inc(sem("p_lo"), 1)
            ph = AT["ple2"]
            dve.wait_ge(sem("norm_summed"), 8)
            dve.memset(facc[:, :], 0.0).then_inc(sem("norm_clear"), 1)
            with dve.Fori(0, KD) as m:
                block_done(m * 2 + (ph.block(1) + 1))
                dve.wait_ge(evac[ph.slot(0)], m + (ph.nth(0) + 1))
                dve.wait_ge(sem("ple_added"), m + 1)
                dve.tensor_tensor(halves(pmt[:, :], S), accv(ph.slot(1), S), halves(psg[:, :], S), ALU.mult)\
                   .then_inc(evac[ph.slot(1)], 1)
                dve.wait_ge(evac[ph.slot(1)], m + (ph.nth(1) + 1))
                hv = h[:, bass.ds(m, 1), T1 - S:T1]
                dve.tensor_tensor(hv, hv, pmt[:, :].unsqueeze(1), ALU.add).then_inc(sem("ple_added"), 1)
                dve.wait_ge(sem("norm_clear"), 8)
                dve.wait_ge(sem("norm_square"), m + (8 * KD + 1))
                dve.wait_ge(sem("norm_added"), m + 8 * KD)
                dve.tensor_tensor(facc[:, :], facc[:, :], fsq[:, 0], ALU.add).then_inc(sem("norm_added"), 1)
            norm(8)


GW = 64
ITEMS = HEADS * (NQT + 1)
MERGE_PARTS = [(0, 0, 3), (0, 3, 6), (0, 6, 8), (1, 0, 4), (1, 4, 8)]
LN_AFTER = 6
TAPS_ITEM = 4
TAPS_MERGE = 15
FFI = {"up0": 0, "up1": 1, "up2": 2, "up3": 3}


def cmul(dve, then, out_r, out_i, a, b, t, minus, last, twice=False):
    each = lambda o, x, y, op: then(dve.tensor_tensor(o, x, y, op))
    each(out_r, a[0], b[0], ALU.mult)
    each(t, a[1], b[1], ALU.mult)
    then(dve.tensor_tensor(out_r, out_r, t, ALU.subtract))
    each(out_i, a[0], b[1], ALU.mult)
    each(t, a[1], b[0], ALU.mult)
    then(dve.tensor_tensor(out_i, out_i, t, ALU.add))
    if minus:
        then(dve.tensor_scalar(out_i, out_i, -1.0, None, ALU.mult))
    dve.sem_inc(last, 4 if twice else 2)


def blocks_of(w):
    K, M = w.shape
    nk, per = K // P, -(-K // (P * BLK))
    t = w.reshape(nk, P, M // P, P).transpose(2, 1, 0, 3)
    out = np.zeros((M // P, P, per * BLK, P), w.dtype)
    out[:, :, :nk] = t
    return out.reshape(M // P, P, per, BLK * P).transpose(0, 2, 1, 3).reshape(M // P * per, P, BLK * P)


def pairs(*ws):
    b = [blocks_of(w) for w in ws]
    return np.stack(b, 1).reshape(-1, P, BLK * P)


def tiles(x, n):
    return x.reshape(n, P).T


def rope_consts(n, dim):
    inv = (np.float32(10000.0) ** (-np.arange(0, dim, 2, dtype=np.float32) / np.float32(dim))).astype(np.float32)
    ang = (np.arange(n, dtype=np.float32)[:, None] * inv[None, :]).astype(np.float32)
    c, s = np.cos(ang).T.astype(np.float32), np.sin(ang).T.astype(np.float32)
    reps = P // dim
    return np.concatenate([c, c] * reps), np.concatenate([-s, s] * reps)


def kernel(**inputs):
    import concourse.bacc as _bacc
    from concourse.bass_utils import run_bass_kernel_spmd as _run

    I = {n: np.asarray(a) for n, a in inputs.items()}
    ws = []
    for l in range(DEPTH):
        w = I["w_in"][l]
        edge = np.cumsum([0, 1024, 256, 256, 512, 64, 8, 1024, 1024, 2048, 3072])
        q, k, v, qi, ki, wi, xr, yg, cv, gt = (w[:, a:b] for a, b in zip(edge[:-1], edge[1:]))
        last = np.zeros((D, P), w.dtype)
        last[:, 0:64], last[:, 64:72] = ki, wi
        ws += [blocks_of(q), blocks_of(k), blocks_of(v), blocks_of(qi), blocks_of(last), pairs(cv[:, D:], cv[:, 0:D]),
               pairs(xr, yg), pairs(gt[:, D:2 * D], I["w_o_rnn"][l]), pairs(gt[:, 0:D], I["w_o_attn"][l]),
               pairs(gt[:, 2 * D:], I["w_o_conv"][l]), blocks_of(I["w_out"][l]),
               pairs(I["w_ffn_gate"][l], I["w_ffn_up"][l]), blocks_of(I["w_ffn_down"][l])]
    w = I["w_in_2"][0]
    ws += [pairs(I["ffn1_w_gate_2"][0], I["ffn1_w_up_2"][0]), blocks_of(I["ffn1_w_down_2"][0]), blocks_of(w[:, 0:1536]),
           blocks_of(w[:, 1536:2048]), blocks_of(I["ssm_glu_w_2"][0]),
           pairs(w[:, 2048:3072], I["w_attn_out_2"][0], w[:, 3072:4096], I["w_ssm_out_2"][0]), blocks_of(I["w_out_2"][0]),
           pairs(I["ffn2_w_gate_2"][0], I["ffn2_w_up_2"][0]), blocks_of(I["ffn2_w_down_2"][0]),
           pairs(I["ple_w_gate_2"][0], I["ple_w_proj_2"][0])]
    wpack = np.concatenate(ws)
    assert wpack.shape[0] == plan()[1]

    cols = []
    for l in range(DEPTH):
        cols += [tiles(I["mix_norm_g"][l], 8), tiles(I["q_norm_g"][l], 1), tiles(I["k_norm_g"][l], 1),
                 *[tiles(I["rnn_conv_w"][l, t], 8) for t in range(CONV)], tiles(I["rnn_conv_b"][l], 8),
                 tiles(I["rnn_ba"][l], 8), tiles(I["rnn_bx"][l], 8), tiles(I["rnn_lambda"][l], 8),
                 *[tiles(I["conv_dw_w"][l, t], 8) for t in range(DW)], tiles(I["conv_dw_b"][l], 8),
                 tiles(I["conv_ln_g"][l], 8), tiles(I["conv_ln_b"][l], 8), tiles(I["ffn_norm_g"][l], 8)]
    cols += [tiles(I["ffn1_norm_2"][0], 8), tiles(I["mix_norm_2"][0], 8), tiles(I["ffn2_norm_2"][0], 8),
             tiles(I["ple_norm_2"][0], 8), tiles(I["final_norm_2"], 8), tiles(I["ssm_d_2"][0], 4), tiles(I["ssm_glu_b_2"][0], 4)]
    par = np.ascontiguousarray(np.concatenate(cols, 1))
    assert par.shape[1] == columns()[1]

    hT = np.concatenate([I["meta"], I["x"][0]]).T.reshape(KD, P, T1).transpose(1, 0, 2)
    rope = np.stack(rope_consts(T1, HD) + rope_consts(T1, IXD)).astype(np.float32)
    gate = np.stack([I["rnn_wa"], I["rnn_wx"]], 1).transpose(0, 1, 3, 2, 4).reshape(DEPTH, 2, P, 8 * P)

    rpb = I["na_rpb_2"][0]
    padded = np.zeros((HEADS, 16, 127), rpb.dtype)
    padded[:, 1:16, 48:79] = rpb
    qc, kc = np.arange(GW)[:, None], np.arange(GW)[None, :]
    natab = np.zeros((2, HEADS, GW, NAR, GW), rpb.dtype)
    for half in range(2):
        for e in range(NAR):
            natab[half, :, :, e] = padded[:, e + 2 - half][:, kc - qc + 63]
    start = np.clip(np.arange(GW) - NAW // 2, 0, GW - NAW)[:, None]
    inside = (kc >= start) & (kc < start + NAW)
    namask = np.tile(np.where(inside, 0.0, NEG).astype(np.float32), (2, 1))

    def states(a):
        a = a.reshape(2, 4, 4, 2, 64, *a.shape[3:])
        a = np.moveaxis(a, [3, 4, 1, 0, 2], [0, 1, 2, 3, 4])
        return a.reshape(P, 32, *a.shape[5:])

    ssm = np.zeros((7, P, 1024), np.float32)
    ssm[0, :, 0:32] = states(np.repeat(I["ssm_log_dt_2"][0][:, :, None], 64, 2))
    ssm[1, :, 0:32] = states(I["ssm_lam_re_2"][0])
    ssm[2, :, 0:32] = states(I["ssm_lam_im_2"][0])
    for n, a in enumerate((I["ssm_b_re_2"][0], I["ssm_b_im_2"][0], I["ssm_c_re_2"][0].transpose(0, 1, 3, 2),
                           I["ssm_c_im_2"][0].transpose(0, 1, 3, 2))):
        a, full = states(a), ssm[3 + n].reshape(P, 32, 32)
        full[0:64, :, 0:16], full[64:, :, 16:] = a[0:64], a[64:]
    chunks = np.tile(np.arange(NC, dtype=np.float32), (P, 1))
    pT = np.ascontiguousarray(I["p_2"][0, 0].T.reshape(2, P, SEQ))

    arrays = {"w": wpack, "par": par, "h": np.ascontiguousarray(hT), "rope": rope, "gate": np.ascontiguousarray(gate),
              "natab": natab, "namask": namask, "ssm": ssm, "chunk": chunks, "p": pT, "ident": np.eye(P, dtype=np.float32)}
    nc = _bacc.Bacc("TRN2", target_bir_lowering=False, num_devices=1)
    args = [nc.dram_tensor(f"in_{n}", a.shape, mybir.dt.from_np(a.dtype), kind="ExternalInput").ap() for n, a in arrays.items()]
    out = nc.dram_tensor("out_0", (KD, P, SEQ), F32, kind="ExternalOutput").ap()
    build(nc, *args, out)
    r = _run(nc, [{f"in_{n}": a for n, a in arrays.items()}], core_ids=[0])
    y = r.results[0]["out_0"]
    return np.ascontiguousarray(y.reshape(D, SEQ).T)[None]
```

```python
from contextlib import ExitStack

import numpy as np

import concourse.bass as bass
from concourse import mybir

F32 = mybir.dt.float32
F32R = mybir.dt.float32r
ALU = mybir.AluOpType
ACT = mybir.ActivationFunctionType
AX = mybir.AxisListType

P = 128
D = 1024
KD = D // P
DEPTH = 2
META = 16
SEQ = 512
T1 = META + SEQ
CHUNK = 64
TOPK = 128
HEADS = 8
KV = 2
HD = 128
IXH = 8
IXD = 64
FF = 2816
KF = FF // P
CONV = 4
DW = 31
NQT = SEQ // P
EPS = 1e-6
NEG = -1.0e30
BARRED = -3.0e38
CHOSEN = -3.4e38
BLK = 8
RAW = 4
TWO_PI = 2.0 * np.pi
MAGIC = 12582912.0
PI_SAFE = 3.1415925
NAW = 16
NAR = 14
HD2 = 64
UNITS = 16
ROUND = 4
SC = 4
NC = SEQ // SC
GW = 64
ITEMS = HEADS * (NQT + 1)
MERGE_PARTS = [(0, 0, 3), (0, 3, 6), (0, 6, 8), (1, 0, 4), (1, 4, 8)]
NA_PARTS = [(0, 0, 4, 8), (0, 4, 8, 8), (1, 0, 2, 4), (1, 2, 4, 4)]
LN_AFTER = 6
TAPS_ITEM = 4
TAPS_MERGE = 15
FFI = {"up0": 0, "up1": 1, "up2": 2, "up3": 3}


def two_pi_parts():
    c1 = np.float32(6.28125)
    r = TWO_PI - float(c1)
    c2 = np.float32(np.round(r * 2.0 ** 21) / 2.0 ** 21)
    return float(c1), float(c2), float(np.float32(r - float(c2)))


def cuts(nk, per):
    return [(c * nk // per, (c + 1) * nk // per - c * nk // per) for c in range(per)]


class Phase:
    def __init__(self, block, used, tiles, per, only):
        self.b0, self.used, self.tiles, self.per, self.only = block, tuple(used), tiles, per, only

    def block(self, i):
        return self.b0 + i * self.per

    def slot(self, i):
        return i % 2 if self.only is None else self.only

    def nth(self, i):
        return self.used[self.slot(i)] + (i // 2 if self.only is None else i)


ATT_MERGE = [x for i in range(4) for x in ((f"att_gate{2 * i}", 1, 1, 0), (f"att_products{i}", 1, 1, 2),
                                          (f"att_gate{2 * i + 1}", 1, 1, 1))]
PLE = [("ple_products0", 1, 1, 2)] + [(f"ple_gate{i}", 1, 1, i % 2) for i in range(5)] + \
      [("ple_products1", 1, 1, 2)] + [(f"ple_gate{i}", 1, 1, i % 2) for i in range(5, 8)]
PHASES = []
for _l in range(DEPTH):
    PHASES += [(f"qk{_l}", 10, 1), (f"v{_l}", 2, 1), (f"qi{_l}", 5, 1), (f"conv{_l}", 16, 1), (f"rnn{_l}", 16, 1),
               (f"mg_rnn{_l}", 16, 1, 0), (f"att{_l}", 8, 0, 1), (f"mg_att{_l}", 16, 1), (f"mg_conv{_l}", 16, 1),
               (f"out{_l}", 8, 1), (f"up{_l}", 2 * KF, 1), (f"down{_l}", 8, 3)]
PHASES += [("up2", 2 * KF, 1), ("down2", 8, 3), ("sin2", 4, 1), ("qkv2", 12, 1), ("glu2", 4, 1), ("mg_ssm2", 16, 1, 0),
           ("att2", 4, 0, 1), *ATT_MERGE, ("out2", 8, 1), ("up3", 2 * KF, 1), ("down3", 8, 3), *PLE]


def plan():
    at, block, used = {}, 0, [0, 0, 0]
    for name, tiles, per, *only in PHASES:
        ph = at[name] = Phase(block, used, tiles, per, only[0] if only else None)
        block += tiles * per
        for i in range(tiles):
            used[ph.slot(i)] += 1
    return at, block


LAYER_COLS = [("mix_g", 8), ("q_g", 1), ("k_g", 1), ("cw", CONV * 8), ("cb", 8), ("ba", 8), ("bx", 8), ("lam", 8),
              ("dw", DW * 8), ("db", 8), ("ln_g", 8), ("ln_b", 8), ("ffn_g", 8)]
TAIL_COLS = [("ffn1_g", 8), ("mix2_g", 8), ("ffn2_g", 8), ("ple_g", 8), ("final_g", 8), ("dskip", 4), ("glu_b", 4)]


def columns():
    at, n = {}, 0
    for layer in range(DEPTH):
        for name, w in LAYER_COLS:
            at[(name, layer)] = n
            n += w
    for name, w in TAIL_COLS:
        at[name] = n
        n += w
    return at, n


def build(nc, A_w, A_par, A_h, A_rope, A_gate, A_natab, A_namask, A_ssm, A_chunk, A_p, A_ident, A_out):
    AT, NBLK = plan()
    COL, NPAR = columns()
    ROW = T1 * 4

    with ExitStack() as ctx:
        sems = {}

        def sem(name):
            if name not in sems:
                sems[name] = ctx.enter_context(nc.semaphore(name))
            return sems[name]

        BASE = 16512
        place = [BASE]

        def fixed(name, shape, dt=F32):
            t = nc.alloc_sbuf_tensor_at(name, shape, dt, offset=place[0])
            n = 4
            for s in shape[1:]:
                n *= s
            place[0] += (n + 31) // 32 * 32
            return t

        ident = fixed("ident", [P, P])
        ones = fixed("ones", [P, P])
        par = fixed("par", [P, NPAR])
        spc = fixed("spc", [P, DEPTH, 8])
        prep = fixed("prep", [P, 7, DEPTH * 8])
        nspc = fixed("nspc", [P, DEPTH, 8])
        hba = fixed("hba", [P, DEPTH, 2, 8])
        h = fixed("h", [P, KD, T1])
        nhi = fixed("nhi", [P, KD, T1], F32R)
        nlo = fixed("nlo", [P, KD, T1], F32R)
        raw = fixed("raw", [P, RAW, BLK * P])
        whi = fixed("whi", [P, 2, BLK * P], F32R)
        wlo = fixed("wlo", [P, 2, BLK * P], F32R)
        zeros = fixed("zeros", [P, 128])
        ARENA = place[0]
        END = 229344

        def at(name, shape, off, dt=F32):
            n = 4
            for s in shape[1:]:
                n *= s
            assert ARENA + off + n <= END, (name, ARENA + off + n - END)
            return nc.alloc_sbuf_tensor_at(name, shape, dt, offset=ARENA + off), off + (n + 31) // 32 * 32

        o = 0
        q, o = at("q", [P, HEADS, T1], o)
        k, o = at("k", [P, KV, T1], o)
        v, o = at("v", [P, 5, KV * HD], o)
        mask, o = at("mask", [P, NQT, T1], o)
        wi, o = at("wi", [P, NQT, IXH], o)
        merged, end_merged = at("merged", [P, KD, T1], o)
        vT, o1 = at("vT", [P, KV, T1], o)
        rnn_w, o1 = at("rnn_w", [P, 2, 8, P], o1)
        assert o1 <= end_merged
        bhi, o = at("bhi", [P, KD, T1], end_merged, F32R)
        blo, o = at("blo", [P, KD, T1], o, F32R)
        area1 = o
        qi, o = at("qi", [P, 4, T1], o)
        ki, o = at("ki", [P, T1], o)
        rope, area2 = at("rope", [P, 4, T1], o)
        cu, _ = at("cu", [P, KD, T1], area1)
        o = area2
        rx, o = at("rx", [P, T1 + CONV - 1], o)
        ru, o = at("ru", [P, T1], o)
        rr, o = at("rr", [P, T1], o)
        ri, o = at("ri", [P, T1], o)
        rt, o = at("rt", [P, T1], o)
        ra, o = at("ra", [P, T1], o)
        rb, o = at("rb", [P, T1], o)
        rh, o = at("rh", [P, T1], o)
        rg, o = at("rg", [P, T1], o)
        o = area2
        tsq, o = at("tsq", [P, 2, T1], o)
        tqg, o = at("tqg", [P, 2, T1], o)
        tsw, o = at("tsw", [P, 2, T1], o)
        tstd, o = at("tstd", [P, T1], o)
        trs, o = at("trs", [P, T1], o)
        wbuf, o = at("wbuf", [32, T1], o)
        top8, o = at("top8", [P, 8], o)
        csg, _ = at("csg", [P, T1], area2 + 6 * ROW)
        o = area2
        sm, o = at("sm", [P, 3, T1], o)
        csq, _ = at("csq", [P, 2, T1], o)
        pts, o = at("pts", [P, 5, P], o)
        cx, o = at("cx", [P, 2, T1 + DW - 1], o)
        sg, o = at("sg", [P, T1], o)
        mt, o = at("mt", [P, T1], o)
        mx, o = at("mx", [P, 4], o)
        nmx, o = at("nmx", [P, 4], o)
        rsum, o = at("rsum", [P, 4], o)
        rrs, o = at("rrs", [P, 4], o)
        cstat, _ = at("cstat", [P, 3, T1], area2)

        o = area2
        fsq, o = at("fsq", [P, 2, T1], o)
        facc, o = at("facc", [P, T1], o)
        ftmp, o = at("ftmp", [P, 2, T1], o)
        fstd, o = at("fstd", [P, T1], o)
        frs, o = at("frs", [P, T1], o)
        o = 0
        ahi, o = at("ahi", [P, KF, T1], o, F32R)
        alo, o = at("alo", [P, KF, T1], o, F32R)
        fsl_place = o
        fsl, o = at("fsl", [P, T1], o)
        fpr, o = at("fpr", [P, T1], o)

        S = SEQ
        o = 0
        attn_hi, o = at("attn_hi", [P, 4, S], o, F32R)
        attn_lo, o = at("attn_lo", [P, 4, S], o, F32R)
        place_of_z = o
        zhi, o = at("zhi", [P, 4, S], o, F32R)
        zlo, o = at("zlo", [P, 4, S], o, F32R)
        place_of_u = o
        uin, o = at("uin", [P, 4, S], o)
        yv, o = at("yv", [P, 4, S], o)
        place_of_q = o
        q2, o = at("q2", [P, 4, S], o)
        k2, o = at("k2", [P, 4, S], o)
        v2, base2 = at("v2", [P, 4, S], o)
        w1s, o = at("w1s", [P, 8, 2, P], 0)
        ap_, o = at("ap_", [P, 2, 8, 4, 32], o)
        assert o <= place_of_z
        st_, o = at("st_", [P, 2, 8, NC + 1], place_of_z)
        w8, o = at("w8", [P, 8, NC], o)
        bb, o = at("bb", [P, 2, 8, 32], o)
        assert o <= place_of_u
        o = base2
        smp, o = at("smp", [P, 3, 32], o)
        sbc, o = at("sbc", [P, 4, 8, 32], o)
        spw, o = at("spw", [P, 20, 32], o)
        lc_r, o = at("lc_r", [P, 32, 5], o)
        lc_i, o = at("lc_i", [P, 32, 5], o)
        lb_r, o = at("lb_r", [P, 32, 4], o)
        lb_i, o = at("lb_i", [P, 32, 4], o)
        chk, o = at("chk", [P, NC], o)
        place_of_reps = o
        reps, o = at("reps", [P, 2, 8, 4, 32], o)
        zz, _ = at("zz", [P, 2, 8, NC], place_of_reps)
        cp_, o = at("cp_", [P, 2, 8, 5, 32], o)
        tm_, o = at("tm_", [P, 4, P], o)
        us, o = at("us", [P, 2, 4, NC], o)
        cs_, o = at("cs_", [P, 2, 8, NC], o)
        m4, o = at("m4", [P, 8, NC], o)
        merged2, o = at("merged2", [P, KD, S], base2)
        natab, o = at("natab", [P, HEADS, NAR, GW], o)
        namask, o = at("namask", [P, GW], o)
        sm2, o = at("sm2", [P, 3, S], place_of_u)
        pts2, o = at("pts2", [P, 4, P], o)
        sg2, o = at("sg2", [P, S], o)
        mt2, o = at("mt2", [P, S], o)
        sga, _ = at("sga", [P, 2, S], place_of_u)
        sc2, o = at("sc2", [P, 4, 3], o)
        assert o <= place_of_q
        mhi, _ = at("mhi", [P, KD, S], place_of_q, F32R)
        mlo, _ = at("mlo", [P, KD, S], place_of_u, F32R)
        o = 0
        psg, o = at("psg", [P, 2, S], o)
        pmt, o = at("pmt", [P, S], o)
        pin, o = at("pin", [P, 2, S], fsl_place)
        plo, o = at("plo", [P, 2, S], fsl_place, F32R)
        phi, o = at("phi", [P, 2, S], o, F32R)
        assert o <= area2
        o = 6 * ROW
        yout, o = at("yout", [P, KD, S], o)

        acc = [ctx.enter_context(nc.psum_tensor(f"acc{i}", [P, 2, 512], F32)) for i in range(2)]
        aux = [ctx.enter_context(nc.psum_tensor(f"aux{i}", [P, 2, 512], F32)) for i in range(2)]

        evac = [sem("acc0_evacuated"), sem("acc1_evacuated")]
        pe_block = sem("pe_block_done")

        def halves(ap2, T):
            return ap2.rearrange("p (a b) -> p a b", a=2)

        def accv(s, T):
            return halves(acc[s][:, 0, :], T) if T == 512 else acc[s][:, :, 0:T // 2]

        def col(name, layer=None, j=0, n=1):
            c = COL[(name, layer)] if layer is not None else COL[name]
            return par[:, c + j:c + j + n]

        def h_ready(eng, phase):
            n = phase.tiles
            for i in (n - 2, n - 1):
                eng.wait_ge(evac[phase.slot(i)], phase.nth(i) + 1)

        def hview(T):
            return h[:, :, T1 - T:T1]

        NORMS = ["mix0", "ffn0", "mix1", "ffn1", "ffn2_1", "mix2", "ffn2_2", "ple2", "final"]
        NORM_G = [("mix_g", 0), ("ffn_g", 0), ("mix_g", 1), ("ffn_g", 1), ("ffn1_g", None), ("mix2_g", None),
                  ("ffn2_g", None), ("ple_g", None), ("final_g", None)]
        NORM_AFTER = [None, "out0", "down0", "out1", "down1", "down2", "out2", "down3", "ple2"]
        NORM_T = [T1] * 4 + [SEQ] * 5

        block = ctx.enter_context(nc.Block())

        @block.sync
        def _(sp):
            for b in range(RAW):
                sp.dma_start(raw[:, b], A_w[b]).then_inc(sem(f"w_loaded{b}"), 16)
            groups = NBLK // RAW
            with sp.Fori(1, groups) as g:
                for r in range(RAW):
                    sp.wait_ge(sem("w_split"), g * RAW + (r - RAW + 1))
                    sp.dma_start(raw[:, r], A_w[bass.ds(g * RAW + r, 1)].rearrange("a p n -> (a p) n"))\
                      .then_inc(sem(f"w_loaded{r}"), 16)
            for b in range(groups * RAW, NBLK):
                sp.wait_ge(sem("w_split"), b - RAW + 1)
                sp.dma_start(raw[:, b % RAW], A_w[b]).then_inc(sem(f"w_loaded{b % RAW}"), 16)
            for j in range(KD):
                sp.wait_ge(sem("final_out"), j + 1)
                sp.dma_start(A_out[j], yout[:, j]).then_inc(sem("stored"), 16)
            sp.wait_ge(sem("stored"), 16 * KD)

        @block.gpsimd
        def _(pool):
            pool.wait_ge(sem("consts_set"), 3)
            zb = zeros[:, :].unsqueeze(1).broadcast_to([P, BLK, P])

            def split(b, r, n):
                s = r % 2
                pool.wait_ge(sem(f"w_loaded{r}"), n)
                w = raw[:, r].rearrange("p (a c) -> p a c", a=BLK)
                hi = whi[:, s].rearrange("p (a c) -> p a c", a=BLK)
                lo = wlo[:, s].rearrange("p (a c) -> p a c", a=BLK)
                pool.tensor_tensor(hi, w, zb, ALU.add).then_inc(sem("w_hi"), 1)
                pool.wait_ge(sem("w_hi"), b + 1)
                pool.tensor_tensor(lo, w, hi.bitcast(F32), ALU.subtract).then_inc(sem("w_split"), 1)

            for b in range(RAW):
                if b >= 2:
                    pool.wait_ge(pe_block, b - 1)
                split(b, b, 16)
            groups = NBLK // RAW
            with pool.Fori(1, groups) as g:
                for r in range(RAW):
                    pool.wait_ge(pe_block, g * RAW + (r - 1))
                    split(g * RAW + r, r, g * 16 + 16)
            for b in range(groups * RAW, NBLK):
                pool.wait_ge(pe_block, b - 1)
                split(b, b % RAW, 16 * (b // RAW + 1))

        @block.tensor
        def _(pe):
            def part(s, slot, j, rhs, T, a, z):
                return products(s, slot, j, 1, rhs, T, a, z, w0=j)

            def products(s, slot, j0, nk, rhs, T, first, last, w0=0):
                TH = T // 2 if T > 512 else T
                for j in range(nk):
                    hi = whi[:, slot, (w0 + j) * P:(w0 + j + 1) * P]
                    lo = wlo[:, slot, (w0 + j) * P:(w0 + j + 1) * P]
                    xh, xl = rhs(j0 + j)
                    a, z = first and j == 0, last and j == nk - 1
                    for f in range(T // TH):
                        pe.matmul(acc[s][:, f, 0:TH], hi, xh[:, f * TH:(f + 1) * TH], start=a, stop=False)
                        pe.matmul(acc[s][:, f, 0:TH], hi, xl[:, f * TH:(f + 1) * TH], start=False, stop=False)
                    for f in range(T // TH):
                        m = pe.matmul(acc[s][:, f, 0:TH], lo, xh[:, f * TH:(f + 1) * TH], start=False, stop=z)
                return m

            def tile(ph, i, rhs, T, nk=KD, m=0, step=0, fresh=None):
                s = ph.slot(i)
                n = ph.nth(i) + m * (step // 2)
                if ph.nth(i):
                    pe.wait_ge(evac[s], n)
                for c in range(ph.per):
                    b = ph.block(i) + c
                    pe.wait_ge(sem("w_split"), b + 1 + m * (step * ph.per))
                    k0, kk = cuts(nk, ph.per)[c]
                    if fresh is None:
                        products(s, b % 2, k0, kk, rhs, T, c == 0, c == ph.per - 1).then_inc(pe_block, 1)
                        continue
                    for j in range(KD):
                        pe.wait_ge(sem("norm_lo"), fresh * KD + j + 1)
                        p = part(s, b % 2, j, rhs, T, j == 0, j == KD - 1)
                    p.then_inc(pe_block, 1)

            def bank(n):
                return aux[n // 2][:, n % 2, :]

            def short(n, slot, w0, nk, rhs):
                for j in range(nk):
                    hi = whi[:, slot, (w0 + j) * P:(w0 + j + 1) * P]
                    lo = wlo[:, slot, (w0 + j) * P:(w0 + j + 1) * P]
                    xh, xl = rhs(j)
                    pe.matmul(bank(n), hi, xh, start=j == 0, stop=False)
                    pe.matmul(bank(n), hi, xl, start=False, stop=False)
                    m = pe.matmul(bank(n), lo, xh, start=False, stop=j == nk - 1)
                return m

            def R(hi, lo, T):
                return lambda j: (hi[:, j, 0:T], lo[:, j, 0:T])

            def sumsq(i):
                T = NORM_T[i]
                pe.wait_ge(sem("norm_added"), (i + 1) * KD)
                for f in range(2):
                    m = pe.matmul(aux[0][:, f, 0:T // 2], ones[:, :],
                                  facc[:, T1 - T + f * (T // 2):T1 - T + (f + 1) * (T // 2)], start=True, stop=True)
                m.then_inc(sem("norm_summed"), 1)

            def ffn(i, up, down, T):
                sumsq(i)
                for j in range(2):
                    tile(AT[up], j, R(nhi, nlo, T), T, fresh=i if j == 0 else None)
                with pe.Fori(1, KF) as m:
                    for j in range(2):
                        tile(AT[up], j, R(nhi, nlo, T), T, m=m, step=2)
                pe.wait_ge(sem("ff_lo"), (FFI[up] + 1) * KF + 1)
                with pe.Fori(0, KD // 2) as m:
                    for j in range(2):
                        tile(AT[down], j, R(ahi, alo, T), T, nk=KF, m=m, step=2)

            def proj(l):
                qk, rhs = AT[f"qk{l}"], R(nhi, nlo, T1)

                def qk_sum(e):
                    it = l * 10 + e
                    pe.wait_ge(sem("qk_square"), it + 1)
                    if it:
                        pe.wait_ge(sem("qk_std"), it)
                    for f in range(2):
                        m = pe.matmul(aux[0][:, f, 0:T1 // 2], ones[:, :],
                                      tsq[:, e % 2, f * (T1 // 2):(f + 1) * (T1 // 2)], start=True, stop=True)
                    m.then_inc(sem("qk_sum"), 1)

                for e in range(10):
                    tile(qk, e, rhs, T1, fresh=2 * l if e == 0 else None)
                    if e:
                        qk_sum(e - 1)
                tile(AT[f"v{l}"], 0, rhs, T1)
                qk_sum(9)
                tile(AT[f"v{l}"], 1, rhs, T1)
                for e in range(4):
                    tile(AT[f"qi{l}"], e, rhs, T1)
                pe.wait_ge(evac[AT[f"v{l}"].slot(1)], AT[f"v{l}"].nth(1) + 1)
                pe.wait_ge(sem("qk_std"), (l + 1) * 10)
                for e in range(KV):
                    for c in range(4):
                        pe.transpose(aux[1][:, e, c * P:(c + 1) * P], vT[:, e, c * P:(c + 1) * P], ident[:, :])
                for e in range(KV):
                    m = pe.transpose(aux[0][0:16, e, 0:P], vT[:, e, 4 * P:T1], ident[:, :])
                m.then_inc(sem("v_turned"), 1)
                tile(AT[f"qi{l}"], 4, rhs, T1)
                pe.wait_ge(sem("wi_rows"), l + 1)
                pe.wait_ge(sem("v_copied"), 4 * (l + 1))
                for i in range(NQT):
                    m = pe.transpose(aux[0][:, 1, i * 32:(i + 1) * 32], wbuf[:, META + i * P:META + (i + 1) * P],
                                     ident[0:32, 0:32])
                m.then_inc(sem("wi_turned"), 1)

            def index(l):
                pe.wait_ge(sem("qi_done"), 5 * (l + 1))
                pe.wait_ge(sem("wi_copied"), l + 1)
                for i in range(NQT):
                    W = META + P * (i + 1)
                    for hh in range(IXH):
                        it = (l * NQT + i) * IXH + hh
                        if it >= 2:
                            pe.wait_ge(sem("ix_relu"), it - 1)
                        rows = slice(64 * (hh % 2), 64 * (hh % 2) + 64)
                        lhs = qi[rows, hh // 2, META + i * P:META + (i + 1) * P]
                        m = pe.matmul(aux[hh % 2][:, 0, 0:min(W, 512)], lhs, ki[rows, 0:min(W, 512)], start=True, stop=True)
                        if W > 512:
                            m = pe.matmul(aux[hh % 2][:, 1, 0:W - 512], lhs, ki[rows, 512:W], start=True, stop=True)
                        m.then_inc(sem("ix_logit"), 1)

            def rnn(l):
                ph, rhs = AT[f"rnn{l}"], R(nhi, nlo, T1)

                def gates(n):
                    it = l * 8 + n
                    pe.wait_ge(sem("rnn_conv"), 4 * (it + 1))
                    if n == 0:
                        pe.wait_ge(sem("rnn_w_loaded"), 16 * (l + 1))
                        pe.wait_ge(sem("ix_relu"), (l + 1) * NQT * IXH)
                    if it:
                        pe.wait_ge(sem("rnn_i"), it)
                    for g in range(2):
                        for f in range(2):
                            m = pe.matmul(aux[g][:, f, 0:T1 // 2], rnn_w[:, g, n],
                                          ru[:, f * (T1 // 2):(f + 1) * (T1 // 2)], start=True, stop=True)
                    m.then_inc(sem("rnn_gates"), 1)

                for n in range(8):
                    tile(ph, 2 * n, rhs, T1)
                    if n:
                        gates(n - 1)
                    tile(ph, 2 * n + 1, rhs, T1)
                gates(7)

            def ln_mean(l):
                for n in range(KD):
                    pe.wait_ge(sem("cv_conv"), (l * 8 + n // 2 * 2 + 2) * DW)
                    if n == 0:
                        pe.wait_ge(sem("at_scored"), (l + 1) * ITEMS)
                    for f in range(2):
                        m = pe.matmul(aux[0][:, f, 0:T1 // 2], ones[:, :], cu[:, n, f * (T1 // 2):(f + 1) * (T1 // 2)],
                                      start=n == 0, stop=n == KD - 1)
                m.then_inc(sem("cv_mean"), 1)

            def ln_square(l):
                for n in range(KD):
                    pe.wait_ge(sem("cv_square"), l * 8 + n + 1)
                    for f in range(2):
                        m = pe.matmul(aux[1][:, f, 0:T1 // 2], ones[:, :], csq[:, n % 2, f * (T1 // 2):(f + 1) * (T1 // 2)],
                                      start=n == 0, stop=n == KD - 1)
                    m.then_inc(sem("cv_summed"), 1)

            def mix(l):
                ph, mg = AT[f"att{l}"], AT[f"mg_rnn{l}"]
                items = [(hh, i) for hh in range(HEADS) for i in range(NQT + 1)]
                n0 = l * len(items)

                def shape(i):
                    return (P, META + i * P, META + (i + 1) * P) if i < NQT else (META, 0, META)

                def scores(j):
                    hh, i = items[j]
                    r, c, W = shape(i)
                    if n0 + j:
                        pe.wait_ge(sem("at_scored"), n0 + j)
                    lhs = q[:, hh, c:c + r]
                    m = pe.matmul(aux[0][0:r, 0, 0:min(W, 512)], lhs, k[:, hh // 4, 0:min(W, 512)], start=True, stop=True)
                    if W > 512:
                        m = pe.matmul(aux[0][0:r, 1, 0:W - 512], lhs, k[:, hh // 4, 512:W], start=True, stop=True)
                    m.then_inc(sem("at_s"), 1)

                def pieces(W):
                    return [(c, min(P, W - c * P)) for c in range(-(-W // P))]

                def turn(j):
                    hh, i = items[j]
                    r, _, W = shape(i)
                    pe.wait_ge(sem("at_p"), n0 + j + 1)
                    if n0 + j:
                        pe.wait_ge(sem("at_pt"), n0 + j)
                    for c, w in pieces(W):
                        m = pe.transpose(aux[1][0:w, c // 4, (c % 4) * P:(c % 4) * P + r], sm[0:r, j % 3, c * P:c * P + w],
                                         ident[0:r, 0:r])
                    m.then_inc(sem("at_turned"), 1)

                def values(j):
                    hh, i = items[j]
                    r, _, W = shape(i)
                    s = ph.slot(hh)
                    if i == 0:
                        pe.wait_ge(evac[s], ph.nth(hh))
                    pe.wait_ge(sem("at_pt"), n0 + j + 1)
                    ps = pieces(W)
                    for c, w in ps:
                        out = acc[s][:, 0, i * P:(i + 1) * P] if i < NQT else acc[s][:, 1, 0:META]
                        m = pe.matmul(out, v[0:w, c, (hh // 4) * P:(hh // 4 + 1) * P], pts[0:w, c, 0:r],
                                      start=c == 0, stop=c == len(ps) - 1)
                    m.then_inc(sem("at_pv"), 1)

                def merge_part(j):
                    i, a, z = MERGE_PARTS[j % 5]
                    t = 2 * (j // 5) + i
                    s, b = mg.slot(t), mg.block(t)
                    if a == 0:
                        pe.wait_ge(evac[s], mg.nth(t))
                        pe.wait_ge(sem("w_split"), b + 1)
                    rhs = R(bhi, blo, T1) if i else R(nhi, nlo, T1)
                    for c in range(a, z):
                        p = part(s, b % 2, c, rhs, T1, c == 0, c == KD - 1)
                    if z == KD:
                        p.then_inc(pe_block, 1)

                pe.wait_ge(sem("qk_done"), (l + 1) * 10)
                pe.wait_ge(sem("mask_done"), l + 1)
                pe.wait_ge(sem("rnn_i"), (l + 1) * 8)
                scores(0)
                scores(1)
                for j in range(len(items)):
                    if j == 3:
                        pe.wait_ge(sem("br_lo"), (l * 4 + 1) * KD)
                    turn(j)
                    if j + 2 < len(items):
                        scores(j + 2)
                    merge_part(j)
                    values(j)

            def turn_v2():
                pe.wait_ge(sem("v2_rows"), 1)
                pe.wait_ge(sem("ss_y"), 64)
                for e in range(4):
                    for c in range(4):
                        m = pe.transpose(aux[e // 2][:, e % 2, c * P:(c + 1) * P], v2[:, e, c * P:(c + 1) * P], ident[:, :])
                m.then_inc(sem("v2_turned"), 1)

            def neighbours():
                items = [(hh, i) for hh in range(HEADS) for i in range(NQT)]
                ph, mg = AT["att2"], AT["mg_ssm2"]
                pe.wait_ge(sem("v2_copied"), 4)

                def scores(j):
                    hh, i = items[j]
                    rows = slice(64 * (hh % 2), 64 * (hh % 2) + 64)
                    if j:
                        pe.wait_ge(sem("na_scored"), j)
                    pe.matmul(aux[0][:, 0, :], q2[rows, hh // 2, i * P:(i + 1) * P], k2[rows, hh // 2, :],
                              start=True, stop=True).then_inc(sem("na_s"), 1)

                def turn(j):
                    pe.wait_ge(sem("na_p"), j + 1)
                    if j:
                        pe.wait_ge(sem("na_pt"), j)
                    for c in range(4):
                        m = pe.transpose(aux[1][:, 0, c * P:(c + 1) * P], sm2[:, j % 3, c * P:(c + 1) * P], ident[:, :])
                    m.then_inc(sem("na_turned"), 1)

                def merge_part(j):
                    i, a, z, end = NA_PARTS[j % NQT]
                    t = 2 * (j // NQT) + i
                    s, b = mg.slot(t), mg.block(t)
                    if a == 0:
                        pe.wait_ge(evac[s], mg.nth(t))
                        pe.wait_ge(sem("w_split"), b + 1)
                        if i:
                            pe.wait_ge(sem("z_lo"), 4)
                    rhs = R(zhi, zlo, S) if i else R(nhi, nlo, S)
                    for c in range(a, z):
                        p = part(s, b % 2, c, rhs, S, c == 0, c == end - 1)
                    if z == end:
                        p.then_inc(pe_block, 1)

                def values(j):
                    hh, i = items[j]
                    if hh % 2 == 0 and i == 0:
                        pe.wait_ge(evac[1], ph.nth(hh // 2))
                    pe.wait_ge(sem("na_pt"), j + 1)
                    for c in range(4):
                        m = pe.matmul(acc[1][64 * (hh % 2):64 * (hh % 2) + 64, 0, i * P:(i + 1) * P],
                                      v2[:, c, 64 * hh:64 * hh + 64], pts2[:, c, :], start=c == 0, stop=c == 3)
                    m.then_inc(sem("na_pv"), 1)

                scores(0)
                scores(1)
                for j in range(len(items)):
                    turn(j)
                    if j + 2 < len(items):
                        scores(j + 2)
                    merge_part(j)
                    values(j)

            def ssm():
                qkv = lambda i: tile(AT["qkv2"], i, R(nhi, nlo, S), S)
                for r in range(4):
                    qkv(3 * r)
                    qkv(3 * r + 1)
                    pe.wait_ge(sem("ss_bpow"), 4 * (r + 1))
                    for g in range(4):
                        if g or r:
                            pe.wait_ge(sem("ss_w1"), 4 * r + g)
                        for c in range(4):
                            e, z = (g * 4 + c) // 2, c % 2
                            m = pe.transpose(aux[1][:, 0, c * P:(c + 1) * P], ap_[:, z, e].rearrange("p a b -> p (a b)"),
                                             ident[:, :])
                        m.then_inc(sem("ss_w1_turned"), 1)
                    pe.wait_ge(sem("ss_rep"), 2 * (r + 1))
                    pe.wait_ge(sem("ss_cpow"), 2 * (r + 1))
                    if r:
                        pe.wait_ge(sem("ss_y"), 16 * r)
                    for d in range(2):
                        for u in range(4):
                            e = d * 4 + u
                            pe.matmul(aux[0][:, d, u * P:(u + 1) * P], reps[:, 0, e].rearrange("p a b -> p (a b)"),
                                      cp_[:, 0, e, d:d + 4].rearrange("p a b -> p (a b)"), start=True, stop=False)
                            m = pe.matmul(aux[0][:, d, u * P:(u + 1) * P], reps[:, 1, e].rearrange("p a b -> p (a b)"),
                                          cp_[:, 1, e, d:d + 4].rearrange("p a b -> p (a b)"), start=False, stop=True)
                    m.then_inc(sem("ss_lags"), 1)
                    pe.wait_ge(sem("ss_w1"), 4 * (r + 1))
                    pe.wait_ge(sem("ss_u"), 32 * (r + 1))
                    pe.wait_ge(sem("ss_t"), r + 1)
                    for z in range(2):
                        for e in range(8):
                            m = pe.matmul(aux[z][:, e // 4, (e % 4) * NC:(e % 4 + 1) * NC], w1s[:, e, z],
                                          us[:, e // 4, e % 4], start=True, stop=True)
                    m.then_inc(sem("ss_s"), 1)
                    qkv(3 * r + 2)
                    pe.wait_ge(sem("ss_x"), 4 * (r + 1))
                    for u in range(4):
                        out = aux[0][:, 0, u * NC:(u + 1) * NC]
                        pe.matmul(out, tm_[:, u], us[:, 0, u], start=True, stop=False)
                        for d in range(2):
                            for z in range(2):
                                lhs = cp_[:, z, d * 4 + u, 1 - d:5 - d].rearrange("p a b -> p (a b)")
                                m = pe.matmul(out, lhs, st_[:, z, d * 4 + u, d:d + NC], start=False, stop=(d, z) == (1, 1))
                    m.then_inc(sem("ss_out"), 1)

            pe.wait_ge(sem("consts_set"), 3)
            pe.wait_ge(sem("ident_loaded"), 16)
            for l in range(DEPTH):
                sumsq(2 * l)
                proj(l)
                index(l)
                for n in range(16):
                    tile(AT[f"conv{l}"], n, R(nhi, nlo, T1), T1)
                rnn(l)
                mix(l)
                pe.wait_ge(sem("br_lo"), (l * 4 + 1) * KD + 1)
                ph = AT[f"mg_att{l}"]
                tile(ph, 0, R(nhi, nlo, T1), T1)
                pe.wait_ge(sem("br_lo"), (l * 4 + 2) * KD)
                tile(ph, 1, R(bhi, blo, T1), T1)
                with pe.Fori(1, LN_AFTER) as m:
                    tile(ph, 0, R(nhi, nlo, T1), T1, m=m, step=2)
                    tile(ph, 1, R(bhi, blo, T1), T1, m=m, step=2)
                ln_mean(l)
                for n in range(2 * LN_AFTER, 2 * LN_AFTER + 2):
                    tile(ph, n, R(bhi, blo, T1) if n % 2 else R(nhi, nlo, T1), T1)
                ln_square(l)
                for n in range(2 * LN_AFTER + 2, 2 * KD):
                    tile(ph, n, R(bhi, blo, T1) if n % 2 else R(nhi, nlo, T1), T1)
                ph = AT[f"mg_conv{l}"]
                tile(ph, 0, R(nhi, nlo, T1), T1)
                pe.wait_ge(sem("br_lo"), (l * 4 + 3) * KD)
                tile(ph, 1, R(bhi, blo, T1), T1)
                with pe.Fori(1, KD) as m:
                    tile(ph, 0, R(nhi, nlo, T1), T1, m=m, step=2)
                    tile(ph, 1, R(bhi, blo, T1), T1, m=m, step=2)
                pe.wait_ge(sem("br_lo"), (l * 4 + 4) * KD)
                with pe.Fori(0, KD // 2) as m:
                    for j in range(2):
                        tile(AT[f"out{l}"], j, R(bhi, blo, T1), T1, m=m, step=2)
                ffn(2 * l + 1, f"up{l}", f"down{l}", T1)
            ffn(4, "up2", "down2", SEQ)
            sumsq(5)
            for i in range(4):
                tile(AT["sin2"], i, R(nhi, nlo, S), S, fresh=5 if i == 0 else None)
            ssm()
            turn_v2()
            pe.wait_ge(sem("y_lo"), 4)
            for i in range(4):
                tile(AT["glu2"], i, R(zhi, zlo, S), S, nk=4)
            neighbours()
            for i in range(4):
                tile(AT[f"att_gate{2 * i}"], 0, R(nhi, nlo, S), S)
                b = AT[f"att_products{i}"].b0
                pe.wait_ge(sem("w_split"), b + 1)
                if i == 0:
                    pe.wait_ge(evac[1], AT["att2"].nth(3) + 1)
                    pe.wait_ge(sem("na_pt"), HEADS * NQT)
                if i >= 2:
                    pe.wait_ge(sem("att_product"), 2 * (i - 1))
                for e in range(2):
                    m = short((2 * i + e) % 4, b % 2, 4 * e, 4, R(attn_hi, attn_lo, S))
                m.then_inc(pe_block, 1)
                tile(AT[f"att_gate{2 * i + 1}"], 0, R(nhi, nlo, S), S)
            pe.wait_ge(sem("m2_lo"), KD)
            with pe.Fori(0, KD // 2) as m:
                for j in range(2):
                    tile(AT["out2"], j, R(mhi, mlo, S), S, m=m, step=2)
            ffn(6, "up3", "down3", SEQ)
            sumsq(7)
            pe.wait_ge(sem("p_lo"), 2)
            for half in range(2):
                b = AT[f"ple_products{half}"].b0
                pe.wait_ge(sem("w_split"), b + 1)
                if half:
                    pe.wait_ge(sem("ple_product"), 4)
                for e in (2, 3, 0, 1):
                    if (half, e) == (0, 0):
                        pe.wait_ge(sem("norm_std"), 8)
                    m = short(e, b % 2, 2 * e, 2, R(phi, plo, S))
                m.then_inc(pe_block, 1)
                for i in range(5) if half == 0 else range(5, KD):
                    tile(AT[f"ple_gate{i}"], 0, R(nhi, nlo, S), S, fresh=7 if i == 0 else None)
            sumsq(8)

        @block.scalar
        def _(act):
            def block_done(b):
                act.wait_ge(pe_block, b)

            def norm(i):
                T = NORM_T[i]
                if i == 0:
                    act.wait_ge(sem("h_loaded"), 16)
                    for j in range(KD):
                        if j >= 2:
                            act.wait_ge(sem("norm_added"), j - 1)
                        act.activation(fsq[:, j % 2, :], h[:, j, :], ACT.Square).then_inc(sem("norm_square"), 1)
                act.wait_ge(sem("norm_summed"), i + 1)
                act.activation(halves(fstd[:, 0:T], T), aux[0][:, :, 0:T // 2], ACT.Sqrt, bias=EPS, scale=1.0 / D)\
                   .then_inc(sem("norm_std"), 1)
                if i == 8:
                    return
                for j in range(KD):
                    act.wait_ge(sem("norm_scaled"), i * KD + j + 1)
                    act.activation(nhi[:, j, 0:T], ftmp[:, j % 2, 0:T], ACT.Copy).then_inc(sem("norm_hi"), 1)

            def ffn(i, up, T):
                norm(i)
                ph, f = AT[up], FFI[up]
                down = AT[up.replace("up", "down")]
                with act.Fori(0, KF) as m:
                    block_done(m * 2 + (ph.block(0) + 1))
                    act.wait_ge(evac[ph.slot(1)], m + ph.nth(1))
                    act.activation(halves(fsl[:, 0:T], T), accv(ph.slot(0), T), ACT.Silu).then_inc(evac[ph.slot(0)], 1)
                    act.wait_ge(evac[ph.slot(1)], m + (ph.nth(1) + 1))
                    act.activation(ahi[:, bass.ds(m, 1), 0:T], fpr[:, 0:T].unsqueeze(1), ACT.Copy).then_inc(sem("ff_hi"), 1)
                if up == "up3":
                    act.wait_ge(sem("ff_lo"), (f + 1) * KF + 1)
                    act.dma_start(pin[:, :, :], A_p.rearrange("a p n -> p a n")).then_inc(sem("p_loaded"), 16)
                    act.wait_ge(sem("p_loaded"), 16)
                    act.activation(phi[:, :, :], pin[:, :, :], ACT.Copy).then_inc(sem("p_hi"), 1)
                squares(i + 1, down)

            def squares(i, ph):
                with act.Fori(0, KD // 2) as m:
                    for j in range(2):
                        act.wait_ge(evac[ph.slot(j)], m + (ph.nth(j) + 1))
                        act.wait_ge(sem("norm_added"), m * 2 + (i * KD + j - 1))
                        act.activation(fsq[:, j].unsqueeze(1), h[:, bass.ds(m * 2 + j, 1), :], ACT.Square)\
                           .then_inc(sem("norm_square"), 1)

            def proj(l):
                qk, vp, qp = AT[f"qk{l}"], AT[f"v{l}"], AT[f"qi{l}"]

                def std(e):
                    it = l * 10 + e
                    act.wait_ge(sem("qk_sum"), it + 1)
                    if it:
                        act.wait_ge(sem("qk_done"), it)
                    act.activation(halves(tstd[:, :], T1), aux[0][:, :, 0:T1 // 2], ACT.Sqrt, bias=EPS, scale=1.0 / HD)\
                       .then_inc(sem("qk_std"), 1)

                for e in range(10):
                    it, s = l * 10 + e, qk.slot(e)
                    block_done(qk.block(e) + 1)
                    if e >= 2:
                        act.wait_ge(sem("qk_sum"), it - 1)
                    act.activation(halves(tsq[:, e % 2, :], T1), accv(s, T1), ACT.Square).then_inc(sem("qk_square"), 1)
                    if e >= 2:
                        act.wait_ge(sem("qk_done"), it - 1)
                    act.activation(halves(tqg[:, e % 2, :], T1), accv(s, T1), ACT.Copy,
                                   scale=col("q_g" if e < 8 else "k_g", l)).then_inc(evac[s], 1)
                    act.wait_ge(evac[s], qk.nth(e) + 1)
                    act.activation(tsw[0:64, e % 2, :], tqg[64:128, e % 2, :], ACT.Copy)
                    act.activation(tsw[64:128, e % 2, :], tqg[0:64, e % 2, :], ACT.Copy).then_inc(sem("qk_swap"), 1)
                    if e:
                        std(e - 1)
                for e in range(KV):
                    block_done(vp.block(e) + 1)
                    act.activation(halves(vT[:, e, :], T1), accv(vp.slot(e), T1), ACT.Copy).then_inc(evac[vp.slot(e)], 1)
                    if e == 0:
                        std(9)
                for e in range(5):
                    it, s = l * 5 + e, qp.slot(e)
                    block_done(qp.block(e) + 1)
                    if e < 2:
                        act.wait_ge(sem("qk_done"), (l + 1) * 10)
                    else:
                        act.wait_ge(sem("qi_done"), it - 1)
                    a, x, w = accv(s, T1), tqg[:, e % 2, :], tsw[:, e % 2, :]
                    if e < 4:
                        act.activation(halves(x, T1), a, ACT.Copy).then_inc(evac[s], 1)
                    else:
                        act.activation(halves(x[0:64], T1), a[0:64], ACT.Copy)
                        act.activation(halves(x[64:128], T1), a[0:64], ACT.Copy)
                        act.activation(halves(wbuf[:, :], T1), a[64:96], ACT.Copy, scale=IXH ** -0.5 * IXD ** -0.5)\
                           .then_inc(evac[s], 1)
                    act.wait_ge(evac[s], qp.nth(e) + 1)
                    for c in range(4):
                        m = act.activation(w[32 * c:32 * c + 32], x[32 * (c ^ 1):32 * (c ^ 1) + 32], ACT.Copy)
                    m.then_inc(sem("qi_swap"), 1)
                    if e == 3:
                        act.wait_ge(sem("v_turned"), l + 1)
                        for c in range(KV):
                            act.activation(v[:, 0:4, c * HD:(c + 1) * HD],
                                           aux[1][:, c, :].rearrange("p (a b) -> p a b", a=4), ACT.Copy).then_inc(sem("v_copied"), 1)
                            act.activation(v[0:16, 4, c * HD:(c + 1) * HD], aux[0][0:16, c, 0:P], ACT.Copy)\
                               .then_inc(sem("v_copied"), 1)
                    if e == 4:
                        act.wait_ge(evac[s], qp.nth(e) + 1)
                        act.sem_inc(sem("wi_rows"), 1)
                act.wait_ge(sem("wi_turned"), l + 1)
                act.activation(wi[:, :, :], aux[0][:, 1, 0:NQT * 32].rearrange("p (a b) -> p a b", a=NQT)[:, :, 0:IXH],
                               ACT.Copy).then_inc(sem("wi_copied"), 1)

            def index(l):
                for i in range(NQT):
                    W = META + P * (i + 1)
                    for hh in range(IXH):
                        it = (l * NQT + i) * IXH + hh
                        act.wait_ge(sem("ix_logit"), it + 1)
                        if hh >= 2 or i:
                            act.wait_ge(sem("ix_acc"), it - 1)
                        src = aux[hh % 2][:, :, :].rearrange("p a b -> p (a b)")[:, 0:W]
                        act.activation(tsq[:, hh % 2, 0:W], src, ACT.Relu).then_inc(sem("ix_relu"), 1)

            def rnn(l):
                ph = AT[f"rnn{l}"]

                def gates(n):
                    it = l * 8 + n
                    act.wait_ge(sem("rnn_gates"), it + 1)
                    if n:
                        act.wait_ge(sem("rnn_b"), it)
                    act.activation(halves(rr[:, :], T1), aux[0][:, :, 0:T1 // 2], ACT.Tanh, bias=hba[:, l, 0, n:n + 1],
                                   scale=0.5).then_inc(sem("rnn_r"), 1)
                    act.activation(halves(ri[:, :], T1), aux[1][:, :, 0:T1 // 2], ACT.Tanh, bias=hba[:, l, 1, n:n + 1],
                                   scale=0.5).then_inc(sem("rnn_i"), 1)
                    act.wait_ge(sem("rnn_r"), it + 1)
                    act.activation(rt[:, :], rr[:, :], ACT.Tanh, bias=spc[:, l, n:n + 1], scale=spc[:, l, n:n + 1])\
                       .then_inc(sem("rnn_t"), 1)
                    if n:
                        act.wait_ge(sem("rnn_scan"), it)
                    act.activation(ra[:, :], rr[:, :], ACT.Exp, bias=nspc[:, l, n:n + 1], scale=nspc[:, l, n:n + 1])\
                       .then_inc(sem("rnn_a"), 1)
                    act.wait_ge(sem("rnn_m"), 3 * (it + 1))
                    act.activation(rb[:, :], rb[:, :], ACT.Sqrt, scale=0.5).then_inc(sem("rnn_sqrt"), 1)

                def part(n):
                    it = l * 8 + n
                    act.wait_ge(sem("rnn_out"), it + 1)
                    act.activation(bhi[:, n, :], rh[:, :], ACT.Copy).then_inc(sem("br_hi"), 1)

                act.wait_ge(sem("rnn_pad"), l + 1)
                for n in range(8):
                    it = l * 8 + n
                    sx, sy = ph.slot(2 * n), ph.slot(2 * n + 1)
                    block_done(ph.block(2 * n) + 1)
                    if n:
                        act.wait_ge(sem("rnn_conv"), 4 * it)
                    act.activation(halves(rx[:, CONV - 1:], T1), accv(sx, T1), ACT.Copy).then_inc(evac[sx], 1)
                    if n:
                        gates(n - 1)
                        part(n - 1)
                    block_done(ph.block(2 * n + 1) + 1)
                    act.activation(halves(rg[:, :], T1), accv(sy, T1), ACT.Gelu_apprx_tanh).then_inc(evac[sy], 1)
                gates(7)
                part(7)

            def merge(l, name):
                ph = AT[f"mg_{name}{l}"]
                with act.Fori(0, KD) as m:
                    block_done(m * 2 + (ph.block(0) + 1))
                    act.wait_ge(evac[ph.slot(1)], m + ph.nth(1))
                    act.activation(halves(sg[:, :], T1), accv(ph.slot(0), T1), ACT.Sigmoid).then_inc(evac[ph.slot(0)], 1)

            def conv_gates(l):
                ph = AT[f"conv{l}"]
                for n in range(KD):
                    block_done(ph.block(2 * n) + 1)
                    if n:
                        act.wait_ge(evac[1], ph.nth(2 * n - 1) + 1)
                    act.activation(halves(csg[:, :], T1), accv(0, T1), ACT.Sigmoid).then_inc(evac[0], 1)

            def att_split(l):
                for n in range(KD):
                    if n == 0:
                        block_done(AT[f"mg_att{l}"].b0)
                    act.wait_ge(evac[1], AT[f"att{l}"].nth(n) + 1)
                    act.activation(bhi[:, n], q[:, n], ACT.Copy).then_inc(sem("br_hi"), 1)

            def gate(ph, m):
                block_done(ph.block(0) + 2 * m + 1)
                act.wait_ge(evac[ph.slot(1)], ph.nth(1) + m)
                act.activation(halves(sg[:, :], T1), accv(ph.slot(0), T1), ACT.Sigmoid).then_inc(evac[ph.slot(0)], 1)

            def mg_att(l):
                ph = AT[f"mg_att{l}"]
                with act.Fori(0, LN_AFTER) as m:
                    block_done(m * 2 + (ph.block(0) + 1))
                    act.wait_ge(evac[ph.slot(1)], m + ph.nth(1))
                    act.activation(halves(sg[:, :], T1), accv(ph.slot(0), T1), ACT.Sigmoid).then_inc(evac[ph.slot(0)], 1)
                ln_first(l)
                gate(ph, LN_AFTER)
                ln_second(l)
                for m in range(LN_AFTER + 1, KD):
                    gate(ph, m)
                for n in range(KD):
                    act.wait_ge(sem("cv_scaled"), l * 8 + n + 1)
                    act.activation(cu[:, n], cu[:, n], ACT.Silu, bias=col("ln_b", l, n), scale=col("ln_g", l, n))\
                       .then_inc(sem("cv_silu"), 1)
                block_done(AT[f"mg_conv{l}"].b0)
                act.wait_ge(sem("cv_silu"), (l + 1) * 8)
                for n in range(KD):
                    act.activation(bhi[:, n], cu[:, n], ACT.Copy).then_inc(sem("br_hi"), 1)

            def ln_first(l):
                act.wait_ge(sem("cv_mean"), l + 1)
                act.activation(halves(cstat[:, 0], T1), aux[0][:, :, 0:T1 // 2], ACT.Copy, scale=1.0 / D)\
                   .then_inc(sem("cv_mean_read"), 1)

            def ln_second(l):
                for n in range(KD):
                    act.wait_ge(sem("cv_centred"), l * 8 + n + 1)
                    if n >= 2:
                        act.wait_ge(sem("cv_summed"), l * 8 + n - 1)
                    act.activation(csq[:, n % 2], cu[:, n], ACT.Square).then_inc(sem("cv_square"), 1)
                act.wait_ge(sem("cv_summed"), (l + 1) * 8)
                act.activation(halves(cstat[:, 1], T1), aux[1][:, :, 0:T1 // 2], ACT.Sqrt, bias=EPS, scale=1.0 / D)\
                   .then_inc(sem("cv_std"), 1)

            def mix(l):
                ph, mg = AT[f"att{l}"], AT[f"mg_rnn{l}"]
                items = [(hh, i) for hh in range(HEADS) for i in range(NQT + 1)]
                n0 = l * len(items)

                def exps(j):
                    b = j % 3
                    r, W = (P, META + (items[j][1] + 1) * P) if items[j][1] < NQT else (META, META)
                    act.wait_ge(sem("at_max"), n0 + j + 1)
                    act.activation(sm[0:r, b, 0:W], sm[0:r, b, 0:W], ACT.Exp, bias=nmx[0:r, b:b + 1],
                                   accum_out=rsum[0:r, b:b + 1]).then_inc(sem("at_exp"), 1)

                def turned(j):
                    i = items[j][1]
                    act.wait_ge(sem("at_turned"), n0 + j + 1)
                    if j:
                        act.wait_ge(sem("at_pv"), n0 + j)
                    if i < NQT:
                        c = i + 1
                        act.activation(pts[:, 0:c, :], aux[1][:, :, :].rearrange("p a (b c) -> p (a b) c", c=P)[:, 0:c, :], ACT.Copy)
                        act.activation(pts[0:META, c, :], aux[1][0:META, c // 4, (c % 4) * P:(c % 4 + 1) * P], ACT.Copy)\
                           .then_inc(sem("at_pt"), 1)
                    else:
                        act.activation(pts[0:META, 0, 0:META], aux[1][0:META, 0, 0:META], ACT.Copy).then_inc(sem("at_pt"), 1)

                exps(0)
                exps(1)
                for j in range(len(items)):
                    hh, i = items[j]
                    turned(j)
                    if i == 0 and hh:
                        s = ph.slot(hh - 1)
                        act.wait_ge(sem("at_pv"), n0 + j)
                        act.activation(q[:, hh - 1, META:], acc[s][:, 0, :], ACT.Copy)
                        act.activation(q[:, hh - 1, 0:META], acc[s][:, 1, 0:META], ACT.Copy).then_inc(evac[s], 1)
                    if j + 2 < len(items):
                        exps(j + 2)
                    if i == 2:
                        t = 2 * hh
                        block_done(mg.block(t) + 1)
                        if t:
                            act.wait_ge(evac[0], mg.nth(t - 1) + 1)
                        act.activation(halves(sg[:, :], T1), accv(0, T1), ACT.Tanh, scale=0.5).then_inc(evac[0], 1)
                s, hh = ph.slot(HEADS - 1), HEADS - 1
                act.wait_ge(sem("at_pv"), n0 + len(items))
                act.activation(q[:, hh, META:], acc[s][:, 0, :], ACT.Copy)
                act.activation(q[:, hh, 0:META], acc[s][:, 1, 0:META], ACT.Copy).then_inc(evac[s], 1)

            def neighbours():
                items = [(hh, i) for hh in range(HEADS) for i in range(NQT)]
                ph, mg = AT["att2"], AT["mg_ssm2"]

                def exps(j):
                    b = j % 3
                    act.wait_ge(sem("na_max"), j + 1)
                    act.activation(sm2[:, b], sm2[:, b], ACT.Exp, bias=sc2[:, 1, b:b + 1],
                                   accum_out=sc2[:, 2, b:b + 1]).then_inc(sem("na_exp"), 1)

                def part(t):
                    act.activation(attn_hi[:, t], acc[1][:, 0, :], ACT.Copy).then_inc(sem("attn2_hi"), 1)

                exps(0)
                exps(1)
                for j in range(len(items)):
                    hh, i = items[j]
                    act.wait_ge(sem("na_turned"), j + 1)
                    if j:
                        act.wait_ge(sem("na_pv"), j)
                    act.activation(pts2[:, :, :], aux[1][:, 0, :].rearrange("p (a b) -> p a b", a=4), ACT.Copy)\
                       .then_inc(sem("na_pt"), 1)
                    if hh and hh % 2 == 0 and i == 0:
                        part(hh // 2 - 1)
                    if j + 2 < len(items):
                        exps(j + 2)
                    if i == 2:
                        t = 2 * hh
                        block_done(mg.block(t) + 1)
                        act.wait_ge(evac[0], mg.nth(t))
                        act.activation(halves(sg2[:, :], S), accv(0, S), ACT.Tanh, scale=0.5).then_inc(evac[0], 1)
                act.wait_ge(sem("na_pv"), len(items))
                part(3)

            def ssm_parameters():
                act.dma_start(smp[:, :, :], A_ssm[0:3].rearrange("a p n -> p a n")[:, :, 0:32]).then_inc(sem("ssm_loaded"), 16)
                act.dma_start(chk[:, :], A_chunk).then_inc(sem("ssm_loaded"), 16)
                load_bc(0)
                act.wait_ge(sem("ssm_loaded"), 32)
                act.activation(spw[:, 0], smp[:, 0], ACT.Exp).then_inc(sem("ss_dt"), 1)
                act.wait_ge(sem("ss_reduced"), 1)
                act.activation(spw[:, 4], spw[:, 2], ACT.Sin)
                act.activation(spw[:, 5], spw[:, 2], ACT.Sin, scale=0.5)
                act.activation(spw[:, 6], spw[:, 1], ACT.Tanh, scale=0.5)
                act.activation(spw[:, 7], spw[:, 1], ACT.Exp, scale=4.0).then_inc(sem("ss_waves"), 1)

            def load_bc(r):
                act.dma_start(sbc[:, :, :, :].rearrange("p a b c -> p a (b c)"),
                              A_ssm[3:7, :, 256 * r:256 * (r + 1)].rearrange("a p n -> p a n")).then_inc(sem("ss_bc_loaded"), 16)

            def ssm():
                qkv = AT["qkv2"]

                def projected(i):
                    dst = (q2, k2, v2)[i // 4][:, i % 4]
                    block_done(qkv.block(i) + 1)
                    act.activation(halves(dst, S), accv(qkv.slot(i), S), ACT.Copy, scale=HD2 ** -0.5 if i < 4 else 1.0)\
                       .then_inc(evac[qkv.slot(i)], 1)

                def repeat_b(r):
                    act.wait_ge(sem("ss_bb"), r + 1)
                    for z in range(2):
                        act.activation(reps[:, z], bb[:, z].unsqueeze(2).broadcast_to([P, 8, 4, 32]), ACT.Copy)\
                           .then_inc(sem("ss_rep"), 1)

                for r in range(4):
                    if r:
                        act.wait_ge(sem("ss_out"), r)
                    for u in range(4):
                        src = uin[32 * u:32 * u + 32, r, :].rearrange("p (c j) -> p j c", j=SC)
                        for j in range(SC):
                            act.activation(us[32 * j:32 * j + 32, 0, u, :], src[:, j, :], ACT.Copy).then_inc(sem("ss_u"), 1)
                            act.activation(us[32 * j:32 * j + 32, 1, u, :], src[:, j, ::-1], ACT.Copy).then_inc(sem("ss_u"), 1)
                    if r == 0:
                        repeat_b(0)
                    projected(3 * r)
                    projected(3 * r + 1)
                    for g in range(4):
                        act.wait_ge(sem("ss_w1_turned"), 4 * r + g + 1)
                        act.activation(w1s[:, 2 * g:2 * g + 2].rearrange("p a b c -> p (a b c)"), aux[1][:, 0, :], ACT.Copy)\
                           .then_inc(sem("ss_w1"), 1)
                    act.wait_ge(sem("ss_angle"), r + 1)
                    act.activation(cs_[:, 1], w8[:, :, :], ACT.Sin)
                    act.activation(cs_[:, 0], w8[:, :, :], ACT.Sin, scale=0.5).then_inc(sem("ss_sines"), 1)
                    act.wait_ge(sem("ss_lags"), r + 1)
                    act.wait_ge(sem("ss_t_zero"), r + 1)
                    if r < 3:
                        act.wait_ge(sem("ss_cpow"), 2 * (r + 1))
                        load_bc(r + 1)
                    lag = aux[0][:, 0, :].rearrange("p (u c) -> p u c", u=4)
                    for j in range(SC):
                        m = act.activation(tm_[32 * j:32 * j + 32, :, 32 * j:P], lag[32 * j:32 * j + 32, :, 0:P - 32 * j], ACT.Copy)
                    m.then_inc(sem("ss_t_forward"), 1)
                    projected(3 * r + 2)
                    if r < 3:
                        repeat_b(r + 1)
                    act.wait_ge(sem("ss_out"), r + 1)
                    for u in range(4):
                        dst = yv[32 * u:32 * u + 32, r, :].rearrange("p (c j) -> p j c", j=SC)
                        for j in range(SC):
                            act.activation(dst[:, j, :], aux[0][32 * j:32 * j + 32, 0, u * NC:(u + 1) * NC], ACT.Copy)\
                               .then_inc(sem("ss_y"), 1)
                for e in range(0, HEADS, 2):
                    act.dma_start(natab[:, e:e + 2], A_natab[:, e:e + 2]).then_inc(sem("na_loaded"), 16)
                act.dma_start(namask[:, :], A_namask).then_inc(sem("na_loaded"), 16)
                h_ready(act, qkv)
                act.sem_inc(sem("v2_rows"), 1)
                for r in range(4):
                    act.wait_ge(sem("ss_skip"), r + 1)
                    act.activation(yv[:, r], yv[:, r], ACT.Gelu_apprx_tanh).then_inc(sem("y_gelu"), 1)
                for r in range(4):
                    act.wait_ge(sem("y_gelu"), r + 1)
                    act.activation(zhi[:, r], yv[:, r], ACT.Copy).then_inc(sem("y_hi"), 1)
                act.wait_ge(sem("v2_turned"), 1)
                for e in range(4):
                    act.activation(v2[:, :, e * P:(e + 1) * P], aux[e // 2][:, e % 2, :].rearrange("p (a b) -> p a b", a=4),
                                   ACT.Copy).then_inc(sem("v2_copied"), 1)
                ph = AT["glu2"]
                for i in range(4):
                    block_done(ph.block(i) + 1)
                    act.activation(halves(uin[:, i], S), accv(ph.slot(i), S), ACT.Sigmoid, bias=col("glu_b", None, i))\
                       .then_inc(evac[ph.slot(i)], 1)
                for i in range(4):
                    act.wait_ge(sem("z_done"), i + 1)
                    if i == 0:
                        block_done(ph.block(3) + 1)
                    act.activation(zhi[:, i], yv[:, i], ACT.Copy).then_inc(sem("z_hi"), 1)

            def square_of(n):
                act.wait_ge(sem("ple_added"), n + 1)
                act.wait_ge(sem("norm_added"), n + 8 * KD)
                act.activation(fsq[:, 0], h[:, n], ACT.Square).then_inc(sem("norm_square"), 1)

            act.dma_start(h[:, :, :], A_h).then_inc(sem("h_loaded"), 16)
            act.dma_start(par[:, :], A_par).then_inc(sem("par_loaded"), 16)
            act.dma_start(ident[:, :], A_ident).then_inc(sem("ident_loaded"), 16)
            for l in range(DEPTH):
                norm(2 * l)
                act.wait_ge(sem("norm_lo"), (2 * l + 1) * KD)
                act.dma_start(rope[:, :, :], A_rope.rearrange("a p n -> p a n")).then_inc(sem("rope_loaded"), 16)
                act.dma_start(rnn_w[:, :, :, :].rearrange("p a b c -> p a (b c)"), A_gate[l].rearrange("a p n -> p a n"))\
                   .then_inc(sem("rnn_w_loaded"), 16)
                proj(l)
                index(l)
                if l == 0:
                    act.wait_ge(sem("lam_abs"), 1)
                    act.activation(prep[:, 1, :], prep[:, 0, :], ACT.Exp, scale=-1.0).then_inc(sem("lam_exp"), 1)
                conv_gates(l)
                act.wait_ge(sem("spc_done"), 1)
                rnn(l)
                mix(l)
                att_split(l)
                mg_att(l)
                merge(l, "conv")
                for n in range(KD):
                    if n == 0:
                        act.wait_ge(sem("mg_add"), (2 * l + 2) * KD + 1)
                        block_done(AT[f"out{l}"].b0)
                    act.activation(bhi[:, n], merged[:, n], ACT.Copy).then_inc(sem("br_hi"), 1)
                squares(2 * l + 1, AT[f"out{l}"])
                ffn(2 * l + 1, f"up{l}", T1)
            ffn(4, "up2", SEQ)
            norm(5)
            act.wait_ge(sem("norm_lo"), 6 * KD)
            ssm_parameters()
            ph = AT["sin2"]
            for i in range(4):
                block_done(ph.block(i) + 1)
                act.activation(halves(uin[:, i], S), accv(ph.slot(i), S), ACT.Copy).then_inc(evac[ph.slot(i)], 1)
            h_ready(act, ph)
            ssm()
            neighbours()
            for n in range(KD):
                ph = AT[f"att_gate{n}"]
                block_done(ph.b0 + 1)
                if n >= 2:
                    act.wait_ge(sem("att_product"), n - 1)
                act.activation(halves(sga[:, n % 2], S), accv(n % 2, S), ACT.Sigmoid).then_inc(evac[n % 2], 1)
            for n in range(KD):
                act.wait_ge(sem("m2_add"), n + 1)
                act.activation(mhi[:, n], merged2[:, n], ACT.Copy).then_inc(sem("m2_hi"), 1)
            squares(6, AT["out2"])
            ffn(6, "up3", SEQ)
            norm(7)
            for n in range(KD):
                block_done(AT[f"ple_gate{n}"].b0 + 1)
                if n >= 2:
                    act.wait_ge(sem("ple_product"), n - 1)
                act.activation(halves(psg[:, n % 2], S), accv(n % 2, S), ACT.Sigmoid).then_inc(evac[n % 2], 1)
                if n:
                    square_of(n - 1)
            square_of(KD - 1)
            norm(8)

        @block.vector
        def _(dve):
            def block_done(b):
                dve.wait_ge(pe_block, b)

            chain = [0]

            def then(ins):
                chain[0] += 1
                ins.then_inc(sem("dve_step"), 1)
                dve.wait_ge(sem("dve_step"), chain[0])

            def norm(i):
                T = NORM_T[i]
                name, l = NORM_G[i]
                if i == 0:
                    then(dve.memset(facc[:, :], 0.0))
                    for j in range(KD):
                        dve.wait_ge(sem("norm_square"), j + 1)
                        if j:
                            dve.wait_ge(sem("norm_added"), j)
                        dve.tensor_tensor(facc[:, :], facc[:, :], fsq[:, j % 2], ALU.add).then_inc(sem("norm_added"), 1)
                    dve.wait_ge(sem("par_loaded"), 16)
                dve.wait_ge(sem("norm_std"), i + 1)
                then(dve.reciprocal(frs[:, 0:T], fstd[:, 0:T]))
                for j in range(KD):
                    if i < 8:
                        if j >= 2:
                            dve.wait_ge(sem("norm_lo"), i * KD + j - 1)
                        dve.scalar_tensor_tensor(ftmp[:, j % 2, 0:T], hview(T)[:, j], col(name, l, j), frs[:, 0:T],
                                                 ALU.mult, ALU.mult).then_inc(sem("norm_scaled"), 1)
                        dve.wait_ge(sem("norm_hi"), i * KD + j + 1)
                        dve.tensor_tensor(nlo[:, j, 0:T], ftmp[:, j % 2, 0:T], nhi[:, j, 0:T].bitcast(F32), ALU.subtract)\
                           .then_inc(sem("norm_lo"), 1)
                    else:
                        dve.scalar_tensor_tensor(yout[:, j], hview(T)[:, j], col(name, l, j), frs[:, 0:T],
                                                 ALU.mult, ALU.mult).then_inc(sem("final_out"), 1)

            def ffn(i, up, down, T, scale):
                norm(i)
                ph, f = AT[up], FFI[up]
                with dve.Fori(0, KF) as m:
                    block_done(m * 2 + (ph.block(1) + 1))
                    dve.wait_ge(evac[ph.slot(0)], m + (ph.nth(0) + 1))
                    dve.wait_ge(sem("ff_lo"), m + (f * KF + 1))
                    dve.tensor_tensor(halves(fpr[:, 0:T], T), accv(ph.slot(1), T), halves(fsl[:, 0:T], T), ALU.mult)\
                       .then_inc(evac[ph.slot(1)], 1)
                    dve.wait_ge(sem("ff_hi"), m + (f * KF + 1))
                    dve.tensor_tensor(alo[:, bass.ds(m, 1), 0:T], fpr[:, 0:T].unsqueeze(1),
                                      ahi[:, bass.ds(m, 1), 0:T].bitcast(F32), ALU.subtract).then_inc(sem("ff_lo"), 1)
                if up == "up3":
                    dve.wait_ge(sem("p_hi"), 1)
                    for n in range(2):
                        dve.tensor_tensor(plo[:, n], pin[:, n], phi[:, n].bitcast(F32), ALU.subtract).then_inc(sem("p_lo"), 1)
                add_to_h(AT[down], T, i + 1, scale)

            def add_to_h(ph, T, i, scale=1.0):
                dve.wait_ge(sem("norm_summed"), i)
                dve.memset(facc[:, :], 0.0).then_inc(sem("norm_clear"), 1)
                with dve.Fori(0, KD // 2) as m:
                    for j in range(2):
                        s = ph.slot(j)
                        block_done(m * (2 * ph.per) + (ph.block(j) + ph.per))
                        hv = h[:, bass.ds(m * 2 + j, 1), T1 - T:T1].rearrange("p a (b c) -> p (a b) c", b=2)
                        if scale == 1.0:
                            dve.tensor_tensor(hv, accv(s, T), hv, ALU.add).then_inc(evac[s], 1)
                        else:
                            dve.scalar_tensor_tensor(hv, accv(s, T), scale, hv, ALU.mult, ALU.add).then_inc(evac[s], 1)
                        dve.wait_ge(sem("norm_clear"), i)
                        dve.wait_ge(sem("norm_square"), m * 2 + (i * KD + j + 1))
                        dve.wait_ge(sem("norm_added"), m * 2 + (i * KD + j))
                        dve.tensor_tensor(facc[:, :], facc[:, :], fsq[:, j], ALU.add).then_inc(sem("norm_added"), 1)

            def proj(l):
                dve.wait_ge(sem("rope_loaded"), 16 * (l + 1))
                for e in range(10):
                    it = l * 10 + e
                    x, w = tqg[:, e % 2], tsw[:, e % 2]
                    dve.wait_ge(sem("qk_swap"), it + 1)
                    then(dve.tensor_tensor(x, x, rope[:, 0], ALU.mult))
                    then(dve.tensor_tensor(w, w, rope[:, 1], ALU.mult))
                    then(dve.tensor_tensor(x, x, w, ALU.add))
                    dve.wait_ge(sem("qk_std"), it + 1)
                    then(dve.reciprocal(trs[:, :], tstd[:, :]))
                    dst = q[:, e] if e < 8 else k[:, e - 8]
                    dve.tensor_tensor(dst, x, trs[:, :], ALU.mult).then_inc(sem("qk_done"), 1)
                for e in range(5):
                    x, w = tqg[:, e % 2], tsw[:, e % 2]
                    dve.wait_ge(sem("qi_swap"), l * 5 + e + 1)
                    then(dve.tensor_tensor(x, x, rope[:, 2], ALU.mult))
                    then(dve.tensor_tensor(w, w, rope[:, 3], ALU.mult))
                    dst = qi[:, e] if e < 4 else ki[:, :]
                    dve.tensor_tensor(dst, x, w, ALU.add).then_inc(sem("qi_done"), 1)

            def index(l):
                dve.wait_ge(sem("wi_copied"), l + 1)
                for i in range(NQT):
                    W = META + P * (i + 1)
                    sc = mask[:, i, 0:W]
                    for hh in range(IXH):
                        it = (l * NQT + i) * IXH + hh
                        r, w = tsq[:, hh % 2, 0:W], wi[:, i, hh:hh + 1]
                        dve.wait_ge(sem("ix_relu"), it + 1)
                        if hh == 0:
                            dve.tensor_scalar(sc, r, w, None, ALU.mult).then_inc(sem("ix_acc"), 1)
                        else:
                            dve.wait_ge(sem("ix_acc"), it)
                            dve.scalar_tensor_tensor(sc, r, w, sc, ALU.mult, ALU.add).then_inc(sem("ix_acc"), 1)
                dve.wait_ge(sem("ix_acc"), (l + 1) * NQT * IXH)

            def choose(l, n):
                for i in range(NQT):
                    W = META + P * (i + 1)
                    sc = mask[:, i, 0:W]
                    if n == 0:
                        then(dve.memset(mask[0:CHUNK, i, W - CHUNK:W], BARRED))
                    for _ in range(TOPK // 8 // KD):
                        then(dve.max(top8[:, :], sc))
                        then(dve.match_replace(sc, top8[:, :], sc, CHOSEN))
                    if n == KD - 1:
                        then(dve.tensor_scalar(sc, sc, CHOSEN, NEG, ALU.not_equal, ALU.mult))
                        then(dve.memset(mask[0:CHUNK, i, W - CHUNK:W], NEG))

            def rnn(l):
                dve.wait_ge(sem("ix_relu"), (l + 1) * NQT * IXH)
                dve.memset(rx[:, 0:CONV - 1], 0.0).then_inc(sem("rnn_pad"), 1)
                dve.wait_ge(sem("rnn_pad"), l + 1)
                ph = AT[f"rnn{l}"]

                def taps(n):
                    it = l * 8 + n
                    dve.wait_ge(evac[ph.slot(2 * n)], ph.nth(2 * n) + 1)
                    if n:
                        dve.wait_ge(sem("rnn_iu"), it)
                        dve.wait_ge(sem("rnn_gates"), it)
                    for j in range(CONV):
                        t = CONV - 1 - j
                        w = col("cw", l, t * 8 + n)
                        if j == 0:
                            dve.tensor_scalar(ru[:, :], rx[:, t:t + T1], w, col("cb", l, n), ALU.mult, ALU.add)\
                               .then_inc(sem("rnn_conv"), 1)
                        else:
                            dve.wait_ge(sem("rnn_conv"), 4 * it + j)
                            dve.scalar_tensor_tensor(ru[:, :], rx[:, t:t + T1], w, ru[:, :], ALU.mult, ALU.add)\
                               .then_inc(sem("rnn_conv"), 1)

                def rest(n):
                    it = l * 8 + n
                    dve.wait_ge(sem("rnn_i"), it + 1)
                    dve.scalar_tensor_tensor(ri[:, :], ri[:, :], 1.0, ru[:, :], ALU.add, ALU.mult).then_inc(sem("rnn_iu"), 1)
                    dve.wait_ge(sem("rnn_t"), it + 1)
                    dve.tensor_scalar(rb[:, :], rt[:, :], 1.0, None, ALU.add).then_inc(sem("rnn_m"), 1)
                    dve.wait_ge(sem("rnn_m"), 3 * it + 1)
                    dve.reciprocal(rb[:, :], rb[:, :]).then_inc(sem("rnn_m"), 1)
                    dve.wait_ge(sem("rnn_m"), 3 * it + 2)
                    dve.tensor_tensor(rb[:, :], rb[:, :], rt[:, :], ALU.mult).then_inc(sem("rnn_m"), 1)
                    if n < 7:
                        taps(n + 1)
                    dve.wait_ge(sem("rnn_sqrt"), it + 1)
                    dve.wait_ge(sem("rnn_iu"), it + 1)
                    dve.tensor_tensor(rb[:, :], rb[:, :], ri[:, :], ALU.mult).then_inc(sem("rnn_b"), 1)
                    dve.wait_ge(sem("rnn_b"), it + 1)
                    dve.wait_ge(sem("rnn_a"), it + 1)
                    dve.tensor_tensor_scan(rh[:, :], ra[:, :], rb[:, :], 0.0, ALU.mult, ALU.add).then_inc(sem("rnn_scan"), 1)
                    dve.wait_ge(sem("rnn_scan"), it + 1)
                    dve.wait_ge(evac[ph.slot(2 * n + 1)], ph.nth(2 * n + 1) + 1)
                    dve.tensor_tensor(rh[:, :], rh[:, :], rg[:, :], ALU.mult).then_inc(sem("rnn_out"), 1)
                    dve.wait_ge(sem("br_hi"), (l * 4) * KD + n + 1)
                    dve.tensor_tensor(blo[:, n], rh[:, :], bhi[:, n].bitcast(F32), ALU.subtract).then_inc(sem("br_lo"), 1)

                taps(0)
                for n in range(8):
                    rest(n)

            def merge(l, name, inst):
                ph = AT[f"mg_{name}{l}"]
                with dve.Fori(0, KD) as m:
                    block_done(m * 2 + (ph.block(1) + 1))
                    dve.wait_ge(evac[ph.slot(0)], m + (ph.nth(0) + 1))
                    a, g = accv(ph.slot(1), T1), halves(sg[:, :], T1)
                    mg = merged[:, bass.ds(m, 1), :]
                    if inst == 0:
                        dve.tensor_tensor(mg.rearrange("p a (b c) -> p (a b) c", b=2), a, g, ALU.mult).then_inc(evac[ph.slot(1)], 1)
                    else:
                        dve.wait_ge(sem("mg_add"), m + ((2 * l + inst - 1) * KD + 1))
                        dve.tensor_tensor(halves(mt[:, :], T1), a, g, ALU.mult).then_inc(evac[ph.slot(1)], 1)
                        dve.wait_ge(evac[ph.slot(1)], m + (ph.nth(1) + 1))
                        dve.tensor_tensor(mg, mg, mt[:, :].unsqueeze(1), ALU.add).then_inc(sem("mg_add"), 1)

            def conv_inputs(l):
                ph = AT[f"conv{l}"]
                for n in range(KD):
                    block_done(ph.block(2 * n + 1) + 1)
                    dve.wait_ge(evac[0], ph.nth(2 * n) + 1)
                    dve.tensor_tensor(halves(cu[:, n], T1), accv(1, T1), halves(csg[:, :], T1), ALU.mult)\
                       .then_inc(evac[1], 1)
                    choose(l, n)
                dve.sem_inc(sem("mask_done"), 1)

            def conv_taps(l):
                then(dve.memset(cx[:, :, 0:DW - 1], 0.0))
                for n in range(0, KD, 2):
                    done = (l * 8 + n) * DW
                    if n:
                        dve.wait_ge(sem("cv_conv"), done)
                    then(dve.tensor_copy(cx[:, :, DW - 1:], cu[:, n:n + 2]))
                    for j in range(DW):
                        t = DW - 1 - j
                        for z in range(2):
                            w = col("dw", l, t * 8 + n + z)
                            x, y = cx[:, z, t:t + T1], cu[:, n + z]
                            if j == 0:
                                dve.tensor_scalar(y, x, w, col("db", l, n + z), ALU.mult, ALU.add).then_inc(sem("cv_conv"), 1)
                            else:
                                dve.wait_ge(sem("cv_conv"), done + 2 * j - 1 + z)
                                dve.scalar_tensor_tensor(y, x, w, y, ALU.mult, ALU.add).then_inc(sem("cv_conv"), 1)
                            yield

            def merged_tile(l, ph, m, inst):
                block_done(ph.block(1) + 2 * m + 1)
                dve.wait_ge(evac[ph.slot(0)], ph.nth(0) + m + 1)
                dve.wait_ge(sem("mg_add"), (2 * l + inst - 1) * KD + m + 1)
                dve.tensor_tensor(halves(mt[:, :], T1), accv(ph.slot(1), T1), halves(sg[:, :], T1), ALU.mult)\
                   .then_inc(evac[ph.slot(1)], 1)
                dve.wait_ge(evac[ph.slot(1)], ph.nth(1) + m + 1)
                dve.tensor_tensor(merged[:, m], merged[:, m], mt[:, :], ALU.add).then_inc(sem("mg_add"), 1)

            def mg_att(l, taps):
                ph = AT[f"mg_att{l}"]
                for n in range(KD):
                    dve.wait_ge(sem("br_hi"), (l * 4 + 1) * KD + n + 1)
                    dve.tensor_tensor(blo[:, n], q[:, n], bhi[:, n].bitcast(F32), ALU.subtract).then_inc(sem("br_lo"), 1)
                for m in range(LN_AFTER):
                    merged_tile(l, ph, m, 1)
                    for _ in range(TAPS_MERGE):
                        next(taps, None)
                for _ in taps:
                    pass
                dve.wait_ge(sem("cv_mean_read"), l + 1)
                for n in range(KD):
                    dve.tensor_tensor(cu[:, n], cu[:, n], cstat[:, 0], ALU.subtract).then_inc(sem("cv_centred"), 1)
                merged_tile(l, ph, LN_AFTER, 1)
                dve.wait_ge(sem("cv_std"), l + 1)
                then(dve.reciprocal(cstat[:, 2], cstat[:, 1]))
                for n in range(KD):
                    dve.tensor_tensor(cu[:, n], cu[:, n], cstat[:, 2], ALU.mult).then_inc(sem("cv_scaled"), 1)
                for m in range(LN_AFTER + 1, KD):
                    merged_tile(l, ph, m, 1)
                for n in range(KD):
                    dve.wait_ge(sem("br_hi"), (l * 4 + 2) * KD + n + 1)
                    dve.tensor_tensor(blo[:, n], cu[:, n], bhi[:, n].bitcast(F32), ALU.subtract).then_inc(sem("br_lo"), 1)

            def mix(l, taps):
                mg = AT[f"mg_rnn{l}"]
                items = [(hh, i) for hh in range(HEADS) for i in range(NQT + 1)]
                n0 = l * len(items)

                def score(j):
                    hh, i = items[j]
                    r, W = (P, META + (i + 1) * P) if i < NQT else (META, META)
                    b = j % 3
                    dve.wait_ge(sem("at_s"), n0 + j + 1)
                    if j >= 3:
                        dve.wait_ge(sem("at_turned"), n0 + j - 2)
                    src = aux[0][0:r].rearrange("p a b -> p (a b)")[:, 0:W]
                    add = mask[0:r, i, 0:W] if i < NQT else zeros[0:r, 0:W]
                    dve.tensor_tensor_reduce(sm[0:r, b, 0:W], src, add, float(HD) ** -0.5, CHOSEN, ALU.add, ALU.max,
                                             mx[0:r, b:b + 1]).then_inc(sem("at_scored"), 1)
                    dve.wait_ge(sem("at_scored"), n0 + j + 1)
                    dve.tensor_scalar(nmx[0:r, b:b + 1], mx[0:r, b:b + 1], -1.0, None, ALU.mult).then_inc(sem("at_max"), 1)

                def share(j):
                    hh, i = items[j]
                    r, W = (P, META + (i + 1) * P) if i < NQT else (META, META)
                    b = j % 3
                    dve.wait_ge(sem("at_exp"), n0 + j + 1)
                    then(dve.reciprocal(rrs[0:r, b:b + 1], rsum[0:r, b:b + 1]))
                    dve.tensor_scalar(sm[0:r, b, 0:W], sm[0:r, b, 0:W], rrs[0:r, b:b + 1], None, ALU.mult)\
                       .then_inc(sem("at_p"), 1)

                dve.wait_ge(sem("br_lo"), (l * 4 + 1) * KD)
                score(0)
                score(1)
                for j in range(len(items)):
                    share(j)
                    for _ in range(TAPS_ITEM // 2):
                        next(taps, None)
                    if j + 2 < len(items):
                        score(j + 2)
                    for _ in range(TAPS_ITEM // 2):
                        next(taps, None)
                    if items[j][1] == NQT:
                        m = items[j][0]
                        block_done(mg.block(2 * m + 1) + 1)
                        then(dve.tensor_scalar(sg[:, :], sg[:, :], 0.5, 0.5, ALU.mult, ALU.add))
                        dve.tensor_tensor(halves(merged[:, m], T1), accv(0, T1), halves(sg[:, :], T1), ALU.mult)\
                           .then_inc(evac[0], 1)

            def neighbours():
                items = [(hh, i) for hh in range(HEADS) for i in range(NQT)]
                ph, mg = AT["att2"], AT["mg_ssm2"]

                def bar(hh):
                    then(dve.tensor_tensor(natab[:, hh], natab[:, hh], namask[:, :].unsqueeze(1).broadcast_to([P, NAR, GW]),
                                           ALU.add))

                def score(j):
                    hh, i = items[j]
                    b = j % 3
                    dve.wait_ge(sem("na_s"), j + 1)
                    if j >= 3:
                        dve.wait_ge(sem("na_turned"), j - 2)
                    add = natab[:, hh, 6 - 2 * i:14 - 2 * i].rearrange("p a b -> p (a b)")
                    dve.tensor_tensor_reduce(sm2[:, b], aux[0][:, 0, :], add, 1.0, CHOSEN, ALU.add, ALU.max,
                                             sc2[:, 0, b:b + 1]).then_inc(sem("na_scored"), 1)
                    dve.wait_ge(sem("na_scored"), j + 1)
                    dve.tensor_scalar(sc2[:, 1, b:b + 1], sc2[:, 0, b:b + 1], -1.0, None, ALU.mult).then_inc(sem("na_max"), 1)

                def part(t):
                    dve.wait_ge(sem("attn2_hi"), t + 1)
                    dve.tensor_tensor(attn_lo[:, t], acc[1][:, 0, :], attn_hi[:, t].bitcast(F32), ALU.subtract)\
                       .then_inc(evac[1], 1)

                dve.wait_ge(sem("na_loaded"), 16 * 5)
                bar(0)
                score(0)
                score(1)
                for j in range(len(items)):
                    hh, i = items[j]
                    b = j % 3
                    dve.wait_ge(sem("na_exp"), j + 1)
                    then(dve.reciprocal(sc2[:, 3, b:b + 1], sc2[:, 2, b:b + 1]))
                    dve.tensor_scalar(sm2[:, b], sm2[:, b], sc2[:, 3, b:b + 1], None, ALU.mult).then_inc(sem("na_p"), 1)
                    if j + 2 < len(items):
                        score(j + 2)
                    if hh and hh % 2 == 0 and i == 0:
                        part(hh // 2 - 1)
                    if i == 0 and hh + 1 < HEADS:
                        bar(hh + 1)
                    if i == NQT - 1:
                        block_done(mg.block(2 * hh + 1) + 1)
                        then(dve.tensor_scalar(sg2[:, :], sg2[:, :], 0.5, 0.5, ALU.mult, ALU.add))
                        dve.tensor_tensor(halves(merged2[:, hh], S), accv(0, S), halves(sg2[:, :], S), ALU.mult)\
                           .then_inc(evac[0], 1)
                part(3)

            C1, C2, C3 = two_pi_parts()

            def reduce_angle(out, kk, x):
                then(dve.tensor_scalar(kk, x, float(1.0 / TWO_PI), MAGIC, ALU.mult, ALU.add))
                then(dve.tensor_scalar(kk, kk, MAGIC, None, ALU.subtract))
                then(dve.scalar_tensor_tensor(out, kk, -C1, x, ALU.mult, ALU.add))
                then(dve.scalar_tensor_tensor(out, kk, -C2, out, ALU.mult, ALU.add))
                then(dve.scalar_tensor_tensor(out, kk, -C3, out, ALU.mult, ALU.add))
                then(dve.tensor_scalar(out, out, PI_SAFE, -PI_SAFE, ALU.min, ALU.max))

            def ssm():
                w = lambda j: spw[:, j]
                tt = lambda o_, a, b_, op: then(dve.tensor_tensor(o_, a, b_, op))
                dve.wait_ge(sem("ss_dt"), 1)
                lre, lim = smp[:, 1], smp[:, 2]
                then(dve.tensor_scalar(lre, lre, -1e-4, None, ALU.min))
                tt(w(1), lre, w(0), ALU.mult)
                tt(w(3), lim, w(0), ALU.mult)
                reduce_angle(w(2), w(8), w(3))
                dve.sem_inc(sem("ss_reduced"), 1)
                tt(w(8), lre, lre, ALU.mult)
                tt(w(9), lim, lim, ALU.mult)
                tt(w(8), w(8), w(9), ALU.add)
                then(dve.reciprocal(w(8), w(8)))
                dve.wait_ge(sem("ss_waves"), 1)
                then(dve.tensor_scalar(w(9), w(6), -1.0, 1.0, ALU.mult, ALU.add))
                then(dve.reciprocal(w(9), w(9)))
                then(dve.scalar_tensor_tensor(w(9), w(6), 2.0, w(9), ALU.mult, ALU.mult))
                then(dve.scalar_tensor_tensor(w(10), w(5), -2.0, w(5), ALU.mult, ALU.mult))
                tt(w(11), w(9), w(10), ALU.mult)
                tt(w(11), w(11), w(9), ALU.add)
                tt(w(11), w(11), w(10), ALU.add)
                then(dve.scalar_tensor_tensor(w(12), w(9), 1.0, w(4), ALU.add, ALU.mult))
                tt(w(13), w(11), lre, ALU.mult)
                tt(w(14), w(12), lim, ALU.mult)
                tt(w(13), w(13), w(14), ALU.add)
                tt(w(13), w(13), w(8), ALU.mult)
                tt(w(14), w(12), lre, ALU.mult)
                tt(w(15), w(11), lim, ALU.mult)
                tt(w(14), w(14), w(15), ALU.subtract)
                tt(w(14), w(14), w(8), ALU.mult)
                then(dve.tensor_scalar(w(11), w(11), 1.0, None, ALU.add))
                then(dve.memset(w(16), 1.0))
                then(dve.memset(w(17), 0.0))
                for p in range(5):
                    for src, c_, b_ in ((w(16), lc_r, lb_r), (w(17), lc_i, lb_i)):
                        s4 = src.rearrange("p (r d u) -> p r d u", r=4, d=2)
                        c4 = c_[:, :, :].rearrange("p (r d u) k -> p r d u k", r=4, d=2)
                        b4 = b_[:, :, :].rearrange("p (r d u) k -> p r d u k", r=4, d=2)
                        then(dve.tensor_copy(c4[:, :, 0, :, p], s4[:, :, 0, :]))
                        then(dve.tensor_copy(c4[:, :, 1, :, 4 - p], s4[:, :, 1, :]))
                        if p < 4:
                            then(dve.tensor_copy(b4[:, :, 0, :, 3 - p], s4[:, :, 0, :]))
                            then(dve.tensor_copy(b4[:, :, 1, :, p], s4[:, :, 1, :]))
                    if p < 4:
                        tt(w(15), w(16), w(12), ALU.mult)
                        tt(w(16), w(16), w(11), ALU.mult)
                        tt(w(18), w(17), w(12), ALU.mult)
                        tt(w(16), w(16), w(18), ALU.subtract)
                        tt(w(17), w(17), w(11), ALU.mult)
                        tt(w(17), w(17), w(15), ALU.add)
                then(dve.tensor_scalar(w(3), w(2), float(SC), None, ALU.mult))
                reduce_angle(w(2), w(0), w(3))

                for r in range(4):
                    u8 = slice(8 * r, 8 * r + 8)
                    f = [w(13)[:, u8].unsqueeze(2).broadcast_to([P, 8, 32]), w(14)[:, u8].unsqueeze(2).broadcast_to([P, 8, 32])]
                    b_, c_ = [sbc[:, 0], sbc[:, 1]], [sbc[:, 2], sbc[:, 3]]
                    t3 = w8[:, :, 0:32]
                    dve.wait_ge(sem("ss_bc_loaded"), 16 * (r + 1))
                    if r:
                        dve.wait_ge(sem("ss_rep"), 2 * r)
                    tt(bb[:, 0], f[0], b_[0], ALU.mult)
                    tt(t3, f[1], b_[1], ALU.mult)
                    tt(bb[:, 0], bb[:, 0], t3, ALU.subtract)
                    tt(bb[:, 1], f[0], b_[1], ALU.mult)
                    tt(t3, f[1], b_[0], ALU.mult)
                    dve.tensor_tensor(bb[:, 1], bb[:, 1], t3, ALU.add).then_inc(sem("ss_bb"), 1)
                    dve.wait_ge(sem("ss_bb"), r + 1)
                    t4 = cs_[:, :, :, :].rearrange("p a b c -> p (a b c)")[:, 0:1024].rearrange("p (a b c) -> p a b c", a=8, b=4)
                    sh = [P, 8, 4, 32]
                    L = [x[:, u8].unsqueeze(3).broadcast_to(sh) for x in (lb_r, lb_i)]
                    B = [bb[:, z].unsqueeze(2).broadcast_to(sh) for z in range(2)]
                    cmul(dve, then, ap_[:, 0], ap_[:, 1], B, L, t4, minus=False, last=sem("ss_bpow"), twice=True)
                    if r:
                        dve.wait_ge(sem("ss_out"), r)
                    sh = [P, 8, 5, 32]
                    L = [x[:, u8].unsqueeze(3).broadcast_to(sh) for x in (lc_r, lc_i)]
                    C = [x.unsqueeze(2).broadcast_to(sh) for x in c_]
                    t5 = cs_[:, :, :, :].rearrange("p a b c -> p (a b c)")[:, 0:1280].rearrange("p (a b c) -> p a b c", a=8, b=5)
                    cmul(dve, then, cp_[:, 0], cp_[:, 1], C, L, t5, minus=True, last=sem("ss_cpow"))
                    ang = w(2)[:, u8].unsqueeze(2).broadcast_to([P, 8, NC])
                    tt(m4[:, :, :], ang, chk[:, :].unsqueeze(1).broadcast_to([P, 8, NC]), ALU.mult)
                    reduce_angle(w8[:, :, :], cs_[:, 0], m4[:, :, :])
                    dve.sem_inc(sem("ss_angle"), 1)
                    then(dve.tensor_copy(m4[:, :, :], w(7)[:, u8].unsqueeze(2).broadcast_to([P, 8, NC])))
                    then(dve.memset(m4[:, :, 0:1], 0.0))
                    then(dve.memset(tm_[:, :, :], 0.0))
                    dve.sem_inc(sem("ss_t_zero"), 1)
                    dve.wait_ge(sem("ss_t_forward"), r + 1)
                    lag = aux[0][:, 1, :].rearrange("p (u c) -> p u c", u=4)
                    for j in range(SC):
                        rows = slice(32 * j, 32 * j + 32)
                        m = dve.tensor_tensor(tm_[rows, :, 0:32 * (j + 1)], tm_[rows, :, 0:32 * (j + 1)],
                                              lag[rows, :, (3 - j) * 32:P], ALU.add)
                    m.then_inc(sem("ss_t"), 1)
                    dve.wait_ge(sem("ss_sines"), r + 1)
                    co, si = cs_[:, 0], cs_[:, 1]
                    tt(co, co, co, ALU.mult)
                    then(dve.tensor_scalar(co, co, -2.0, 1.0, ALU.mult, ALU.add))
                    dve.wait_ge(sem("ss_s"), r + 1)
                    sr = aux[0][:, :, :].rearrange("p a (b c) -> p (a b) c", c=NC)
                    si_ = aux[1][:, :, :].rearrange("p a (b c) -> p (a b) c", c=NC)
                    zr, zi, t = zz[:, 0], zz[:, 1], w8[:, :, :]
                    tt(zr, sr, co, ALU.mult)
                    tt(t, si_, si, ALU.mult)
                    tt(zr, zr, t, ALU.add)
                    tt(zi, si_, co, ALU.mult)
                    tt(t, sr, si, ALU.mult)
                    tt(zi, zi, t, ALU.subtract)
                    flat = lambda x: x.rearrange("p a b -> p (a b)")
                    for z in (zr, zi):
                        then(dve.tensor_tensor_scan(flat(z), flat(m4[:, :, :]), flat(z), 0.0, ALU.mult, ALU.add))
                    if r == 0:
                        then(dve.memset(st_[:, :, 0:4, 0:1], 0.0))
                        then(dve.memset(st_[:, :, 4:8, NC:NC + 1], 0.0))
                    for z, (a, b2, op) in enumerate(((zr, zi, ALU.subtract), (zi, zr, ALU.add))):
                        tt(t, a, co, ALU.mult)
                        tt(m4[:, :, :], b2, si, ALU.mult)
                        dve.tensor_tensor(st_[:, z, 0:4, 1:NC + 1], t[:, 0:4], m4[:, 0:4], op).then_inc(sem("ss_x"), 1)
                        dve.tensor_tensor(st_[:, z, 4:8, NC - 1::-1], t[:, 4:8], m4[:, 4:8], op).then_inc(sem("ss_x"), 1)
                        dve.wait_ge(sem("ss_x"), 4 * r + 2 * z + 2)
                for r in range(4):
                    dve.wait_ge(sem("ss_y"), 16 * (r + 1))
                    dve.scalar_tensor_tensor(yv[:, r], uin[:, r], col("dskip", None, r), yv[:, r], ALU.mult, ALU.add)\
                       .then_inc(sem("ss_skip"), 1)
                for r in range(4):
                    dve.wait_ge(sem("y_hi"), r + 1)
                    dve.tensor_tensor(zlo[:, r], yv[:, r], zhi[:, r].bitcast(F32), ALU.subtract).then_inc(sem("y_lo"), 1)
                ph = AT["glu2"]
                for i in range(4):
                    dve.wait_ge(evac[ph.slot(i)], ph.nth(i) + 1)
                    dve.wait_ge(sem("y_lo"), 4)
                    dve.tensor_tensor(yv[:, i], yv[:, i], uin[:, i], ALU.mult).then_inc(sem("z_done"), 1)
                for i in range(4):
                    dve.wait_ge(sem("z_hi"), i + 1)
                    dve.tensor_tensor(zlo[:, i], yv[:, i], zhi[:, i].bitcast(F32), ALU.subtract).then_inc(sem("z_lo"), 1)

            def decay_rates():
                pp = lambda j: prep[:, j, :]
                for l in range(DEPTH):
                    then(dve.tensor_copy(prep[:, 2, 8 * l:8 * l + 8], col("lam", l, 0, 8)))
                then(dve.tensor_scalar(pp(3), pp(2), -1.0, None, ALU.mult))
                dve.tensor_tensor(pp(0), pp(2), pp(3), ALU.max).then_inc(sem("lam_abs"), 1)
                dve.wait_ge(sem("lam_exp"), 1)
                then(dve.tensor_scalar(pp(4), pp(1), 2.0, None, ALU.add))
                then(dve.reciprocal(pp(4), pp(4)))
                then(dve.tensor_tensor(pp(4), pp(4), pp(1), ALU.mult))
                then(dve.tensor_tensor(pp(5), pp(4), pp(4), ALU.mult))
                then(dve.tensor_scalar(pp(6), pp(5), 1.0 / 17, 1.0 / 15, ALU.mult, ALU.add))
                for d in (13, 11, 9, 7, 5, 3, 1):
                    then(dve.tensor_tensor(pp(6), pp(6), pp(5), ALU.mult))
                    then(dve.tensor_scalar(pp(6), pp(6), 1.0 / d, None, ALU.add))
                then(dve.tensor_tensor(pp(6), pp(6), pp(4), ALU.mult))
                then(dve.tensor_scalar(pp(3), pp(3), 0.0, None, ALU.max))
                then(dve.scalar_tensor_tensor(pp(6), pp(6), 2.0, pp(3), ALU.mult, ALU.add))
                for l in range(DEPTH):
                    for g, name in enumerate(("ba", "bx")):
                        then(dve.tensor_scalar(hba[:, l, g], col(name, l, 0, 8), 0.5, None, ALU.mult))
                then(dve.tensor_scalar(spc[:, :, :].rearrange("p a b -> p (a b)"), pp(6), 4.0, None, ALU.mult))
                dve.tensor_scalar(nspc[:, :, :].rearrange("p a b -> p (a b)"), pp(6), -4.0, None, ALU.mult)\
                   .then_inc(sem("spc_done"), 1)

            then(dve.memset(ones[:, :], 1.0))
            dve.sem_inc(sem("consts_set"), 1)
            then(dve.memset(zeros[:, :], 0.0))
            for name in ("mg_add", "ff_lo"):
                dve.sem_inc(sem(name), 1)
            dve.sem_inc(sem("consts_set"), 2)
            for l in range(DEPTH):
                norm(2 * l)
                proj(l)
                index(l)
                if l == 0:
                    decay_rates()
                conv_inputs(l)
                rnn(l)
                taps = conv_taps(l)
                mix(l, taps)
                mg_att(l, taps)
                merge(l, "conv", 2)
                for n in range(KD):
                    dve.wait_ge(sem("br_hi"), (l * 4 + 3) * KD + n + 1)
                    dve.tensor_tensor(blo[:, n], merged[:, n], bhi[:, n].bitcast(F32), ALU.subtract).then_inc(sem("br_lo"), 1)
                add_to_h(AT[f"out{l}"], T1, 2 * l + 1)
                ffn(2 * l + 1, f"up{l}", f"down{l}", T1, 1.0)
            ffn(4, "up2", "down2", SEQ, 0.5)
            norm(5)
            ssm()
            neighbours()
            for n in range(KD):
                dve.wait_ge(evac[n % 2], AT[f"att_gate{n}"].nth(0) + 1)
                block_done(AT[f"att_products{n // 2}"].b0 + 1)
                dve.tensor_tensor(mt2[:, :], aux[n % 4 // 2][:, n % 2, :], sga[:, n % 2], ALU.mult)\
                   .then_inc(sem("att_product"), 1)
                dve.wait_ge(sem("att_product"), n + 1)
                dve.tensor_tensor(merged2[:, n], merged2[:, n], mt2[:, :], ALU.add).then_inc(sem("m2_add"), 1)
                if n + 1 < KD:
                    dve.wait_ge(sem("m2_add"), n + 1)
            dve.wait_ge(sem("m2_add"), KD)
            for n in range(KD):
                dve.wait_ge(sem("m2_hi"), n + 1)
                dve.tensor_tensor(mlo[:, n], merged2[:, n], mhi[:, n].bitcast(F32), ALU.subtract).then_inc(sem("m2_lo"), 1)
            add_to_h(AT["out2"], SEQ, 6)
            ffn(6, "up3", "down3", SEQ, 0.5)
            norm(7)
            dve.wait_ge(sem("norm_summed"), 8)
            dve.memset(facc[:, :], 0.0).then_inc(sem("norm_clear"), 1)
            dve.wait_ge(sem("norm_clear"), 8)
            for n in range(KD):
                dve.wait_ge(evac[n % 2], AT[f"ple_gate{n}"].nth(0) + 1)
                block_done(AT[f"ple_products{n // 4}"].b0 + 1)
                if n:
                    dve.wait_ge(sem("ple_added"), n)
                dve.tensor_tensor(pmt[:, :], aux[n % 4 // 2][:, n % 2, :], psg[:, n % 2], ALU.mult)\
                   .then_inc(sem("ple_product"), 1)
                dve.wait_ge(sem("ple_product"), n + 1)
                hv = h[:, n, T1 - S:T1]
                dve.tensor_tensor(hv, hv, pmt[:, :], ALU.add).then_inc(sem("ple_added"), 1)
                dve.wait_ge(sem("norm_square"), n + (8 * KD + 1))
                dve.wait_ge(sem("norm_added"), n + 8 * KD)
                dve.tensor_tensor(facc[:, :], facc[:, :], fsq[:, 0], ALU.add).then_inc(sem("norm_added"), 1)
            norm(8)


def cmul(dve, then, out_r, out_i, a, b, t, minus, last, twice=False):
    each = lambda o, x, y, op: then(dve.tensor_tensor(o, x, y, op))
    each(out_r, a[0], b[0], ALU.mult)
    each(t, a[1], b[1], ALU.mult)
    then(dve.tensor_tensor(out_r, out_r, t, ALU.subtract))
    each(out_i, a[0], b[1], ALU.mult)
    each(t, a[1], b[0], ALU.mult)
    then(dve.tensor_tensor(out_i, out_i, t, ALU.add))
    if minus:
        then(dve.tensor_scalar(out_i, out_i, -1.0, None, ALU.mult))
    dve.sem_inc(last, 4 if twice else 2)


def blocks_of(w):
    K, M = w.shape
    nk, per = K // P, -(-K // (P * BLK))
    t = w.reshape(nk, P, M // P, P).transpose(2, 1, 0, 3)
    out = np.zeros((M // P, P, per * BLK, P), w.dtype)
    for c, (k0, kk) in enumerate(cuts(nk, per)):
        out[:, :, c * BLK:c * BLK + kk] = t[:, :, k0:k0 + kk]
    return out.reshape(M // P, P, per, BLK * P).transpose(0, 2, 1, 3).reshape(M // P * per, P, BLK * P)


def pairs(*ws):
    b = [blocks_of(w) for w in ws]
    return np.stack(b, 1).reshape(-1, P, BLK * P)


def packed(w):
    K, M = w.shape
    nk, n = K // P, BLK // (K // P)
    return w.reshape(nk, P, M // P // n, n, P).transpose(2, 1, 3, 0, 4).reshape(-1, P, BLK * P)


def between(a, b, places):
    return np.insert(a, list(places), b, axis=0)


def tiles(x, n):
    return x.reshape(n, P).T


def rope_consts(n, dim):
    inv = (np.float32(10000.0) ** (-np.arange(0, dim, 2, dtype=np.float32) / np.float32(dim))).astype(np.float32)
    ang = (np.arange(n, dtype=np.float32)[:, None] * inv[None, :]).astype(np.float32)
    c, s = np.cos(ang).T.astype(np.float32), np.sin(ang).T.astype(np.float32)
    reps = P // dim
    return np.concatenate([c, c] * reps), np.concatenate([-s, s] * reps)


def kernel(**inputs):
    import concourse.bacc as _bacc
    from concourse.bass_utils import run_bass_kernel_spmd as _run

    I = {n: np.asarray(a) for n, a in inputs.items()}
    ws = []
    for l in range(DEPTH):
        w = I["w_in"][l]
        edge = np.cumsum([0, 1024, 256, 256, 512, 64, 8, 1024, 1024, 2048, 3072])
        q, k, v, qi, ki, wi, xr, yg, cv, gt = (w[:, a:b] for a, b in zip(edge[:-1], edge[1:]))
        last = np.zeros((D, P), w.dtype)
        last[:, 0:64], last[:, 64:72] = ki, wi
        ws += [blocks_of(q), blocks_of(k), blocks_of(v), blocks_of(qi), blocks_of(last), pairs(cv[:, D:], cv[:, 0:D]),
               pairs(xr, yg), pairs(gt[:, D:2 * D], I["w_o_rnn"][l]), pairs(gt[:, 0:D], I["w_o_attn"][l]),
               pairs(gt[:, 2 * D:], I["w_o_conv"][l]), blocks_of(I["w_out"][l]),
               pairs(I["w_ffn_gate"][l], I["w_ffn_up"][l]), blocks_of(I["w_ffn_down"][l])]
    w = I["w_in_2"][0]
    ws += [pairs(I["ffn1_w_gate_2"][0], I["ffn1_w_up_2"][0]), blocks_of(I["ffn1_w_down_2"][0]), blocks_of(w[:, 1536:2048]),
           blocks_of(w[:, 0:1536]), blocks_of(I["ssm_glu_w_2"][0]),
           pairs(w[:, 3072:4096], I["w_ssm_out_2"][0]), between(blocks_of(w[:, 2048:3072]), packed(I["w_attn_out_2"][0]), (1, 3, 5, 7)), blocks_of(I["w_out_2"][0]),
           pairs(I["ffn2_w_gate_2"][0], I["ffn2_w_up_2"][0]), blocks_of(I["ffn2_w_down_2"][0]),
           between(blocks_of(I["ple_w_gate_2"][0]), packed(I["ple_w_proj_2"][0]), (0, 5))]
    wpack = np.concatenate(ws)
    assert wpack.shape[0] == plan()[1]

    cols = []
    for l in range(DEPTH):
        cols += [tiles(I["mix_norm_g"][l], 8), tiles(I["q_norm_g"][l], 1), tiles(I["k_norm_g"][l], 1),
                 *[tiles(I["rnn_conv_w"][l, t], 8) for t in range(CONV)], tiles(I["rnn_conv_b"][l], 8),
                 tiles(I["rnn_ba"][l], 8), tiles(I["rnn_bx"][l], 8), tiles(I["rnn_lambda"][l], 8),
                 *[tiles(I["conv_dw_w"][l, t], 8) for t in range(DW)], tiles(I["conv_dw_b"][l], 8),
                 tiles(I["conv_ln_g"][l], 8), tiles(I["conv_ln_b"][l], 8), tiles(I["ffn_norm_g"][l], 8)]
    cols += [tiles(I["ffn1_norm_2"][0], 8), tiles(I["mix_norm_2"][0], 8), tiles(I["ffn2_norm_2"][0], 8),
             tiles(I["ple_norm_2"][0], 8), tiles(I["final_norm_2"], 8), tiles(I["ssm_d_2"][0], 4), tiles(I["ssm_glu_b_2"][0], 4)]
    par = np.ascontiguousarray(np.concatenate(cols, 1))
    assert par.shape[1] == columns()[1]

    hT = np.concatenate([I["meta"], I["x"][0]]).T.reshape(KD, P, T1).transpose(1, 0, 2)
    rope = np.stack(rope_consts(T1, HD) + rope_consts(T1, IXD)).astype(np.float32)
    gate = np.stack([I["rnn_wa"], I["rnn_wx"]], 1).transpose(0, 1, 3, 2, 4).reshape(DEPTH, 2, P, 8 * P)

    rpb = I["na_rpb_2"][0]
    padded = np.zeros((HEADS, 16, 127), rpb.dtype)
    padded[:, 1:16, 48:79] = rpb
    qc, kc = np.arange(GW)[:, None], np.arange(GW)[None, :]
    natab = np.zeros((2, HEADS, GW, NAR, GW), rpb.dtype)
    for half in range(2):
        for e in range(NAR):
            natab[half, :, :, e] = padded[:, e + 2 - half][:, kc - qc + 63]
    start = np.clip(np.arange(GW) - NAW // 2, 0, GW - NAW)[:, None]
    inside = (kc >= start) & (kc < start + NAW)
    namask = np.tile(np.where(inside, 0.0, NEG).astype(np.float32), (2, 1))

    def states(a):
        a = a.reshape(2, 4, 4, 2, 64, *a.shape[3:])
        a = np.moveaxis(a, [3, 4, 1, 0, 2], [0, 1, 2, 3, 4])
        return a.reshape(P, 32, *a.shape[5:])

    ssm = np.zeros((7, P, 1024), np.float32)
    ssm[0, :, 0:32] = states(np.repeat(I["ssm_log_dt_2"][0][:, :, None], 64, 2))
    ssm[1, :, 0:32] = states(I["ssm_lam_re_2"][0])
    ssm[2, :, 0:32] = states(I["ssm_lam_im_2"][0])
    for n, a in enumerate((I["ssm_b_re_2"][0], I["ssm_b_im_2"][0], I["ssm_c_re_2"][0].transpose(0, 1, 3, 2),
                           I["ssm_c_im_2"][0].transpose(0, 1, 3, 2))):
        a, full = states(a), ssm[3 + n].reshape(P, 32, 32)
        full[0:64, :, 0:16], full[64:, :, 16:] = a[0:64], a[64:]
    chunks = np.tile(np.arange(NC, dtype=np.float32), (P, 1))
    pT = np.ascontiguousarray(I["p_2"][0, 0].T.reshape(2, P, SEQ))

    arrays = {"w": wpack, "par": par, "h": np.ascontiguousarray(hT), "rope": rope, "gate": np.ascontiguousarray(gate),
              "natab": np.ascontiguousarray(natab.transpose(0, 2, 1, 3, 4).reshape(P, HEADS, NAR, GW)), "namask": namask, "ssm": ssm, "chunk": chunks, "p": pT, "ident": np.eye(P, dtype=np.float32)}
    nc = _bacc.Bacc("TRN2", target_bir_lowering=False, num_devices=1)
    args = [nc.dram_tensor(f"in_{n}", a.shape, mybir.dt.from_np(a.dtype), kind="ExternalInput").ap() for n, a in arrays.items()]
    out = nc.dram_tensor("out_0", (KD, P, SEQ), F32, kind="ExternalOutput").ap()
    build(nc, *args, out)
    r = _run(nc, [{f"in_{n}": a for n, a in arrays.items()}], core_ids=[0])
    y = r.results[0]["out_0"]
    return np.ascontiguousarray(y.reshape(D, SEQ).T)[None]
```
